# Optimizing a Trainium2 kernel written in Bass

```python
import math
import jax, jax.numpy as jnp
from jax import lax
import numpy as np

D_MODEL = 1024
BATCH = 1
SEQ = 512
DEPTH = 2

GRID_W = 64
CTX_LEN = 256
HEAD_DIM = 64
ROPE_BASE = 10000.0
EPS = 1e-6
NEG_INF = -1e30
ATTN_SCALE = HEAD_DIM ** -0.5
Q_BLOCK = 128
CHUNK = 128
A_GROUPS = 4
A_GROUP_DIM = 128
A_WIDTH = A_GROUPS * A_GROUP_DIM
B_HEADS = 4
B_QK_WIDTH = 2 * B_HEADS * HEAD_DIM
B_V_DIM = 2 * HEAD_DIM
B_V_WIDTH = B_HEADS * B_V_DIM
KV_START = 2 * A_WIDTH + B_QK_WIDTH
EVEN_IN = 2 * A_WIDTH + 2 * B_QK_WIDTH + B_V_WIDTH
EVEN_OUT = A_WIDTH + B_V_WIDTH
C_HEADS = 16
C_KV_HEADS = 4
C_GROUP = C_HEADS // C_KV_HEADS
WINDOW = 128
C_Q_WIDTH = C_HEADS * HEAD_DIM
C_KV_WIDTH = C_KV_HEADS * HEAD_DIM
C_IN = C_Q_WIDTH + 2 * C_KV_WIDTH
FFN_HIDDEN = ((8 * D_MODEL + 3 * 256 - 1) // (3 * 256)) * 256
N_EVEN = (DEPTH + 1) // 2
N_ODD = DEPTH // 2


def rmsnorm(x, g):
    xf = x.astype(jnp.float32)
    y = xf * lax.rsqrt(jnp.mean(xf * xf, axis=-1, keepdims=True) + EPS)
    return (y * g.astype(jnp.float32)).astype(x.dtype)

def modulate(x, g, shift, scale):
    return rmsnorm(x, g) * (1 + scale) + shift

def rope_tables(s_len, dtype):
    rows = s_len // GRID_W
    row = jnp.repeat(jnp.arange(rows), GRID_W).astype(jnp.float32)
    col = jnp.tile(jnp.arange(GRID_W), rows).astype(jnp.float32)
    nf = HEAD_DIM // 4
    inv = ROPE_BASE ** (-jnp.arange(nf, dtype=jnp.float32) / nf)
    ang = jnp.stack([row[:, None] * inv, col[:, None] * inv], axis=1)
    ang = jnp.broadcast_to(ang[:, :, None, :], (s_len, 2, 2, nf)).reshape(s_len, HEAD_DIM)
    return jnp.cos(ang).astype(dtype), jnp.sin(ang).astype(dtype)

def apply_rope(x, cos, sin):
    xr = x.reshape(x.shape[:-1] + (2, 2, HEAD_DIM // 4))
    rot = jnp.stack([-xr[..., 1, :], xr[..., 0, :]], axis=-2).reshape(x.shape)
    return x * cos[None, :, None, :] + rot * sin[None, :, None, :]

def swiglu(h, w_in, w_out):
    g, u = jnp.split(h @ w_in, 2, axis=-1)
    return (jax.nn.silu(g) * u) @ w_out

def chunk_mlp(u, v, w_s, b_s):
    b, t, _ = u.shape
    shp = (b, t // CHUNK, CHUNK, A_GROUPS, A_GROUP_DIM)
    u = jax.nn.gelu(u, approximate=False).reshape(shp)
    vf = jax.nn.gelu(v.astype(jnp.float32), approximate=False).reshape(shp)
    mu = jnp.mean(vf, axis=-1, keepdims=True)
    vf = (vf - mu) * lax.rsqrt(jnp.mean(jnp.square(vf - mu), axis=-1, keepdims=True) + EPS)
    mixed = jnp.einsum('gpq,bnqgc->bnpgc', w_s.astype(jnp.float32), vf) + b_s.astype(jnp.float32).T[None, None, :, :, None]
    return (u * mixed.astype(u.dtype)).reshape(b, t, A_WIDTH)

def diff_attn(q, k, v, lam):
    b, tq = q.shape[0], q.shape[1]
    tk = k.shape[1]
    s = jnp.einsum('bqhd,bkhd->bhqk', q, k).astype(jnp.float32) * ATTN_SCALE
    p = jax.nn.softmax(s, axis=-1).reshape(b, B_HEADS, 2, tq, tk)
    a = p[:, :, 0] - lam * p[:, :, 1]
    return jnp.einsum('bhqk,bkhe->bqhe', a.astype(v.dtype), v)

def diff_out(o, g, lam_init):
    b, t = o.shape[0], o.shape[1]
    return (rmsnorm(o, g) * (1.0 - lam_init)).reshape(b, t, B_V_WIDTH)

def sink_attend(q, kvs, sink):
    scores = []
    for k, v, mask in kvs:
        s = jnp.einsum('bqhgd,bkhd->bhgqk', q, k).astype(jnp.float32) * ATTN_SCALE
        if mask is not None:
            s = jnp.where(mask, s, NEG_INF)
        scores.append(s)
    s_sink = jnp.broadcast_to(sink.astype(jnp.float32).reshape(1, C_KV_HEADS, C_GROUP, 1, 1), scores[0].shape[:-1] + (1,))
    p = jax.nn.softmax(jnp.concatenate(scores + [s_sink], axis=-1), axis=-1)
    out = None
    start = 0
    for k, v, _ in kvs:
        tk = k.shape[1]
        o = jnp.einsum('bhgqk,bkhd->bqhgd', p[..., start:start + tk].astype(v.dtype), v)
        out = o if out is None else out + o
        start += tk
    return out

def even_mixer(h, hc, w_in, w_out, w_s, b_s, lq1, lk1, lq2, lk2, subln_g, lam_init, cos, sin, need_ctx):
    b, s_len, _ = h.shape
    nb = s_len // Q_BLOCK
    f32 = jnp.float32
    lam = (jnp.exp(jnp.sum(lq1.astype(f32) * lk1.astype(f32)))
           - jnp.exp(jnp.sum(lq2.astype(f32) * lk2.astype(f32))) + lam_init)
    u, v, q, k, vv = jnp.split(h @ w_in, [A_WIDTH, 2 * A_WIDTH, KV_START, KV_START + B_QK_WIDTH], axis=-1)
    q = apply_rope(q.reshape(b, s_len, 2 * B_HEADS, HEAD_DIM), cos, sin)
    k = apply_rope(k.reshape(b, s_len, 2 * B_HEADS, HEAD_DIM), cos, sin)
    vv = vv.reshape(b, s_len, B_HEADS, B_V_DIM)
    kc, vvc = jnp.split(hc @ w_in[:, KV_START:], [B_QK_WIDTH], axis=-1)
    kc = kc.reshape(b, -1, 2 * B_HEADS, HEAD_DIM)
    vvc = vvc.reshape(b, -1, B_HEADS, B_V_DIM)
    k_all = jnp.concatenate([k, kc], axis=1)
    v_all = jnp.concatenate([vv, vvc], axis=1)
    q_blocks = q.reshape(b, nb, Q_BLOCK, 2 * B_HEADS, HEAD_DIM).transpose(1, 0, 2, 3, 4)
    o = lax.map(lambda qb: diff_attn(qb, k_all, v_all, lam), q_blocks)
    o = o.transpose(1, 0, 2, 3, 4).reshape(b, s_len, B_HEADS, B_V_DIM)
    y = jnp.concatenate([chunk_mlp(u, v, w_s, b_s), diff_out(o, subln_g, lam_init)], axis=-1) @ w_out
    yc = None
    if need_ctx:
        uc, vc_, qc = jnp.split(hc @ w_in[:, :KV_START], [A_WIDTH, 2 * A_WIDTH], axis=-1)
        qc = qc.reshape(b, -1, 2 * B_HEADS, HEAD_DIM)
        oc = diff_attn(qc, kc, vvc, lam)
        yc = jnp.concatenate([chunk_mlp(uc, vc_, w_s, b_s), diff_out(oc, subln_g, lam_init)], axis=-1) @ w_out
    return y, yc

def odd_mixer(h, hc, w_qkv, w_out, sink, cos, sin, need_ctx):
    b, s_len, _ = h.shape
    nb = s_len // Q_BLOCK
    q, k, v = jnp.split(h @ w_qkv, [C_Q_WIDTH, C_Q_WIDTH + C_KV_WIDTH], axis=-1)
    q = apply_rope(q.reshape(b, s_len, C_HEADS, HEAD_DIM), cos, sin).reshape(b, s_len, C_KV_HEADS, C_GROUP, HEAD_DIM)
    k = apply_rope(k.reshape(b, s_len, C_KV_HEADS, HEAD_DIM), cos, sin)
    v = v.reshape(b, s_len, C_KV_HEADS, HEAD_DIM)
    kc, vc = jnp.split(hc @ w_qkv[:, C_Q_WIDTH:], 2, axis=-1)
    kc = kc.reshape(b, -1, C_KV_HEADS, HEAD_DIM)
    vc = vc.reshape(b, -1, C_KV_HEADS, HEAD_DIM)
    pad = ((0, 0), (WINDOW, WINDOW), (0, 0), (0, 0))
    k_pad = jnp.pad(k, pad)
    v_pad = jnp.pad(v, pad)
    band = Q_BLOCK + 2 * WINDOW
    q_blocks = q.reshape(b, nb, Q_BLOCK, C_KV_HEADS, C_GROUP, HEAD_DIM).transpose(1, 0, 2, 3, 4, 5)

    def block(args):
        i, qb = args
        start = i * Q_BLOCK
        kb = lax.dynamic_slice_in_dim(k_pad, start, band, axis=1)
        vb = lax.dynamic_slice_in_dim(v_pad, start, band, axis=1)
        qpos = start + jnp.arange(Q_BLOCK)
        kpos = start - WINDOW + jnp.arange(band)
        mask = ((kpos >= 0)[None, :] & (kpos < s_len)[None, :]
                & (jnp.abs(qpos[:, None] - kpos[None, :]) <= WINDOW))
        return sink_attend(qb, [(kb, vb, mask), (kc, vc, None)], sink)

    o = lax.map(block, (jnp.arange(nb), q_blocks))
    y = o.transpose(1, 0, 2, 3, 4, 5).reshape(b, s_len, C_Q_WIDTH) @ w_out
    yc = None
    if need_ctx:
        qc = (hc @ w_qkv[:, :C_Q_WIDTH]).reshape(b, -1, C_KV_HEADS, C_GROUP, HEAD_DIM)
        yc = sink_attend(qc, [(kc, vc, None)], sink).reshape(b, -1, C_Q_WIDTH) @ w_out
    return y, yc

def first_inputs(seed: int = 0) -> dict:
    key = jax.random.key(seed)
    ks = jax.random.split(key, 24)
    n = jax.random.normal
    f32 = jnp.float32
    return {
        'x': n(ks[0], (BATCH, SEQ, D_MODEL), f32),
        'c': n(ks[1], (BATCH, D_MODEL), f32),
        'ctx': n(ks[2], (BATCH, CTX_LEN, D_MODEL), f32),
        'c_ctx': n(ks[3], (D_MODEL,), f32),
        'ada_w': n(ks[4], (DEPTH, D_MODEL, 6 * D_MODEL), f32) * (0.5 * D_MODEL ** -0.5),
        'ada_b': n(ks[5], (DEPTH, 6 * D_MODEL), f32) * 0.02,
        'norm1_g': 1.0 + 0.02 * n(ks[6], (DEPTH, D_MODEL), f32),
        'norm2_g': 1.0 + 0.02 * n(ks[7], (DEPTH, D_MODEL), f32),
        'ffn_w_in': n(ks[8], (DEPTH, D_MODEL, 2 * FFN_HIDDEN), f32) * D_MODEL ** -0.5,
        'ffn_w_out': n(ks[9], (DEPTH, FFN_HIDDEN, D_MODEL), f32) * FFN_HIDDEN ** -0.5,
        'even_w_in': n(ks[10], (N_EVEN, D_MODEL, EVEN_IN), f32) * D_MODEL ** -0.5,
        'even_w_out': n(ks[11], (N_EVEN, EVEN_OUT, D_MODEL), f32) * EVEN_OUT ** -0.5,
        'sgu_w': n(ks[12], (N_EVEN, A_GROUPS, CHUNK, CHUNK), f32) * CHUNK ** -0.5,
        'sgu_b': 1.0 + 0.1 * n(ks[13], (N_EVEN, A_GROUPS, CHUNK), f32),
        'diff_lq1': 0.1 * n(ks[14], (N_EVEN, HEAD_DIM), f32),
        'diff_lk1': 0.1 * n(ks[15], (N_EVEN, HEAD_DIM), f32),
        'diff_lq2': 0.1 * n(ks[16], (N_EVEN, HEAD_DIM), f32),
        'diff_lk2': 0.1 * n(ks[17], (N_EVEN, HEAD_DIM), f32),
        'diff_subln_g': 1.0 + 0.02 * n(ks[18], (N_EVEN, B_V_DIM), f32),
        'odd_w_qkv': n(ks[19], (N_ODD, D_MODEL, C_IN), f32) * D_MODEL ** -0.5,
        'odd_w_out': n(ks[20], (N_ODD, C_Q_WIDTH, D_MODEL), f32) * C_Q_WIDTH ** -0.5,
        'odd_sink': 0.5 * n(ks[21], (N_ODD, C_HEADS), f32),
        'final_g': 1.0 + 0.02 * n(ks[22], (D_MODEL,), f32),
    }

def first_block(x, c, ctx, c_ctx, ada_w, ada_b, norm1_g, norm2_g, ffn_w_in, ffn_w_out,
              even_w_in, even_w_out, sgu_w, sgu_b, diff_lq1, diff_lk1, diff_lq2, diff_lk2,
              diff_subln_g, odd_w_qkv, odd_w_out, odd_sink, final_g):
    s_len = x.shape[1]
    cos, sin = rope_tables(s_len, x.dtype)
    silu_c = jax.nn.silu(c)
    silu_cc = jax.nn.silu(c_ctx)
    h, hc = x, ctx
    for l in range(DEPTH):
        need_ctx = l < DEPTH - 1
        j = l // 2
        mod = silu_c @ ada_w[l] + ada_b[l]
        modc = silu_cc @ ada_w[l] + ada_b[l]
        sh1, sc1, g1, sh2, sc2, g2 = [m[:, None, :] for m in jnp.split(mod, 6, axis=-1)]
        csh1, csc1, cg1, csh2, csc2, cg2 = [m[None, None, :] for m in jnp.split(modc, 6, axis=-1)]
        a = modulate(h, norm1_g[l], sh1, sc1)
        ac = modulate(hc, norm1_g[l], csh1, csc1)
        if l % 2 == 0:
            lam_init = 0.8 - 0.6 * math.exp(-0.3 * l)
            y, yc = even_mixer(a, ac, even_w_in[j], even_w_out[j], sgu_w[j], sgu_b[j],
                               diff_lq1[j], diff_lk1[j], diff_lq2[j], diff_lk2[j], diff_subln_g[j],
                               lam_init, cos, sin, need_ctx)
        else:
            y, yc = odd_mixer(a, ac, odd_w_qkv[j], odd_w_out[j], odd_sink[j], cos, sin, need_ctx)
        h = h + g1 * y
        h = h + g2 * swiglu(modulate(h, norm2_g[l], sh2, sc2), ffn_w_in[l], ffn_w_out[l])
        if need_ctx:
            hc = hc + cg1 * yc
            hc = hc + cg2 * swiglu(modulate(hc, norm2_g[l], csh2, csc2), ffn_w_in[l], ffn_w_out[l])
    return rmsnorm(h, final_g)


ALPHA = (2 * DEPTH) ** 0.25
BETA = (8 * DEPTH) ** -0.25
LN_EPS = 1e-6
D_FF = ((math.ceil(8 * D_MODEL / 3) + 255) // 256) * 256

RWKV_HEAD = 64
D_A = 3 * D_MODEL // 4
H_A = D_A // RWKV_HEAD
DECAY_LORA = 64
ICL_LORA = 64
GATE_LORA = 128
GN_EPS = 64e-5
D_B = D_MODEL - D_A
POOL_WINDOWS = (2, 4, 8, 16)
POOL_GROUP = D_B // len(POOL_WINDOWS)
C_RW = 3 * D_A + 2 * DECAY_LORA + 2 * ICL_LORA + GATE_LORA
D_IN_EVEN = C_RW + D_B
NA_HEAD = 64
H_C = D_MODEL // NA_HEAD
NA_KH = 8
NA_KW = 16

N_EVEN_2 = (DEPTH + 1) // 2
N_ODD_2 = DEPTH // 2


def layer_norm(x, g, b):
    xf = x.astype(jnp.float32)
    mu = xf.mean(-1, keepdims=True)
    var = jnp.mean(jnp.square(xf - mu), -1, keepdims=True)
    return ((xf - mu) * lax.rsqrt(var + LN_EPS)).astype(x.dtype) * g + b

def swiglu_2(h, w1, w3, w2):
    return (jax.nn.silu(h @ w1) * (h @ w3)) @ w2

def centred_shift_mix(p, mu):
    zero = jnp.zeros_like(p[:, :1])
    prev = jnp.concatenate([zero, p[:, :-1]], axis=1)
    nxt = jnp.concatenate([p[:, 1:], zero], axis=1)
    return p + (prev - p) * mu[0] + (nxt - p) * mu[1]

def rwkv_prepare(p, mu, w0, w2, a0, a2, g2, k_k, k_a):
    B, T, _ = p.shape
    p = centred_shift_mix(p, mu)
    s1 = D_A; s2 = 2 * D_A; s3 = 3 * D_A; s4 = s3 + 2 * DECAY_LORA; s5 = s4 + 2 * ICL_LORA
    r, k, v, wd, ad, gd = jnp.split(p, [s1, s2, s3, s4, s5], axis=-1)
    wd = wd.reshape(B, T, 2, DECAY_LORA)
    ad = ad.reshape(B, T, 2, ICL_LORA)
    f32 = jnp.float32
    logw = -jax.nn.softplus(-(w0 + jnp.einsum('btdr,drc->btdc', jnp.tanh(wd), w2)).astype(f32)) - 0.5
    decay = jnp.exp(-jnp.exp(logw))
    a = jax.nn.sigmoid((a0 + jnp.einsum('btdr,drc->btdc', ad, a2)).astype(f32))
    g = jax.nn.sigmoid(gd) @ g2
    r = r.astype(f32); k = k.astype(f32); v = v.astype(f32)
    kk = (k * k_k).reshape(B, T, H_A, RWKV_HEAD)
    kk = kk / jnp.maximum(jnp.linalg.norm(kk, axis=-1, keepdims=True), 1e-12)
    kd = k[:, :, None, :] * (1.0 + (a - 1.0) * k_a)
    bd = kk.reshape(B, T, 1, D_A) * a
    hs = (B, T, 2, H_A, RWKV_HEAD)
    return (r.reshape(B, T, H_A, RWKV_HEAD), v.reshape(B, T, H_A, RWKV_HEAD), kk,
            decay.reshape(hs), kd.reshape(hs), bd.reshape(hs), g)

def wkv_scan(S0, r, w, k, v, kk, b, reverse):
    def step(S, inp):
        r_t, w_t, k_t, v_t, kk_t, b_t = inp
        sa = -jnp.einsum('bhij,bhj->bhi', S, kk_t)
        S = S * w_t[:, :, None, :] + sa[..., :, None] * b_t[:, :, None, :] + v_t[..., :, None] * k_t[:, :, None, :]
        return S, jnp.einsum('bhij,bhj->bhi', S, r_t)
    xs = tuple(jnp.swapaxes(t, 0, 1) for t in (r, w, k, v, kk, b))
    S, ys = lax.scan(step, S0, xs, reverse=reverse)
    return S, jnp.swapaxes(ys, 0, 1)

def rwkv_readout(y, r, v, kd, g, r_k, lnx_g, lnx_b):
    B, T = y.shape[:2]
    mu = y.mean(-1, keepdims=True)
    var = jnp.mean(jnp.square(y - mu), -1, keepdims=True)
    yn = ((y - mu) * lax.rsqrt(var + GN_EPS)).reshape(B, T, D_A) * lnx_g + lnx_b
    coef = jnp.sum(r[:, :, None] * kd * r_k, axis=(2, 4))
    bonus = (coef[..., None] * v).reshape(B, T, D_A)
    return ((yn + bonus) * g).astype(g.dtype)

def multiscale_pool(p, pool_w, pool_scale):
    B, T, _ = p.shape
    pf = p.astype(jnp.float32)
    cs = jnp.concatenate([jnp.zeros((B, 1, D_B), jnp.float32), jnp.cumsum(pf, axis=1)], axis=1)
    t = jnp.arange(T)
    groups = []
    for gi, win in enumerate(POOL_WINDOWS):
        lo = jnp.clip(t - win // 2, 0, T)
        hi = jnp.clip(t + win // 2, 0, T)
        sl = slice(gi * POOL_GROUP, (gi + 1) * POOL_GROUP)
        cg = cs[:, :, sl]
        mean = (cg[:, hi] - cg[:, lo]) / (hi - lo).astype(jnp.float32)[None, :, None]
        groups.append(mean - pf[:, :, sl])
    pooled = jnp.stack(groups, axis=2).astype(p.dtype)
    y = jnp.einsum('btgc,gcd->btgd', pooled, pool_w).reshape(B, T, D_B)
    return y * pool_scale

def rwkv_pool_mixer(h, hc, want_ctx, w_in, shift_mu, w0, w2, a0, a2, g2, k_k, k_a, r_k,
                    lnx_g, lnx_b, pool_w, pool_scale, w_out):
    B = h.shape[0]
    p_lat = h @ w_in
    p_ctx = hc @ w_in
    lat = rwkv_prepare(p_lat[..., :C_RW], shift_mu, w0, w2, a0, a2, g2, k_k, k_a)
    cx = rwkv_prepare(p_ctx[..., :C_RW], shift_mu, w0, w2, a0, a2, g2, k_k, k_a)
    S0 = jnp.zeros((B, H_A, RWKV_HEAD, RWKV_HEAD), jnp.float32)
    y_lat = 0.0
    y_ctx = 0.0
    for d in range(2):
        rev = d == 1
        S_c, yc = wkv_scan(S0, cx[0], cx[3][:, :, d], cx[4][:, :, d], cx[1], cx[2], cx[5][:, :, d], rev)
        _, yl = wkv_scan(S_c, lat[0], lat[3][:, :, d], lat[4][:, :, d], lat[1], lat[2], lat[5][:, :, d], rev)
        y_lat = y_lat + yl
        if want_ctx:
            y_ctx = y_ctx + yc
    a_lat = rwkv_readout(y_lat, lat[0], lat[1], lat[4], lat[6], r_k, lnx_g, lnx_b)
    b_lat = multiscale_pool(p_lat[..., C_RW:], pool_w, pool_scale)
    out_lat = jnp.concatenate([a_lat, b_lat], axis=-1) @ w_out
    if not want_ctx:
        return out_lat, None
    a_ctx = rwkv_readout(y_ctx, cx[0], cx[1], cx[4], cx[6], r_k, lnx_g, lnx_b)
    b_ctx = multiscale_pool(p_ctx[..., C_RW:], pool_w, pool_scale)
    out_ctx = jnp.concatenate([a_ctx, b_ctx], axis=-1) @ w_out
    return out_lat, out_ctx

def neighbourhood_attention(q, k, v, kc, vc, rpb):
    B, rows = q.shape[:2]
    kh = min(NA_KH, rows)
    kw = NA_KW
    n_loc = kh * kw
    scale = NA_HEAD ** -0.5
    cols = jnp.arange(GRID_W)
    col_start = jnp.clip(cols - kw // 2, 0, GRID_W - kw)
    col_idx = col_start[:, None] + jnp.arange(kw)[None, :]
    col_off = col_idx - cols[:, None] + (NA_KW - 1)

    def row_block(r):
        sr = jnp.clip(r - kh // 2, 0, rows - kh)
        qr = lax.dynamic_index_in_dim(q, r, axis=1, keepdims=False)
        kr = lax.dynamic_slice_in_dim(k, sr, kh, axis=1)
        vr = lax.dynamic_slice_in_dim(v, sr, kh, axis=1)
        kg = jnp.take(kr, col_idx, axis=2).transpose(0, 2, 1, 3, 4, 5).reshape(B, GRID_W, n_loc, H_C, NA_HEAD)
        vg = jnp.take(vr, col_idx, axis=2).transpose(0, 2, 1, 3, 4, 5).reshape(B, GRID_W, n_loc, H_C, NA_HEAD)
        row_off = sr - r + jnp.arange(kh) + (NA_KH - 1)
        bias = rpb[:, row_off[:, None, None], col_off[None, :, :]]
        bias = bias.transpose(0, 2, 1, 3).reshape(H_C, GRID_W, n_loc).astype(jnp.float32)
        s_loc = jnp.einsum('bqhd,bqnhd->bhqn', qr, kg).astype(jnp.float32) * scale + bias
        s_ctx = jnp.einsum('bqhd,bnhd->bhqn', qr, kc).astype(jnp.float32) * scale
        p = jax.nn.softmax(jnp.concatenate([s_loc, s_ctx], axis=-1), axis=-1).astype(v.dtype)
        return (jnp.einsum('bhqn,bqnhd->bqhd', p[..., :n_loc], vg)
                + jnp.einsum('bhqn,bnhd->bqhd', p[..., n_loc:], vc))

    o = lax.map(row_block, jnp.arange(rows))
    return jnp.moveaxis(o, 0, 1)

def na_mixer(h, hc, want_ctx, w_in, rpb, w_out):
    B, L, D = h.shape
    rows = L // GRID_W
    n_ctx = hc.shape[1]
    q, k, v = jnp.split(h @ w_in, 3, axis=-1)
    kc, vc = jnp.split(hc @ w_in[:, D:], 2, axis=-1)
    kc = kc.reshape(B, n_ctx, H_C, NA_HEAD)
    vc = vc.reshape(B, n_ctx, H_C, NA_HEAD)
    gs = (B, rows, GRID_W, H_C, NA_HEAD)
    o = neighbourhood_attention(q.reshape(gs), k.reshape(gs), v.reshape(gs), kc, vc, rpb)
    out_lat = o.reshape(B, L, D) @ w_out
    if not want_ctx:
        return out_lat, None
    qc = (hc @ w_in[:, :D]).reshape(B, n_ctx, H_C, NA_HEAD)
    s = jnp.einsum('bqhd,bkhd->bhqk', qc, kc).astype(jnp.float32) * NA_HEAD ** -0.5
    p = jax.nn.softmax(s, axis=-1).astype(vc.dtype)
    oc = jnp.einsum('bhqk,bkhd->bqhd', p, vc).reshape(B, n_ctx, D)
    return out_lat, oc @ w_out

def second_inputs(seed: int = 0) -> dict:
    key = jax.random.key(seed)
    ks = jax.random.split(key, 32)
    D = D_MODEL
    f32 = jnp.float32

    def n(k, shape, s):
        return jax.random.normal(k, shape, f32) * s

    return {
        'x': n(ks[0], (BATCH, SEQ, D), 1.0),
        'c': n(ks[1], (BATCH, D), 1.0),
        'ctx': n(ks[2], (BATCH, CTX_LEN, D), 1.0),
        'c_ctx': n(ks[3], (D,), 1.0),
        'ada_w': n(ks[4], (DEPTH, D, 6 * D), 0.5 * D ** -0.5),
        'ada_b': n(ks[5], (DEPTH, 6 * D), 0.02),
        'ln_g': 1.0 + n(ks[6], (DEPTH, 2, D), 0.05),
        'ln_b': n(ks[7], (DEPTH, 2, D), 0.02),
        'ffn_w1': n(ks[8], (DEPTH, D, D_FF), D ** -0.5),
        'ffn_w3': n(ks[9], (DEPTH, D, D_FF), D ** -0.5),
        'ffn_w2': n(ks[10], (DEPTH, D_FF, D), BETA * D_FF ** -0.5),
        'ev_w_in': n(ks[11], (N_EVEN_2, D, D_IN_EVEN), D ** -0.5),
        'ev_shift_mu': jax.random.uniform(ks[12], (N_EVEN_2, 2, C_RW), f32, 0.0, 0.5),
        'ev_w0': jax.random.uniform(ks[13], (N_EVEN_2, 2, D_A), f32, -6.5, -1.5),
        'ev_w2': n(ks[14], (N_EVEN_2, 2, DECAY_LORA, D_A), 0.5 * DECAY_LORA ** -0.5),
        'ev_a0': n(ks[15], (N_EVEN_2, 2, D_A), 0.1),
        'ev_a2': n(ks[16], (N_EVEN_2, 2, ICL_LORA, D_A), 0.5 * ICL_LORA ** -0.5),
        'ev_g2': n(ks[17], (N_EVEN_2, GATE_LORA, D_A), GATE_LORA ** -0.5),
        'ev_k_k': 0.85 + n(ks[18], (N_EVEN_2, D_A), 0.05),
        'ev_k_a': 1.0 + n(ks[19], (N_EVEN_2, D_A), 0.05),
        'ev_r_k': n(ks[20], (N_EVEN_2, H_A, RWKV_HEAD), 0.1),
        'ev_lnx_g': 1.0 + n(ks[21], (N_EVEN_2, D_A), 0.05),
        'ev_lnx_b': n(ks[22], (N_EVEN_2, D_A), 0.02),
        'ev_pool_w': n(ks[23], (N_EVEN_2, len(POOL_WINDOWS), POOL_GROUP, POOL_GROUP), POOL_GROUP ** -0.5),
        'ev_pool_scale': 1.0 + n(ks[24], (N_EVEN_2, D_B), 0.1),
        'ev_w_out': n(ks[25], (N_EVEN_2, D, D), BETA * D ** -0.5),
        'od_w_in': n(ks[26], (N_ODD_2, D, 3 * D), D ** -0.5),
        'od_rpb': n(ks[27], (N_ODD_2, H_C, 2 * NA_KH - 1, 2 * NA_KW - 1), 0.05),
        'od_w_out': n(ks[28], (N_ODD_2, D, D), BETA * D ** -0.5),
    }

def second_block(x, c, ctx, c_ctx, ada_w, ada_b, ln_g, ln_b, ffn_w1, ffn_w3, ffn_w2,
              ev_w_in, ev_shift_mu, ev_w0, ev_w2, ev_a0, ev_a2, ev_g2, ev_k_k, ev_k_a, ev_r_k,
              ev_lnx_g, ev_lnx_b, ev_pool_w, ev_pool_scale, ev_w_out,
              od_w_in, od_rpb, od_w_out):
    xc = ctx
    for i in range(DEPTH):
        last = i == DEPTH - 1
        want_ctx = not last
        j = i // 2
        mod = jax.nn.silu(c) @ ada_w[i] + ada_b[i]
        mod_c = jax.nn.silu(c_ctx) @ ada_w[i] + ada_b[i]
        sh_m, sc_m, g_m, sh_f, sc_f, g_f = jnp.split(mod[:, None, :], 6, axis=-1)
        shc_m, scc_m, gc_m, shc_f, scc_f, gc_f = jnp.split(mod_c, 6, axis=-1)
        h = x * (1.0 + sc_m) + sh_m
        hc = xc * (1.0 + scc_m) + shc_m
        if i % 2 == 0:
            y, yc = rwkv_pool_mixer(h, hc, want_ctx, ev_w_in[j], ev_shift_mu[j], ev_w0[j], ev_w2[j],
                                    ev_a0[j], ev_a2[j], ev_g2[j], ev_k_k[j], ev_k_a[j], ev_r_k[j],
                                    ev_lnx_g[j], ev_lnx_b[j], ev_pool_w[j], ev_pool_scale[j], ev_w_out[j])
        else:
            y, yc = na_mixer(h, hc, want_ctx, od_w_in[j], od_rpb[j], od_w_out[j])
        x = layer_norm(ALPHA * x + g_m * y, ln_g[i, 0], ln_b[i, 0])
        h = x * (1.0 + sc_f) + sh_f
        x = layer_norm(ALPHA * x + g_f * swiglu_2(h, ffn_w1[i], ffn_w3[i], ffn_w2[i]), ln_g[i, 1], ln_b[i, 1])
        if want_ctx:
            xc = layer_norm(ALPHA * xc + gc_m * yc, ln_g[i, 0], ln_b[i, 0])
            hc = xc * (1.0 + scc_f) + shc_f
            xc = layer_norm(ALPHA * xc + gc_f * swiglu_2(hc, ffn_w1[i], ffn_w3[i], ffn_w2[i]), ln_g[i, 1], ln_b[i, 1])
    return x


def setup_inputs(seed=0):
    out = dict(first_inputs(seed))
    for name, value in second_inputs(seed + 1).items():
        if name != "x":
            out[name + "_2"] = value
    return out


def reference(
    x, c, ctx, c_ctx, ada_w, ada_b, norm1_g, norm2_g, ffn_w_in, ffn_w_out, even_w_in,
    even_w_out, sgu_w, sgu_b, diff_lq1, diff_lk1, diff_lq2, diff_lk2, diff_subln_g, odd_w_qkv,
    odd_w_out, odd_sink, final_g, c_2, ctx_2, c_ctx_2, ada_w_2, ada_b_2, ln_g_2, ln_b_2,
    ffn_w1_2, ffn_w3_2, ffn_w2_2, ev_w_in_2, ev_shift_mu_2, ev_w0_2, ev_w2_2, ev_a0_2, ev_a2_2,
    ev_g2_2, ev_k_k_2, ev_k_a_2, ev_r_k_2, ev_lnx_g_2, ev_lnx_b_2, ev_pool_w_2, ev_pool_scale_2,
    ev_w_out_2, od_w_in_2, od_rpb_2, od_w_out_2,
):
    x = first_block(
        x, c, ctx, c_ctx, ada_w, ada_b, norm1_g, norm2_g, ffn_w_in, ffn_w_out, even_w_in,
        even_w_out, sgu_w, sgu_b, diff_lq1, diff_lk1, diff_lq2, diff_lk2, diff_subln_g,
        odd_w_qkv, odd_w_out, odd_sink, final_g,
    )
    return second_block(
        x, c_2, ctx_2, c_ctx_2, ada_w_2, ada_b_2, ln_g_2, ln_b_2, ffn_w1_2, ffn_w3_2, ffn_w2_2,
        ev_w_in_2, ev_shift_mu_2, ev_w0_2, ev_w2_2, ev_a0_2, ev_a2_2, ev_g2_2, ev_k_k_2,
        ev_k_a_2, ev_r_k_2, ev_lnx_g_2, ev_lnx_b_2, ev_pool_w_2, ev_pool_scale_2, ev_w_out_2,
        od_w_in_2, od_rpb_2, od_w_out_2,
    )


_drawn_inputs = setup_inputs


def setup_inputs(seed=0):
    import zlib

    import numpy as np

    out = dict(_drawn_inputs(seed))
    spreads = {}
    factors = {'norm1_g': 8.0,
     'norm2_g': 6.718,
     'sgu_b': 3.604,
     'diff_lq1': 200.0,
     'diff_lk1': 4.423,
     'diff_lq2': 4.447,
     'diff_subln_g': 8.0,
     'odd_sink': 8.0,
     'final_g': 2.812,
     'ctx_2': 14.806,
     'ada_b_2': 5.44,
     'ev_w2_2': 8.0,
     'ev_a0_2': 8.0,
     'ev_a2_2': 6.339,
     'ev_k_k_2': 170.932,
     'ev_k_a_2': 6.936,
     'ev_r_k_2': 3.054,
     'ev_lnx_g_2': 200.0,
     'ev_lnx_b_2': 200.0,
     'ev_pool_scale_2': 37.187,
     'od_rpb_2': 64.0}
    for name, (base, spread) in spreads.items():
        noise = np.random.default_rng([zlib.crc32(name.encode()), seed]).standard_normal(out[name].shape)
        drawn = base * np.exp(spread * noise) if base else spread * noise
        out[name] = __import__('jax').numpy.asarray(drawn.astype(out[name].dtype))
    for name, factor in factors.items():
        out[name] = (out[name] * factor).astype(out[name].dtype)
    return out
```

```python
import math
from contextlib import ExitStack

import concourse.bass as bass
from concourse import mybir

F32 = mybir.dt.float32
ALU = mybir.AluOpType
ACT = mybir.ActivationFunctionType
AX = mybir.AxisListType

P = 128
D = 1024
KC = D // P
LAT, CTX = 512, 256
TOK = LAT + CTX
HEAD = 64
GRID_W = 64
FF = 2816
FC = FF // P
HALF = FC // 2
RING = 4
SLOT = HALF * P
EPS = 1e-6
GN_EPS = 64e-5
ALPHA = 4 ** 0.25
LAM_INIT = 0.8 - 0.6 * math.exp(-0.3 * 0)
SCALE = HEAD ** -0.5
RC = 64
NCH = TOK // RC
PAIRS = 6
RW = 21
NEG = -1e30
DR = 2 * 8 - 1
DCOL = 2 * 16 - 1
PADW = 2 * GRID_W - 1
LEVELS = 6

SMALL = [("c", 8), ("cc", 8), ("c2", 8), ("cc2", 8), ("ada_b", 96), ("ada_b2", 96), ("norm1", 16), ("norm2", 16),
         ("final", 8), ("subln", 1), ("ln_g", 32), ("ln_b", 32), ("mu_lora", 6), ("pool_scale", 2)]
COL = {}
for _name, _n in SMALL:
    COL[_name] = (sum(n for _, n in SMALL[:len(COL)]), _n)
NSMALL = sum(n for _, n in SMALL)
PAIRCOL = {n: c for c, n in enumerate(["mu0r", "mu0k", "mu0v", "mu1r", "mu1k", "mu1v", "w0_0", "w0_1", "a0_0", "a0_1",
                                       "k_k", "k_a", "r_k", "lnx_g", "lnx_b"])}
NPAIR = len(PAIRCOL)
ROWCOL = {"lam": 0, "sink": 256, "sgu_b": 272}
NROWS = 784


class Stage:

    def __init__(self, k, name):
        self.k, self.name = k, name

    def __enter__(self):
        k = self.k
        self.ids = list(k.sem_pools[k.stage_no % 2])
        self.clear = k.sem_pools[(k.stage_no + 1) % 2] if k.stage_no else None
        self.first = self.ids[0]
        self.mine = []
        self.stack = ExitStack()
        self.block = self.stack.enter_context(k.nc.Block(f"{self.name}_{k.stage_no}", no_gpsimd_drain=True))
        k.stage_no += 1
        return self

    def sem(self, name):
        s = self.k.nc.alloc_semaphore(f"{self.name}_{self.k.stage_no}_{name}", num=self.ids.pop(0))
        self.mine.append(s)
        return s

    def sb(self, name, shape):
        return self.k.tmp.enter_context(self.k.nc.sbuf_tensor(f"{self.name}_{self.k.stage_no}_{name}", shape, F32))

    def clear_last(self, pool):
        if self.clear:
            pool.sem_clear(range(self.clear[0], self.clear[-1] + 1))

    def __exit__(self, *a):
        self.stack.close()
        for s in self.mine:
            self.k.nc.release_semaphore(s)


class Feed:

    def __init__(self, k, plan):
        self.plan, self.at = plan, 0
        self.ring = k.ring
        self.landed = [k.nc.alloc_semaphore(f"weights_landed{s}") for s in range(RING)]
        self.used = [k.nc.alloc_semaphore(f"weights_used{s}") for s in range(RING)]
        base = [0] * RING
        self.base = []
        for _, n, pattern in plan:
            self.base.append(list(base))
            for slot, *_ in pattern:
                base[slot] += n

    def count(self, stage, j):
        _, _, pattern = self.plan[stage]
        slot = pattern[j][0]
        before = self.base[stage][slot] + sum(1 for e in pattern[:j] if e[0] == slot)
        return slot, before, sum(1 for e in pattern if e[0] == slot)

    def issue(self, sp, stage, i, ahead=None):
        for j, (slot, src, mul, off) in enumerate(self.plan[stage][2]):
            slot, before, per = self.count(stage, j)
            if ahead is not None and ahead != (before == self.base[stage][slot]):
                continue
            if not (isinstance(i, int) and before + per * i == 0):
                sp.wait_ge(self.used[slot], per * i + before)
            w = src.shape[2]
            t = src[mul * i + off] if isinstance(i, int) else src[bass.ds(mul * i + off, 1)].rearrange("a p w -> (a p) w")
            sp.dma_start(self.ring[:, slot, 0:w], t).then_inc(self.landed[slot], 16)

    def program(self, sp):
        s = self.at
        n = self.plan[s][1]
        self.issue(sp, s, 0, ahead=False)
        if n > 1:
            with sp.Fori(1, n) as i:
                self.issue(sp, s, i)
        if s + 1 < len(self.plan):
            self.issue(sp, s + 1, 0, ahead=True)

    def wait(self, pe, i, j):
        slot, before, per = self.count(self.at, j)
        pe.wait_ge(self.landed[slot], 16 * per * i + 16 * (before + 1))
        return slot

    def done(self, matmul, j):
        matmul.then_inc(self.used[self.count(self.at, j)[0]], 1)

    def wait_done(self, eng, i, j):
        slot, before, per = self.count(self.at, j)
        eng.wait_ge(self.used[slot], per * i + before + 1)


def spans(tokens):
    return [(0, LAT, 0), (LAT, TOK, 1)] if tokens == TOK else [(0, LAT, 0)]


class K:
    pass


def program(nc, io, out):
    k = K()
    k.nc = nc
    k.io = io
    k.stage_no = 0
    with ExitStack() as ctx:
        def sb(name, shape):
            return ctx.enter_context(nc.sbuf_tensor(name, shape, F32))

        k.h = sb("h", [P, KC, TOK])
        k.hn = sb("hn", [P, KC, TOK])
        k.mo = sb("mo", [P, KC, TOK])
        k.ring = sb("ring", [P, RING, SLOT])
        k.small = sb("small", [P, NSMALL])
        k.mod = sb("mod", [P, 6 * KC, 2])
        k.ident = sb("ident", [P, P])
        k.ones = sb("ones", [P, P])
        k.eps = sb("eps", [P, 2])
        k.ps = ctx.enter_context(nc.psum_tensor("ps", [P, 8, 512], F32))
        k.psf = k.ps[:, :, :].rearrange("p b n -> p (b n)")
        k.setup_sem = nc.alloc_semaphore("setup_sem")
        k.out_sem = nc.alloc_semaphore("out_sem")
        k.rows_sem = nc.alloc_semaphore("rows_sem")
        k.bias_sem = nc.alloc_semaphore("bias_sem")
        k.pair_landed = nc.alloc_semaphore("pair_landed")
        k.bias_landed = [nc.alloc_semaphore(f"bias_landed{j}") for j in range(4)]
        k.feed = Feed(k, weight_plan(io))
        first = max(s.num for s in k.feed.used) + 1
        k.sem_pools = [range(first, first + 40), range(first + 40, first + 80)]
        k.padded = nc.dram_tensor("padded_bias", (16 * DR, PADW), F32).ap()
        k.toeplitz = nc.dram_tensor("toeplitz_bias", (16, GRID_W, DR, GRID_W), F32).ap()

        load_inputs(k)
        modulation(k, "c", "cc", "ada_b", 0)
        rms_modulate(k, TOK, 1, 0, "norm1", 0)
        with ExitStack() as k.tmp:
            gating_mlp(k)
        with ExitStack() as k.tmp:
            diff_attention(k)
        project_out(k, TOK, 2)
        rms_modulate(k, TOK, 4, 3, "norm2", 0)
        with ExitStack() as k.tmp:
            feed_forward(k, TOK, 5)
        modulation(k, "c", "cc", "ada_b", 1)
        rms_modulate(k, TOK, 1, 0, "norm1", 1)
        with ExitStack() as k.tmp:
            window_attention(k)
        project_out(k, LAT, 2)
        rms_modulate(k, LAT, 4, 3, "norm2", 1)
        with ExitStack() as k.tmp:
            feed_forward(k, LAT, 5)
        rms_modulate(k, LAT, None, None, "final", 0)
        modulation(k, "c2", "cc2", "ada_b2", 0)
        affine(k, TOK, 1, 0, load_context=True)
        with ExitStack() as k.tmp:
            rwkv(k)
        project_out(k, TOK, 2)
        layer_norm(k, TOK, 0)
        affine(k, TOK, 4, 3)
        with ExitStack() as k.tmp:
            feed_forward(k, TOK, 5)
        layer_norm(k, TOK, 1)
        modulation(k, "c2", "cc2", "ada_b2", 1)
        affine(k, TOK, 1, 0)
        with ExitStack() as k.tmp:
            neighbourhood_attention(k)
        project_out(k, LAT, 2)
        layer_norm(k, LAT, 2)
        affine(k, LAT, 4, 3)
        with ExitStack() as k.tmp:
            feed_forward(k, LAT, 5)
        layer_norm(k, LAT, 3)
        store(k, out)


def weight_plan(io):
    def ada(w):
        return ("modulation", 12, [(s, w, 4, s) for s in range(4)])

    def out(w):
        return ("project_out", 2, [(s, w, 4, s) for s in range(4)])

    def ffn(g, u, d):
        return [("feed_up", FC // 2, [(0, g, 2, 0), (1, u, 2, 0), (2, g, 2, 1), (3, u, 2, 1)]),
                ("feed_down", 4, [(s, d, 4, s) for s in range(4)])]

    ew, ow, rw, nw = io["even_in"], io["odd_in"], io["ev_in"], io["od_in"]
    return [
        ada(io["ada0"]),
        ("gating", 2, [(0, ew, 2, 0), (1, ew, 2, 4), (2, ew, 2, 1), (3, ew, 2, 5)]),
        ("diff", 4, [(0, ew, 1, 8), (1, ew, 1, 12), (2, ew, 1, 16)]),
        out(io["even_out"]), *ffn(io["ffn_g0"], io["ffn_u0"], io["ffn_d0"]),
        ada(io["ada1"]),
        ("window", 2, [(0, ow, 1, 8), (1, ow, 1, 10)] + [((2 + j) % 4, ow, 4, j) for j in range(4)]),
        out(io["odd_out"]), *ffn(io["ffn_g1"], io["ffn_u1"], io["ffn_d1"]),
        ada(io["ada2"]),
        ("lora", 1, [(j % 4, rw, 0, 18 + j) for j in range(5)]),
        ("rwkv", PAIRS, [(1, rw, 1, 0), (2, rw, 1, 6), (3, rw, 1, 12)]),
        out(io["ev_out"]), *ffn(io["ffn_g2"], io["ffn_u2"], io["ffn_d2"]),
        ada(io["ada3"]),
        ("neighbour", 8, [(0, nw, 1, 0), (1, nw, 1, 8), (2, nw, 1, 16)]),
        out(io["od_out"]), *ffn(io["ffn_g3"], io["ffn_u3"], io["ffn_d3"]),
    ]


def col(k, name, at=0, n=1):
    a = COL[name][0] + at
    return k.small[:, a:a + n]


def region(k, r, n=TOK):
    return k.psf[:, 1024 * r:1024 * r + n]


def load_inputs(k):
    with Stage(k, "load") as st:
        @st.block.sync
        def _(sp):
            for dst, src in ((k.small[:, :], k.io["small"]), (k.ident[:, :], k.io["ident"]),
                             (k.h[:, :, :], k.io["h0"])):
                sp.dma_start(dst, src).then_inc(k.setup_sem, 16)
            k.feed.issue(sp, 0, 0, ahead=True)
            sp.wait_ge(k.setup_sem, 48)

        @st.block.gpsimd
        def _(pool):
            zeros = k.mo[0:120, 0, 0:2 * PADW]
            pool.memset(k.mo[:, 0, :], 0.0)
            pool.drain()
            pool.dma_start(k.padded.rearrange("(p r) c -> p (r c)", p=120), zeros).then_inc(k.bias_sem, 16)
            pool.wait_ge(k.bias_sem, 16)
            left = (PADW - DCOL) // 2
            pool.dma_start(k.padded[:, left:left + DCOL], k.io["rpb"]).then_inc(k.bias_sem, 16)
            pool.wait_ge(k.bias_sem, 32)
            with pool.Fori(0, GRID_W) as q:
                pool.dma_start(k.toeplitz[:, bass.ds(q, 1), :, :].rearrange("h a r c -> (h a) r c"),
                               k.padded.rearrange("(h r) c -> h r c", h=16)[:, :, bass.ds(GRID_W - 1 - q, GRID_W)]).then_inc(k.bias_sem, 16)

        @st.block.vector
        def _(dve):
            dve.memset(k.ones[:, :], 1.0)
            dve.memset(k.eps[:, 0:1], EPS)
            dve.memset(k.eps[:, 1:2], GN_EPS)


def store(k, out):
    with Stage(k, "store") as st:
        @st.block.sync
        def _(sp):
            sp.dma_start(out, k.h[:, :, 0:LAT]).then_inc(k.out_sem, 16)
            sp.wait_ge(k.out_sem, 16)


def modulation(k, c, cc, bias, layer):
    feed = k.feed
    with ExitStack() as k.tmp, Stage(k, "modulation") as st:
        vec = st.sb("vec", [P, KC, 2])
        silu_ready, products_read = st.sem("silu_ready"), st.sem("products_read")
        psum = k.ps[:, 0:RING, 0:2]

        @st.block.sync
        def _(sp):
            feed.program(sp)

        @st.block.gpsimd
        def _(pool):
            st.clear_last(pool)

        @st.block.scalar
        def _(act):
            act.activation(vec[:, :, 0], col(k, c, 0, KC), ACT.Silu)
            act.activation(vec[:, :, 1], col(k, cc, 0, KC), ACT.Silu).then_inc(silu_ready, 1)

        @st.block.tensor
        def _(pe):
            pe.wait_ge(silu_ready, 1)
            with pe.Fori(0, 12) as i:
                pe.wait_ge(products_read, i + 1)
                for j in range(RING):
                    slot = feed.wait(pe, i, j)
                    for c_ in range(KC):
                        mm = pe.matmul(psum[:, j, :], k.ring[:, slot, c_ * P:(c_ + 1) * P], vec[:, c_, :],
                                       start=c_ == 0, stop=c_ == KC - 1)
                    feed.done(mm, j)

        @st.block.vector
        def _(dve):
            b = col(k, bias, layer * 48, 48)
            dve.sem_inc(products_read, 1)
            with dve.Fori(0, 12) as i:
                feed.wait_done(dve, i, RING - 1)
                for s in range(2):
                    ins = dve.tensor_tensor(k.mod[:, bass.ds(4 * i, 4), s], psum[:, :, s], b[:, bass.ds(4 * i, 4)], ALU.add)
                ins.then_inc(products_read, 1)
    feed.at += 1


def rms_modulate(k, tokens, scale_at, shift_at, gain, layer):
    final = scale_at is None
    dst = k.h if final else k.hn
    with ExitStack() as k.tmp, Stage(k, "rms") as st:
        sq = st.sb("sq", [P, 2, TOK])
        gains = st.sb("gains", [P, KC, 2])
        rstd = st.sb("rstd", [P, TOK])
        squared, summed, gains_ready = st.sem("squared"), st.sem("summed"), st.sem("gains_ready")
        var_ready, root_ready = st.sem("var_ready"), st.sem("root_ready")
        scaled, shifted = st.sem("scaled"), st.sem("shifted")
        acc = region(k, 0, tokens)

        @st.block.gpsimd
        def _(pool):
            st.clear_last(pool)

        @st.block.scalar
        def _(act):
            for c in range(KC):
                if c >= 2:
                    act.wait_ge(summed, c - 1)
                act.activation(sq[:, c % 2, 0:tokens], k.h[:, c, 0:tokens], ACT.Square).then_inc(squared, 1)
            act.wait_ge(var_ready, 1)
            act.activation(rstd[:, 0:tokens], rstd[:, 0:tokens], ACT.Sqrt).then_inc(root_ready, 1)
            act.wait_ge(gains_ready, 1)
            for c in range(KC):
                act.wait_ge(scaled, c + 1)
                for a, b, s in spans(tokens):
                    shift = 0.0 if final else k.mod[:, shift_at * KC + c, s:s + 1]
                    ins = act.activation(dst[:, c, a:b], sq[:, c % 2, a:b], ACT.Identity,
                                         scale=gains[:, c, s:s + 1], bias=shift)
                ins.then_inc(shifted, 1)

        @st.block.tensor
        def _(pe):
            for c in range(KC):
                pe.wait_ge(squared, c + 1)
                for a, b, _ in spans(tokens):
                    mm = pe.matmul(acc[:, a:b], k.ones[:, :], sq[:, c % 2, a:b], start=c == 0, stop=c == KC - 1)
                mm.then_inc(summed, 1)

        @st.block.vector
        def _(dve):
            g = col(k, gain, layer * KC, KC)
            for s in range(2):
                if final:
                    ins = dve.tensor_copy(gains[:, :, s], g)
                else:
                    ins = dve.scalar_tensor_tensor(out=gains[:, :, s], in0=k.mod[:, scale_at * KC:(scale_at + 1) * KC, s],
                                                   scalar=1.0, in1=g, op0=ALU.add, op1=ALU.mult)
            ins.then_inc(gains_ready, 1)
            dve.wait_ge(summed, KC)
            dve.tensor_scalar(rstd[:, 0:tokens], acc, 1.0 / D, EPS, ALU.mult, ALU.add).then_inc(var_ready, 1)
            dve.wait_ge(root_ready, 1)
            dve.reciprocal(rstd[:, 0:tokens], rstd[:, 0:tokens])
            dve.drain()
            for c in range(KC):
                if c >= 2:
                    dve.wait_ge(shifted, c - 1)
                dve.tensor_tensor(sq[:, c % 2, 0:tokens], k.h[:, c, 0:tokens], rstd[:, 0:tokens], ALU.mult).then_inc(scaled, 1)


def affine(k, tokens, scale_at, shift_at, load_context=False):
    with ExitStack() as k.tmp, Stage(k, "affine") as st:
        gains = st.sb("gains", [P, KC, 2])
        gains_ready, copied, context_landed = st.sem("gains_ready"), st.sem("copied"), st.sem("context_landed")

        @st.block.sync
        def _(sp):
            if load_context:
                sp.dma_start(k.h[:, :, LAT:TOK], k.io["ctx2"]).then_inc(context_landed, 16)

        @st.block.gpsimd
        def _(pool):
            st.clear_last(pool)

        @st.block.scalar
        def _(act):
            act.wait_ge(gains_ready, 1)
            if load_context:
                act.wait_ge(context_landed, 16)
            for c in range(KC):
                for a, b, s in spans(tokens):
                    ins = act.activation(k.hn[:, c, a:b], k.h[:, c, a:b], ACT.Identity,
                                         scale=gains[:, c, s:s + 1], bias=k.mod[:, shift_at * KC + c, s:s + 1])
                ins.then_inc(copied, 1)

        @st.block.vector
        def _(dve):
            dve.tensor_scalar(gains[:, :, :], k.mod[:, scale_at * KC:(scale_at + 1) * KC, :], 1.0, None,
                              ALU.add).then_inc(gains_ready, 1)
            for c in range(KC):
                dve.wait_ge(copied, c + 1)
                dve.tensor_scalar(k.h[:, c, 0:tokens], k.h[:, c, 0:tokens], ALPHA, None, ALU.mult)


def layer_norm(k, tokens, which):
    with ExitStack() as k.tmp, Stage(k, "layernorm") as st:
        sq = st.sb("sq", [P, 2, TOK])
        rstd = st.sb("rstd", [P, TOK])
        mean_ready, centred, squared, summed = st.sem("mean_ready"), st.sem("centred"), st.sem("squared"), st.sem("summed")
        var_ready, root_ready, scaled = st.sem("var_ready"), st.sem("root_ready"), st.sem("scaled")
        total, acc = region(k, 0, tokens), region(k, 1, tokens)

        @st.block.gpsimd
        def _(pool):
            st.clear_last(pool)

        @st.block.tensor
        def _(pe):
            for c in range(KC):
                for a, b, _ in spans(tokens):
                    mm = pe.matmul(total[:, a:b], k.ones[:, :], k.h[:, c, a:b], start=c == 0, stop=c == KC - 1)
            mm.then_inc(mean_ready, 1)
            for c in range(KC):
                pe.wait_ge(squared, c + 1)
                for a, b, _ in spans(tokens):
                    mm = pe.matmul(acc[:, a:b], k.ones[:, :], sq[:, c % 2, a:b], start=c == 0, stop=c == KC - 1)
                mm.then_inc(summed, 1)

        @st.block.vector
        def _(dve):
            dve.wait_ge(mean_ready, 1)
            for c in range(KC):
                dve.scalar_tensor_tensor(out=k.h[:, c, 0:tokens], in0=total, scalar=-1.0 / D, in1=k.h[:, c, 0:tokens],
                                         op0=ALU.mult, op1=ALU.add).then_inc(centred, 1)
            dve.wait_ge(summed, KC)
            dve.tensor_scalar(rstd[:, 0:tokens], acc, 1.0 / D, EPS, ALU.mult, ALU.add).then_inc(var_ready, 1)
            dve.wait_ge(root_ready, 1)
            dve.reciprocal(rstd[:, 0:tokens], rstd[:, 0:tokens])
            dve.drain()
            for c in range(KC):
                dve.tensor_tensor(k.h[:, c, 0:tokens], k.h[:, c, 0:tokens], rstd[:, 0:tokens], ALU.mult).then_inc(scaled, 1)

        @st.block.scalar
        def _(act):
            for c in range(KC):
                act.wait_ge(centred, c + 1)
                if c >= 2:
                    act.wait_ge(summed, c - 1)
                act.activation(sq[:, c % 2, 0:tokens], k.h[:, c, 0:tokens], ACT.Square).then_inc(squared, 1)
            act.wait_ge(var_ready, 1)
            act.activation(rstd[:, 0:tokens], rstd[:, 0:tokens], ACT.Sqrt).then_inc(root_ready, 1)
            for c in range(KC):
                act.wait_ge(scaled, c + 1)
                act.activation(k.h[:, c, 0:tokens], k.h[:, c, 0:tokens], ACT.Identity,
                               scale=col(k, "ln_g", which * KC + c), bias=col(k, "ln_b", which * KC + c))


def tile_products(k, pe, i, j, dst, src, tokens, chunks=range(KC), first=True, last=True):
    slot = k.feed.wait(pe, i, j)
    for a, b, _ in spans(tokens):
        for n, c in enumerate(chunks):
            mm = pe.matmul(dst[:, a:b], k.ring[:, slot, n * P:(n + 1) * P], src[:, c, a:b],
                           start=first and n == 0, stop=last and n == len(chunks) - 1)
    k.feed.done(mm, j)


def token_products(k, pe, i, j, dst, src, tokens):
    slot = k.feed.wait(pe, i, j)
    for t in range(tokens // P):
        for c in range(KC):
            mm = pe.matmul(dst[:, t * P:(t + 1) * P], src[:, c, t * P:(t + 1) * P], k.ring[:, slot, c * P:(c + 1) * P],
                           start=c == 0, stop=c == KC - 1)
    k.feed.done(mm, j)


def project_out(k, tokens, gate_at):
    with ExitStack() as k.tmp, Stage(k, "project") as st:
        free = st.sem("psum_free")

        @st.block.sync
        def _(sp):
            k.feed.program(sp)

        @st.block.gpsimd
        def _(pool):
            st.clear_last(pool)

        @st.block.tensor
        def _(pe):
            with pe.Fori(0, 2) as i:
                for j in range(4):
                    pe.wait_ge(free, 4 * i + j + 1)
                    tile_products(k, pe, i, j, region(k, j, tokens), k.mo, tokens)

        @st.block.vector
        def _(dve):
            dve.sem_inc(free, 4)
            with dve.Fori(0, 2) as i:
                for j in range(4):
                    k.feed.wait_done(dve, i, j)
                    residual(k, dve, tokens, gate_at, 4 * i + j, j).then_inc(free, 1)
    k.feed.at += 1


def residual(k, dve, tokens, gate_at, n, r):
    for a, b, s in spans(tokens):
        hs = k.h[:, bass.ds(n, 1), a:b].rearrange("p a t -> p (a t)")
        ins = dve.scalar_tensor_tensor(out=hs, in0=region(k, r)[:, a:b], scalar=k.mod[:, bass.ds(n + gate_at * KC, 1), s],
                                       in1=hs, op0=ALU.mult, op1=ALU.add)
    return ins


def feed_forward(k, tokens, gate_at):
    feed = k.feed
    with ExitStack() as k.tmp:
        hidden = k.tmp.enter_context(k.nc.sbuf_tensor(f"hidden{k.stage_no}", [P, FC, tokens], F32))
        with Stage(k, "feed_up") as st:
            gate = st.sb("gate", [P, 2, tokens])
            gate_free, up_free = st.sem("gate_free"), st.sem("up_free")

            @st.block.sync
            def _(sp):
                feed.program(sp)

            @st.block.gpsimd
            def _(pool):
                st.clear_last(pool)

            @st.block.tensor
            def _(pe):
                with pe.Fori(0, FC // 2) as i:
                    for p in range(2):
                        pe.wait_ge(gate_free, 2 * i + p + 1)
                        tile_products(k, pe, i, 2 * p, region(k, 2 * p, tokens), k.hn, tokens)
                        pe.wait_ge(up_free, 2 * i + p + 1)
                        tile_products(k, pe, i, 2 * p + 1, region(k, 2 * p + 1, tokens), k.hn, tokens)

            @st.block.scalar
            def _(act):
                act.sem_inc(gate_free, 2)
                with act.Fori(0, FC // 2) as i:
                    for p in range(2):
                        feed.wait_done(act, i, 2 * p)
                        act.wait_ge(up_free, 2 * i + p + 1)
                        act.activation(gate[:, p, :], region(k, 2 * p, tokens), ACT.Silu).then_inc(gate_free, 1)

            @st.block.vector
            def _(dve):
                dve.sem_inc(up_free, 2)
                with dve.Fori(0, FC // 2) as i:
                    for p in range(2):
                        feed.wait_done(dve, i, 2 * p + 1)
                        dve.wait_ge(gate_free, 2 * i + p + 3)
                        dve.tensor_tensor(hidden[:, bass.ds(2 * i + p, 1), :].rearrange("p a t -> p (a t)"),
                                          gate[:, p, :], region(k, 2 * p + 1, tokens), ALU.mult).then_inc(up_free, 1)
        feed.at += 1
        with Stage(k, "feed_down") as st:
            free = st.sem("psum_free")

            @st.block.sync
            def _(sp):
                feed.program(sp)

            @st.block.gpsimd
            def _(pool):
                st.clear_last(pool)

            @st.block.tensor
            def _(pe):
                with pe.Fori(0, 4) as i:
                    for b in range(2):
                        pe.wait_ge(free, 2 * i + b + 1)
                        for a0, b0, _ in spans(tokens):
                            for half in range(2):
                                slot = feed.wait(pe, i, 2 * b + half)
                                for n in range(HALF):
                                    mm = pe.matmul(region(k, b)[:, a0:b0], k.ring[:, slot, n * P:(n + 1) * P],
                                                   hidden[:, half * HALF + n, a0:b0], start=half == 0 and n == 0,
                                                   stop=half == 1 and n == HALF - 1)
                                if b0 == tokens:
                                    feed.done(mm, 2 * b + half)

            @st.block.vector
            def _(dve):
                dve.sem_inc(free, 2)
                with dve.Fori(0, 4) as i:
                    for b in range(2):
                        feed.wait_done(dve, i, 2 * b + 1)
                        residual(k, dve, tokens, gate_at, 2 * i + b, b).then_inc(free, 1)
        feed.at += 1


def constants(k, st, *names):
    return [st.sb(n, list(k.io[n].shape)) for n in names]


class Attention:

    def __init__(self, k, st, units, subs, scale, prepare=None, sinks=None, lam=None):
        self.k, self.st, self.units, self.subs, self.scale = k, st, units, subs, scale
        self.prepare, self.sinks, self.lam = prepare, sinks, lam
        self.probs = st.sb("probs", [P, 2, TOK])
        self.turned = st.sb("turned", [P, 2, TOK])
        self.scores = st.sb("scores", [P, 2, TOK]) if prepare else None
        self.mixed = st.sb("mixed", [P, TOK]) if subs == 2 else None
        self.negmax = st.sb("negmax", [P, 2])
        self.rowmax = st.sb("rowmax", [P, 2])
        self.sums = st.sb("sums", [P, 2])
        self.sinkexp = st.sb("sinkexp", [P, 2])
        self.recip = st.sb("recip", [P, 2])
        self.scores_ready = st.sem("scores_ready")
        self.max_ready = st.sem("max_ready")
        self.exp_done = st.sem("exp_done")
        self.probs_ready = st.sem("probs_ready")
        self.turn_done = st.sem("turn_done")
        self.turned_ready = st.sem("turned_ready")
        self.values_done = st.sem("values_done")

    def slot(self, u, s):
        return s if self.subs == 2 else u % 2

    def tensor(self, pe, i, lo, hi):
        U = len(self.units)

        def scores(u):
            for s, products in enumerate(self.units[u]["scores"]):
                if self.subs == 2 and u > 0:
                    pe.wait_ge(self.exp_done, i * U + u)
                if self.subs == 1 and u > 1:
                    pe.wait_ge(self.max_ready, i * U + u - 1)
                for q, key, c, n in products:
                    mm = pe.matmul(region(self.k, 1 + self.slot(u, s))[:, c:c + n], q, key, start=True, stop=True)
                mm.then_inc(self.scores_ready, 1)

        def turn(u):
            pe.wait_ge(self.probs_ready, i * U + u + 1)
            if u > 0:
                pe.wait_ge(self.turned_ready, i * U + u)
            src = self.mixed[:, :] if self.subs == 2 else self.probs[:, u % 2, :]
            for b in range(self.units[u]["n"] // P):
                mm = pe.transpose(region(self.k, 3)[:, b * P:(b + 1) * P], src[:, b * P:(b + 1) * P], self.k.ident[:, :])
            mm.then_inc(self.turn_done, 1)

        def values(u):
            pe.wait_ge(self.turned_ready, i * U + u + 1)
            v = self.units[u]["values"]
            for b, val in enumerate(v):
                mm = pe.matmul(self.units[u]["out"], val, self.turned[:, u % 2, b * P:(b + 1) * P],
                               start=b == 0, stop=b == len(v) - 1)
            mm.then_inc(self.values_done, 1)

        scores(lo)
        for u in range(lo, hi):
            if u + 1 < hi:
                scores(u + 1)
            turn(u)
            if u > lo:
                values(u - 1)
        values(hi - 1)

    def vector(self, dve, i, lo, hi):
        U, S = len(self.units), self.subs

        def maxima(u):
            n = self.units[u]["n"]
            if S == 1 and u > 1:
                dve.wait_ge(self.exp_done, i * U + u - 1)
            for s in range(S):
                r = self.slot(u, s)
                dve.wait_ge(self.scores_ready, i * (U * S) + u * S + s + 1)
                src = region(self.k, 1 + r, n)
                if self.prepare:
                    self.prepare(dve, self.units[u], src, self.scores[:, r, 0:n])
                    dve.drain()
                    src = self.scores[:, r, 0:n]
                dve.tensor_reduce(self.rowmax[:, r:r + 1], src, AX.X, ALU.max)
                dve.drain()
                if self.sinks is not None:
                    sink = self.sinks[:, self.units[u]["sink"]:self.units[u]["sink"] + 1]
                    dve.tensor_scalar(self.rowmax[:, r:r + 1], self.rowmax[:, r:r + 1], self.scale, sink, ALU.mult, ALU.max)
                    dve.drain()
                    dve.tensor_scalar(self.negmax[:, r:r + 1], self.rowmax[:, r:r + 1], -1.0, None, ALU.mult).then_inc(self.max_ready, 1)
                else:
                    dve.tensor_scalar(self.negmax[:, r:r + 1], self.rowmax[:, r:r + 1], -self.scale, None, ALU.mult).then_inc(self.max_ready, 1)

        def finish(u):
            n = self.units[u]["n"]
            dve.wait_ge(self.exp_done, i * U + u + 1)
            if S == 2:
                dve.reciprocal(self.recip[:, :], self.sums[:, :])
                dve.drain()
                dve.tensor_tensor(self.recip[:, 1:2], self.recip[:, 1:2], self.lam, ALU.mult)
                dve.drain()
                if u > 0:
                    dve.wait_ge(self.turn_done, i * U + u)
                dve.tensor_scalar(self.probs[:, 1, 0:n], self.probs[:, 1, 0:n], self.recip[:, 1:2], None, ALU.mult)
                dve.drain()
                dve.scalar_tensor_tensor(out=self.mixed[:, 0:n], in0=self.probs[:, 0, 0:n], scalar=self.recip[:, 0:1],
                                         in1=self.probs[:, 1, 0:n], op0=ALU.mult, op1=ALU.subtract).then_inc(self.probs_ready, 1)
            else:
                r = u % 2
                total = self.sums[:, r:r + 1]
                if self.sinks is not None:
                    dve.tensor_tensor(total, total, self.sinkexp[:, r:r + 1], ALU.add)
                    dve.drain()
                dve.reciprocal(self.recip[:, r:r + 1], total)
                dve.drain()
                dve.tensor_scalar(self.probs[:, r, 0:n], self.probs[:, r, 0:n], self.recip[:, r:r + 1], None,
                                  ALU.mult).then_inc(self.probs_ready, 1)

        for u in range(lo, hi):
            maxima(u)
            if u > lo:
                finish(u - 1)
        finish(hi - 1)

    def scalar(self, act, i, lo, hi):
        U, S = len(self.units), self.subs

        def exps(u):
            n = self.units[u]["n"]
            if S == 2 and u > 0:
                act.wait_ge(self.probs_ready, i * U + u)
            if S == 1 and u > 1:
                act.wait_ge(self.turn_done, i * U + u - 1)
            for s in range(S):
                r = self.slot(u, s)
                act.wait_ge(self.max_ready, i * (U * S) + u * S + s + 1)
                if self.sinks is not None:
                    sink = self.sinks[:, self.units[u]["sink"]:self.units[u]["sink"] + 1]
                    act.activation(self.sinkexp[:, r:r + 1], sink, ACT.Exp, bias=self.negmax[:, r:r + 1])
                src = self.scores[:, r, 0:n] if self.prepare else region(self.k, 1 + r, n)
                ins = act.activation(self.probs[:, r, 0:n], src, ACT.Exp, bias=self.negmax[:, r:r + 1], scale=self.scale,
                                     accum_out=self.sums[:, r:r + 1])
            ins.then_inc(self.exp_done, 1)

        def copy(u):
            n = self.units[u]["n"]
            act.wait_ge(self.turn_done, i * U + u + 1)
            if u > 1:
                act.wait_ge(self.values_done, i * U + u - 1)
            act.activation(self.turned[:, u % 2, 0:n], region(self.k, 3, n), ACT.Copy).then_inc(self.turned_ready, 1)

        for u in range(lo, hi):
            exps(u)
            if u > lo:
                copy(u - 1)
        copy(hi - 1)


def gating_mlp(k):
    nc, feed = k.nc, k.feed
    T = TOK // P
    with Stage(k, "gating") as st:
        u = st.sb("u", [P, 4, TOK])
        v = st.sb("v", [P, 4, T, P])
        wst = st.sb("wst", [P, 4, P])
        rows = st.sb("rows", [P, NROWS])
        stats = st.sb("stats", [P, 4, T, 6])
        mv = st.sb("mv", [P, 4, T, 2])
        rstd = st.sb("rstd", [P, 4, T])
        landed = st.sem("constants_landed")
        u_ready, v_ready, var_ready, root_ready = st.sem("u_ready"), st.sem("v_ready"), st.sem("var_ready"), st.sem("root_ready")
        normed, mixed, done = st.sem("normed"), st.sem("mixed"), st.sem("gated")

        @st.block.sync
        def _(sp):
            sp.dma_start(wst[:, :, :], k.io["sgu_wt"]).then_inc(landed, 16)
            sp.dma_start(rows[:, :], k.io["rows"].partition_broadcast(P)).then_inc(landed, 16)
            feed.program(sp)

        @st.block.gpsimd
        def _(pool):
            st.clear_last(pool)

        @st.block.tensor
        def _(pe):
            def mix(g):
                b = g % 2
                pe.wait_ge(normed, g + 1)
                for t in range(T):
                    mm = pe.matmul(region(k, 2 * b + 1)[:, t * P:(t + 1) * P], v[:, g, t, :], wst[:, g, :], start=True, stop=True)
                mm.then_inc(mixed, 1)

            pe.wait_ge(landed, 32)
            for g in range(4):
                i, b = divmod(g, 2)
                if g >= 2:
                    pe.wait_ge(u_ready, g - 1)
                    pe.wait_ge(done, g - 1)
                tile_products(k, pe, i, 2 * b, region(k, 2 * b), k.hn, TOK)
                token_products(k, pe, i, 2 * b + 1, region(k, 2 * b + 1), k.hn, TOK)
                mix(g)

        @st.block.scalar
        def _(act):
            for g in range(4):
                i, b = divmod(g, 2)
                feed.wait_done(act, i, 2 * b)
                act.activation(u[:, g, :], region(k, 2 * b), ACT.Gelu).then_inc(u_ready, 1)
                feed.wait_done(act, i, 2 * b + 1)
                act.activation(v[:, g, :, :].rearrange("p t c -> p (t c)"), region(k, 2 * b + 1), ACT.Gelu).then_inc(v_ready, 1)
                act.wait_ge(var_ready, g + 1)
                act.activation(rstd[:, g, :], mv[:, g, :, 1], ACT.Sqrt, bias=k.eps[:, 0:1]).then_inc(root_ready, 1)

        @st.block.vector
        def _(dve):
            for g in range(4):
                b = g % 2
                dve.wait_ge(v_ready, g + 1)
                for t in range(T):
                    dve.bn_stats(stats[:, g, t, :], v[:, g, t, :])
                dve.drain()
                for t in range(T):
                    ins = dve.bn_aggr(mv[:, g, t, :], stats[:, g, t, :])
                ins.then_inc(var_ready, 1)
                dve.wait_ge(root_ready, g + 1)
                dve.reciprocal(rstd[:, g, :], rstd[:, g, :])
                dve.drain()
                for t in range(T):
                    ins = dve.tensor_scalar(v[:, g, t, :], v[:, g, t, :], mv[:, g, t, 0:1], rstd[:, g, t:t + 1], ALU.subtract, ALU.mult)
                ins.then_inc(normed, 1)
                dve.wait_ge(mixed, g + 1)
                bias = rows[:, ROWCOL["sgu_b"] + g * P:ROWCOL["sgu_b"] + (g + 1) * P]
                mo = k.mo[:, g, :]
                dve.tensor_tensor(mo.rearrange("p (t c) -> p t c", t=T), region(k, 2 * b + 1).rearrange("p (t c) -> p t c", t=T),
                                  bias.unsqueeze(1).to_broadcast([P, T, P]), ALU.add)
                dve.drain()
                dve.wait_ge(u_ready, g + 1)
                dve.tensor_tensor(mo, mo, u[:, g, :], ALU.mult).then_inc(done, 1)
    feed.at += 1


def rope(k, dve, x, rotated, cos, sin, tmp):
    dve.tensor_tensor(tmp, rotated, sin, ALU.mult)
    dve.tensor_tensor(x, x, cos, ALU.mult)
    dve.drain()
    return dve.tensor_tensor(x, x, tmp, ALU.add)


def diff_attention(k):
    nc, feed = k.nc, k.feed
    T = TOK // P
    with Stage(k, "diff") as st:
        q, key, v = st.sb("q", [P, TOK]), st.sb("key", [P, TOK]), st.sb("v", [P, T, P])
        tmp = st.sb("tmp", [P, LAT])
        rot, cos, sin = constants(k, st, "rot", "cos", "sin")
        rows = st.sb("rows", [P, NROWS])
        dots, lam, gain = st.sb("dots", [P, 2]), st.sb("lam", [P, 1]), st.sb("gain", [P, 1])
        junk = st.sb("junk", [P, HEAD])
        rstd, sq = st.sb("rstd", [P, TOK]), st.sb("sq", [P, TOK])
        landed, dots_ready, lam_exp = st.sem("constants_landed"), st.sem("dots_ready"), st.sem("lam_exp")
        copied, rotated, roped = st.sem("copied"), st.sem("rotated"), st.sem("roped")
        squared, summed, var_ready, root_ready, head_done = (st.sem("squared"), st.sem("summed"), st.sem("var_ready"),
                                                             st.sem("root_ready"), st.sem("head_done"))
        units = []
        for t in range(T):
            keys = [(0, 512), (512, 256)] if t < LAT // P else [(512, 256)]
            off = keys[0][0]
            units.append(dict(
                n=TOK - off, out=region(k, 0)[:, t * P:(t + 1) * P], values=[v[:, b, :] for b in range(off // P, T)],
                scores=[[(q[64 * s:64 * s + 64, t * P:(t + 1) * P], key[64 * s:64 * s + 64, a:a + n], a - off, n)
                         for a, n in keys] for s in range(2)]))
        att = Attention(k, st, units, 2, SCALE, lam=lam[:, :])
        U = len(units)

        @st.block.sync
        def _(sp):
            for dst, name in ((rot, "rot"), (cos, "cos"), (sin, "sin")):
                sp.dma_start(dst[:, :], k.io[name]).then_inc(landed, 16)
            sp.dma_start(rows[:, :], k.io["rows"].partition_broadcast(P)).then_inc(landed, 16)
            feed.program(sp)

        @st.block.gpsimd
        def _(pool):
            st.clear_last(pool)

        @st.block.tensor
        def _(pe):
            pe.wait_ge(landed, 64)
            with pe.Fori(0, 4) as i:
                pe.wait_ge(head_done, i + 1)
                tile_products(k, pe, i, 0, region(k, 0), k.hn, TOK)
                tile_products(k, pe, i, 1, region(k, 1), k.hn, TOK)
                token_products(k, pe, i, 2, region(k, 2), k.hn, TOK)
                pe.wait_ge(copied, 3 * i + 1)
                pe.matmul(region(k, 3, LAT), rot[:, :], q[:, 0:LAT], start=True, stop=True).then_inc(rotated, 1)
                pe.wait_ge(copied, 3 * i + 2)
                pe.matmul(region(k, 0, LAT), rot[:, :], key[:, 0:LAT], start=True, stop=True).then_inc(rotated, 1)
                pe.wait_ge(copied, 3 * i + 3)
                pe.wait_ge(roped, 2 * i + 2)
                att.tensor(pe, i, 0, U)
                pe.wait_ge(squared, i + 1)
                for a, b, _ in spans(TOK):
                    mm = pe.matmul(region(k, 1)[:, a:b], k.ones[:, :], sq[:, a:b], start=True, stop=True)
                mm.then_inc(summed, 1)

        @st.block.scalar
        def _(act):
            act.wait_ge(dots_ready, 1)
            act.activation(dots[:, :], dots[:, :], ACT.Exp).then_inc(lam_exp, 1)
            with act.Fori(0, 4) as i:
                for j, dst in enumerate((q[:, :], key[:, :], v[:, :, :].rearrange("p t c -> p (t c)"))):
                    feed.wait_done(act, i, j)
                    act.activation(dst, region(k, j), ACT.Copy).then_inc(copied, 1)
                att.scalar(act, i, 0, U)
                act.wait_ge(att.values_done, U * i + U)
                act.activation(sq[:, :], region(k, 0), ACT.Square).then_inc(squared, 1)
                act.wait_ge(var_ready, i + 1)
                act.activation(rstd[:, :], rstd[:, :], ACT.Sqrt).then_inc(root_ready, 1)

        @st.block.vector
        def _(dve):
            dve.sem_inc(head_done, 1)
            dve.wait_ge(landed, 64)
            for j in range(2):
                ins = dve.tensor_tensor_reduce(junk[:, :], rows[:, 128 * j:128 * j + 64], rows[:, 128 * j + 64:128 * j + 128],
                                               1.0, 0.0, ALU.mult, ALU.add, dots[:, j:j + 1])
                dve.drain()
            dve.tensor_scalar(gain[:, :], col(k, "subln"), 1.0 - LAM_INIT, None, ALU.mult).then_inc(dots_ready, 1)
            dve.wait_ge(lam_exp, 1)
            dve.scalar_tensor_tensor(out=lam[:, :], in0=dots[:, 0:1], scalar=LAM_INIT, in1=dots[:, 1:2],
                                     op0=ALU.add, op1=ALU.subtract)
            dve.drain()
            with dve.Fori(0, 4) as i:
                for j, (x, r) in enumerate(((q, 3), (key, 0))):
                    dve.wait_ge(rotated, 2 * i + j + 1)
                    rope(k, dve, x[:, 0:LAT], region(k, r, LAT), cos[:, :], sin[:, :], tmp[:, :]).then_inc(roped, 1)
                    dve.drain()
                att.vector(dve, i, 0, U)
                dve.wait_ge(summed, i + 1)
                dve.tensor_scalar(rstd[:, :], region(k, 1), 1.0 / P, EPS, ALU.mult, ALU.add).then_inc(var_ready, 1)
                dve.wait_ge(root_ready, i + 1)
                dve.reciprocal(rstd[:, :], rstd[:, :])
                dve.drain()
                dve.scalar_tensor_tensor(out=k.mo[:, bass.ds(i + 4, 1), :].rearrange("p a t -> p (a t)"), in0=region(k, 0),
                                         scalar=gain[:, :], in1=rstd[:, :], op0=ALU.mult, op1=ALU.mult).then_inc(head_done, 1)
    feed.at += 1


def window_attention(k):
    nc, feed = k.nc, k.feed
    T = TOK // P
    with Stage(k, "window") as st:
        q, key, v = st.sb("q", [P, LAT]), st.sb("key", [P, TOK]), st.sb("v", [P, T, P])
        tmp = st.sb("tmp", [P, LAT])
        rot, cos, sin, mask = constants(k, st, "rot", "cos", "sin", "window_mask")
        rows, sinks = st.sb("rows", [P, NROWS]), st.sb("sinks", [P, 8])
        landed = st.sem("constants_landed")
        kv_copied, q_copied, rotated, roped, chunk_done = (st.sem("kv_copied"), st.sem("q_copied"), st.sem("rotated"),
                                                           st.sem("roped"), st.sem("chunk_done"))
        units = []
        for j in range(4):
            for s in range(2):
                for t in range(4):
                    qt = q[64 * s:64 * s + 64, t * P:(t + 1) * P]
                    kt = key[64 * s:64 * s + 64, :]
                    left = P if t > 0 else 0
                    products = [(qt, kt[:, t * P - left:(t + 1) * P], 0, left + P), (qt, kt[:, LAT:TOK], left + P, CTX)]
                    tiles = ([t - 1] if left else []) + [t, 4, 5]
                    n = left + P + CTX
                    if t < 3:
                        products.append((qt, kt[:, (t + 1) * P:(t + 2) * P], n, P))
                        tiles.append(t + 1)
                        n += P
                    units.append(dict(n=n, scores=[products], values=[v[:, b, 64 * s:64 * s + 64] for b in tiles],
                                      out=region(k, 0)[64 * s:64 * s + 64, t * P:(t + 1) * P], sink=4 * s + j,
                                      mask=0 if left else P))

        def prepare(dve, unit, src, dst):
            dve.tensor_tensor(dst, src, mask[:, unit["mask"]:unit["mask"] + unit["n"]], ALU.add)

        att = Attention(k, st, units, 1, SCALE, prepare=prepare, sinks=sinks)
        U = len(units)

        @st.block.sync
        def _(sp):
            for dst, name in ((rot, "rot"), (cos, "cos"), (sin, "sin"), (mask, "window_mask")):
                sp.dma_start(dst[:, :], k.io[name]).then_inc(landed, 16)
            sp.dma_start(rows[:, :], k.io["rows"].partition_broadcast(P)).then_inc(landed, 16)
            feed.program(sp)

        @st.block.gpsimd
        def _(pool):
            st.clear_last(pool)

        @st.block.tensor
        def _(pe):
            pe.wait_ge(landed, 80)
            with pe.Fori(0, 2) as i:
                pe.wait_ge(chunk_done, 4 * i + 1)
                tile_products(k, pe, i, 0, region(k, 1), k.hn, TOK)
                token_products(k, pe, i, 1, region(k, 2), k.hn, TOK)
                pe.wait_ge(kv_copied, 2 * i + 1)
                pe.matmul(region(k, 3, LAT), rot[:, :], key[:, 0:LAT], start=True, stop=True).then_inc(rotated, 1)
                for j in range(4):
                    pe.wait_ge(chunk_done, 4 * i + j + 1)
                    tile_products(k, pe, i, 2 + j, region(k, 0), k.hn, LAT)
                    pe.wait_ge(q_copied, 4 * i + j + 1)
                    pe.wait_ge(roped, 5 * i + j + 1)
                    pe.matmul(region(k, 3, LAT), rot[:, :], q[:, 0:LAT], start=True, stop=True).then_inc(rotated, 1)
                    pe.wait_ge(roped, 5 * i + j + 2)
                    pe.wait_ge(kv_copied, 2 * i + 2)
                    att.tensor(pe, i, 8 * j, 8 * j + 8)

        @st.block.scalar
        def _(act):
            with act.Fori(0, 2) as i:
                feed.wait_done(act, i, 0)
                act.activation(key[:, :], region(k, 1), ACT.Copy).then_inc(kv_copied, 1)
                feed.wait_done(act, i, 1)
                act.activation(v[:, :, :].rearrange("p t c -> p (t c)"), region(k, 2), ACT.Copy).then_inc(kv_copied, 1)
                for j in range(4):
                    feed.wait_done(act, i, 2 + j)
                    act.activation(q[:, :], region(k, 0, LAT), ACT.Copy).then_inc(q_copied, 1)
                    att.scalar(act, i, 8 * j, 8 * j + 8)

        @st.block.vector
        def _(dve):
            dve.sem_inc(chunk_done, 1)
            dve.wait_ge(landed, 80)
            with dve.Fori(0, 2) as i:
                dve.wait_ge(rotated, 5 * i + 1)
                rope(k, dve, key[:, 0:LAT], region(k, 3, LAT), cos[:, :], sin[:, :], tmp[:, :]).then_inc(roped, 1)
                dve.tensor_copy(sinks[:, :], rows[:, bass.ds(8 * i + ROWCOL["sink"], 8)])
                dve.drain()
                for j in range(4):
                    dve.wait_ge(rotated, 5 * i + j + 2)
                    rope(k, dve, q[:, 0:LAT], region(k, 3, LAT), cos[:, :], sin[:, :], tmp[:, :]).then_inc(roped, 1)
                    dve.drain()
                    att.vector(dve, i, 8 * j, 8 * j + 8)
                    dve.wait_ge(att.values_done, i * U + 8 * j + 8)
                    dve.tensor_copy(k.mo[:, bass.ds(4 * i + j, 1), 0:LAT].rearrange("p a t -> p (a t)"),
                                    region(k, 0, LAT)).then_inc(chunk_done, 1)
    feed.at += 1


def neighbourhood_attention(k):
    nc, feed = k.nc, k.feed
    T = TOK // P
    NB = (DR - 1) * GRID_W
    with Stage(k, "neighbour") as st:
        q, key, v = st.sb("q", [P, LAT]), st.sb("key", [P, TOK]), st.sb("v", [P, T, P])
        mask, = constants(k, st, "column_mask")
        bias = st.sb("bias", [P, 2, NB])
        landed, bias_landed, bias_ready, bias_free = (st.sem("mask_landed"), k.bias_landed,
                                                      st.sem("bias_ready"), st.sem("bias_free"))
        copied, pair_done = st.sem("copied"), st.sem("pair_done")
        units = []
        for s in range(2):
            for t in range(4):
                qt = q[64 * s:64 * s + 64, t * P:(t + 1) * P]
                kt = key[64 * s:64 * s + 64, :]
                units.append(dict(n=TOK, scores=[[(qt, kt[:, 0:LAT], 0, LAT), (qt, kt[:, LAT:TOK], LAT, CTX)]],
                                  values=[v[:, b, 64 * s:64 * s + 64] for b in range(T)],
                                  out=region(k, 0)[64 * s:64 * s + 64, t * P:(t + 1) * P],
                                  bias=bias[:, s, (6 - 2 * t) * GRID_W:(6 - 2 * t) * GRID_W + LAT]))

        def prepare(dve, unit, src, dst):
            dve.scalar_tensor_tensor(out=dst[:, 0:LAT], in0=src[:, 0:LAT], scalar=SCALE, in1=unit["bias"],
                                     op0=ALU.mult, op1=ALU.add)
            dve.tensor_scalar(dst[:, LAT:TOK], src[:, LAT:TOK], SCALE, None, ALU.mult)

        att = Attention(k, st, units, 1, 1.0, prepare=prepare)
        U = len(units)

        @st.block.sync
        def _(sp):
            sp.dma_start(mask[:, :], k.io["column_mask"]).then_inc(landed, 16)
            feed.program(sp)

        @st.block.gpsimd
        def _(pool):
            st.clear_last(pool)
            pool.wait_ge(k.bias_sem, 16 * (2 + GRID_W))
            with pool.Fori(0, 8) as i:
                pool.wait_ge(bias_free, i + 1)
                for s in range(2):
                    for half in range(2):
                        src = k.toeplitz[bass.ds(2 * i + s, 1), :, 1 - half:DR - half, :]
                        pool.dma_start(bias[64 * half:64 * half + 64, s, :],
                                       src.rearrange("a q r c -> (a q) (r c)")).then_inc(bias_landed[2 * s + half], 16)

        @st.block.tensor
        def _(pe):
            with pe.Fori(0, 8) as i:
                pe.wait_ge(pair_done, i + 1)
                tile_products(k, pe, i, 0, region(k, 0), k.hn, LAT)
                tile_products(k, pe, i, 1, region(k, 1), k.hn, TOK)
                token_products(k, pe, i, 2, region(k, 2), k.hn, TOK)
                pe.wait_ge(copied, 3 * i + 3)
                att.tensor(pe, i, 0, U)

        @st.block.scalar
        def _(act):
            with act.Fori(0, 8) as i:
                for j, (dst, n) in enumerate(((q[:, :], LAT), (key[:, :], TOK), (v[:, :, :].rearrange("p t c -> p (t c)"), TOK))):
                    feed.wait_done(act, i, j)
                    act.activation(dst, region(k, j, n), ACT.Copy).then_inc(copied, 1)
                att.scalar(act, i, 0, U)

        @st.block.vector
        def _(dve):
            dve.sem_inc(pair_done, 1)
            dve.sem_inc(bias_free, 1)
            dve.wait_ge(landed, 16)
            with dve.Fori(0, 8) as i:
                for s in range(4):
                    dve.wait_ge(bias_landed[s], 16 * i + 16)
                for s in range(2):
                    b3 = bias[:, s, :].rearrange("p (r c) -> p r c", c=GRID_W)
                    dve.tensor_tensor(b3, b3, mask[:, :].unsqueeze(1).to_broadcast([P, DR - 1, GRID_W]), ALU.add)
                dve.drain()
                att.vector(dve, i, 0, U)
                dve.sem_inc(bias_free, 1)
                dve.wait_ge(att.values_done, i * U + U)
                dve.tensor_copy(k.mo[:, bass.ds(i, 1), 0:LAT].rearrange("p a t -> p (a t)"),
                                region(k, 0, LAT)).then_inc(pair_done, 1)
    feed.at += 1


def shift_mix(dve, dst, raw, own, before, after):
    for op in range(3):
        for a, n, off in ((0, LAT, 1), (LAT, CTX, LAT + 2)):
            d = dst[:, a:a + n]
            if op == 0:
                ins = dve.tensor_scalar(d, raw[:, off:off + n], own, None, ALU.mult)
            else:
                o = off - 1 if op == 1 else off + 1
                ins = dve.scalar_tensor_tensor(out=d, in0=raw[:, o:o + n], scalar=before if op == 1 else after, in1=d,
                                               op0=ALU.mult, op1=ALU.add)
        if op < 2:
            dve.drain()
    return ins


RAWW = TOK + 3
POOLW = 8 + LAT + 8 + CTX + 8


def rwkv(k):
    keep = k.tmp
    new = lambda name, n: keep.enter_context(k.nc.sbuf_tensor(f"rwkv_{name}", [P, n], F32))
    wd, ad, gd = new("wd", TOK), new("ad", TOK), new("gd", TOK)
    with ExitStack() as k.tmp:
        lora_and_pooling(k, wd, ad, gd)
    with ExitStack() as k.tmp:
        rwkv_pairs(k, wd, ad, gd)


def lora_and_pooling(k, wd, ad, gd):
    feed = k.feed
    with Stage(k, "lora") as st:
        raw = st.sb("raw", [P, 3, RAWW])
        own = st.sb("own", [P, 3])
        pads = [st.sb(f"pooled{j}", [P, 2, POOLW]) for j in range(5)]
        pooled = st.sb("pooled", [P, 2, TOK])
        invc, poolw = constants(k, st, "pool_inv", "pool_w")
        zeroed, copied, mixed, landed, pooled_ready, products = (st.sem("zeroed"), st.sem("copied"), st.sem("mixed"),
                                                                 st.sem("landed"), st.sem("pooled_ready"), st.sem("pool_products"))
        seqs = ((0, LAT, 8), (LAT, CTX, 16 + LAT))

        @st.block.sync
        def _(sp):
            sp.dma_start(invc[:, :, :], k.io["pool_inv"]).then_inc(landed, 16)
            sp.dma_start(poolw[:, :, :], k.io["pool_w"]).then_inc(landed, 16)
            feed.program(sp)

        @st.block.gpsimd
        def _(pool):
            st.clear_last(pool)
            pool.memset(raw[:, :, :], 0.0)
            pool.memset(pads[0][:, :, :], 0.0).then_inc(zeroed, 1)

        @st.block.tensor
        def _(pe):
            for j in range(4):
                tile_products(k, pe, 0, j, region(k, j), k.hn, TOK)
            pe.wait_ge(copied, 1)
            tile_products(k, pe, 0, 4, region(k, 0), k.hn, TOK)
            pe.wait_ge(landed, 32)
            pe.wait_ge(pooled_ready, 1)
            pe.wait_ge(copied, 4)
            for j in range(2):
                for h in range(2):
                    for a, b, _ in spans(TOK):
                        mm = pe.matmul(region(k, 2 + j)[64 * h:64 * h + 64, a:b], poolw[64 * h:64 * h + 64, j, :],
                                       pooled[64 * h:64 * h + 64, j, a:b], start=True, stop=True)
            mm.then_inc(products, 1)

        @st.block.scalar
        def _(act):
            act.wait_ge(zeroed, 1)
            for j in range(5):
                feed.wait_done(act, 0, j)
                for a, n, off in (((0, LAT, 1), (LAT, CTX, LAT + 2)) if j < 3 else seqs):
                    dst = raw[:, j, off:off + n] if j < 3 else pads[0][:, j - 3, off:off + n]
                    ins = act.activation(dst, region(k, j % 4)[:, a:a + n], ACT.Copy)
                ins.then_inc(copied, 1)
            act.wait_ge(mixed, 3)
            act.activation(wd[:, :], wd[:, :], ACT.Tanh)
            act.activation(gd[:, :], gd[:, :], ACT.Sigmoid)
            act.wait_ge(products, 1)
            for j in range(2):
                act.activation(k.mo[:, 6 + j, :], region(k, 2 + j), ACT.Identity, scale=col(k, "pool_scale", j))

        @st.block.vector
        def _(dve):
            mu = lambda d, j: col(k, "mu_lora", 3 * d + j)
            dve.tensor_tensor(own[:, :], col(k, "mu_lora", 0, 3), col(k, "mu_lora", 3, 3), ALU.add)
            dve.drain()
            dve.tensor_scalar(own[:, :], own[:, :], -1.0, 1.0, ALU.mult, ALU.add)
            dve.drain()
            for j, dst in enumerate((wd, ad, gd)):
                dve.wait_ge(copied, j + 1)
                shift_mix(dve, dst, raw[:, j, :], own[:, j:j + 1], mu(0, j), mu(1, j)).then_inc(mixed, 1)
            dve.wait_ge(copied, 5)
            for n, (left, right) in enumerate(((1, 0), (1, 1), (2, 2), (4, 4))):
                a, b = pads[n], pads[n + 1]
                if n == 0:
                    dve.memset(b[:, :, 0:1], 0.0)
                edge = (1, 2, 4, 8)[n]
                m = POOLW - 2 * edge
                dve.tensor_tensor(b[:, :, edge:edge + m], a[:, :, edge - left:edge - left + m],
                                  a[:, :, edge + right:edge + right + m], ALU.add)
                dve.drain()
            dve.wait_ge(landed, 32)
            for a, n, off in seqs:
                for j in range(2):
                    for h in range(2):
                        dve.tensor_tensor(pooled[64 * h:64 * h + 64, j, a:a + n], pads[1 + 2 * j + h][64 * h:64 * h + 64, j, off:off + n],
                                          invc[64 * h:64 * h + 64, j, a:a + n], ALU.mult)
            dve.drain()
            for a, n, off in seqs:
                ins = dve.tensor_tensor(pooled[:, :, a:a + n], pooled[:, :, a:a + n], pads[0][:, :, off:off + n], ALU.subtract)
            ins.then_inc(pooled_ready, 1)
    feed.at += 1


def rwkv_pairs(k, wd, ad, gd):
    feed = k.feed
    GR = NCH // 2
    with Stage(k, "rwkv") as st:
        pw = st.sb("pair_weights", [P, NPAIR + 3 * P])
        bones, ident2, reset, lmask, levels = constants(k, st, "bones", "ident2", "reset", "tri_mask", "level_mask")
        own = st.sb("own", [P, 4])
        raw = st.sb("raw", [P, 3, RAWW])
        y, t1, t2 = (raw[:, j, 0:TOK] for j in range(3))
        r, kf, v, kk = (st.sb(n, [P, TOK]) for n in ("r", "kf", "v", "kk"))
        c, cm, em = (st.sb(n, [P, TOK]) for n in ("c", "cm", "em"))
        a, kd, kds = (st.sb(n, [P, TOK]) for n in ("a", "kd", "kds"))
        mid = st.sb("mid", [P, 2, NCH])
        factor = st.sb("factor", [P, NCH])
        qq = st.sb("qq", [P, NCH, 2, RC])
        bb, kb = st.sb("bb", [P, NCH, RC]), st.sb("kb", [P, NCH, RC])
        vt, bt, kt = (st.sb(n, [P, NCH, RC]) for n in ("vt", "bt", "kt"))
        lt = st.sb("lt", [P, NCH, 4, RC])
        x, xt, g = (st.sb(n, [P, NCH, RC]) for n in ("x", "xt", "g"))
        ct = st.sb("ct", [P, 2, NCH, RC])
        sm, sf = st.sb("sm", [P, 2, HEAD]), st.sb("sf", [P, HEAD])
        zs, sa = st.sb("zs", [P, HEAD]), st.sb("sa", [P, HEAD])
        par = {n: pw[:, i:i + 1] for n, i in PAIRCOL.items()}
        w2, a2, g2 = (pw[:, NPAIR + P * j:NPAIR + P * (j + 1)] for j in range(3))
        S = {n: st.sem(n) for n in (
            "constants", "padded", "pair_done", "copied", "kk_ready", "sq_ready", "norm_summed", "norm_root",
            "mix_done", "vtok_done", "vtok_copied", "lora_done", "sig_done", "cum_ready", "exp_ready", "qk_ready",
            "tok_done", "tok_copied", "l_done", "lt_ready", "ct_ready", "g_done", "g_copied", "u_done", "x_ready",
            "state_ready", "z_done", "z_copied", "sa_done", "sa_copied", "ds_done", "y_done", "y_read")}
        S.update({n: st.sem(n) for n in ("mean_done", "centred", "ysq_ready", "var_done", "var_ready", "var_root")})
        S["pair_landed"] = k.pair_landed
        halves = (0, 64)
        order = [list(range(8, 12)) + list(range(8)), list(range(11, 7, -1)) + list(range(7, -1, -1))]
        def flat(t):
            return t[:, :, :].rearrange("p n c -> p (n c)")

        def chunked(t):
            return t.rearrange("p (n c) -> p n c", c=RC)

        def hold(eng, sem, value):
            eng.wait_ge(sem, value)
            eng.nop(nofuse=True)

        @st.block.sync
        def _(sp):
            for dst, name in ((bones, "bones"), (ident2, "ident2"), (reset, "reset"), (lmask, "tri_mask"), (levels, "level_mask")):
                sp.dma_start(dst[:], k.io[name]).then_inc(S["constants"], 16)
            feed.program(sp)

        @st.block.gpsimd
        def _(pool):
            st.clear_last(pool)
            pool.wait_ge(S["constants"], 80)
            with pool.Fori(0, PAIRS) as i:
                hold(pool, S["pair_done"], i + 1)
                pool.memset(raw[:, :, 0:1], 0.0)
                pool.memset(raw[:, :, LAT + 1:LAT + 2], 0.0)
                pool.memset(raw[:, :, TOK + 2:TOK + 3], 0.0).then_inc(S["padded"], 1)
                pool.dma_start(pw[:, :], k.io["pair"][bass.ds(i, 1)].rearrange("a p w -> (a p) w")).then_inc(S["pair_landed"], 16)
                for d in range(2):
                    dd = 2 * i + d
                    for l in range(LEVELS):
                        for gr in range(2):
                            ns = slice(GR * gr, GR * gr + GR)
                            if l == 0:
                                pool.wait_ge(S["lt_ready"], 6 * dd + 3 * gr + 3)
                            if l >= 2:
                                pool.wait_ge(S["g_done"], 12 * dd + 2 * (l - 2) + gr + 1)
                            ins = pool.tensor_tensor(ct[:, l % 2, ns, :], lt[:, ns, 0, :],
                                                     levels[:, d, l, :].unsqueeze(1).to_broadcast([P, GR, RC]), ALU.mult)
                            if l == 0:
                                pool.drain()
                                ins = pool.tensor_tensor(xt[:, ns, :], ident2[:, :].unsqueeze(1).to_broadcast([P, GR, RC]),
                                                         ct[:, 0, ns, :], ALU.subtract)
                            ins.then_inc(S["ct_ready"], 1)

        @st.block.tensor
        def _(pe):
            def turned(dst, src):
                for n in range(NCH):
                    for h in halves:
                        mm = pe.matmul(dst[h:h + 64, n * RC:(n + 1) * RC], src[h:h + 64, n * RC:(n + 1) * RC], ident2[h:h + 64, :],
                                       start=True, stop=True)
                return mm

            def summed(dst, src):
                for a_, b_, _ in spans(TOK):
                    mm = pe.matmul(dst[:, a_:b_], bones[:, :], src[:, a_:b_], start=True, stop=True)
                return mm

            def invert(dd):
                hold(pe, S["tok_copied"], 2 * dd + 2)
                for l in range(LEVELS):
                    for gr in range(2):
                        hold(pe, S["ct_ready"], 12 * dd + 2 * l + gr + 1)
                        if l > 0:
                            hold(pe, S["x_ready"], 12 * dd + 2 * (l - 1) + gr + 1)
                        for n in range(GR * gr, GR * gr + GR):
                            for h in halves:
                                rhs = x[h:h + 64, n, :] if l else ident2[h:h + 64, :]
                                mm = pe.matmul(k.ps[h:h + 64, gr, (n - GR * gr) * RC:(n - GR * gr + 1) * RC],
                                               ct[h:h + 64, l % 2, n, :], rhs, start=True, stop=True)
                        mm.then_inc(S["g_done"], 1)
                    if l == 0:
                        continue
                    for gr in range(2):
                        hold(pe, S["g_copied"], 10 * dd + 2 * (l - 1) + gr + 1)
                        for n in range(GR * gr, GR * gr + GR):
                            cols = slice((n - GR * gr) * RC, (n - GR * gr + 1) * RC)
                            for h in halves:
                                if l < LEVELS - 1:
                                    pe.matmul(k.ps[h:h + 64, 2 + gr, cols], xt[h:h + 64, n, :], g[h:h + 64, n, :], start=True, stop=True)
                                mm = pe.matmul(k.ps[h:h + 64, 4 + gr, cols], g[h:h + 64, n, :], xt[h:h + 64, n, :], start=True, stop=True)
                        mm.then_inc(S["u_done"], 1)

            def recur(dd, d):
                hold(pe, S["x_ready"], 12 * dd + 12)
                Z, A, DS, Y = k.ps[:, 0, 0:64], k.ps[:, 1, 0:64], k.ps[:, 2, 0:64], region(k, 3)
                for s, n in enumerate(order[d]):
                    last = s == NCH - 1
                    state = sm[:, s % 2, :]
                    yc = Y[:, n * RC:(n + 1) * RC]
                    hold(pe, S["state_ready"], 12 * dd + s + 1)
                    for h in halves:
                        hs = slice(h, h + 64)
                        pe.matmul(Z[hs, :], qq[hs, n, 0, :], state[hs, :], start=True, stop=False)
                        mm = pe.matmul(Z[hs, :], lt[hs, n, 2, :], vt[hs, n, :], start=False, stop=True)
                    mm.then_inc(S["z_done"], 1)
                    for h in halves:
                        hs = slice(h, h + 64)
                        pe.matmul(yc[hs, :], state[hs, :], qq[hs, n, 1, :], start=True, stop=False)
                        pe.matmul(yc[hs, :], vt[hs, n, :], lt[hs, n, 3, :], start=False, stop=False)
                    hold(pe, S["z_copied"], 12 * dd + s + 1)
                    for h in halves:
                        hs = slice(h, h + 64)
                        mm = pe.matmul(A[hs, :], xt[hs, n, :], zs[hs, :], start=True, stop=True)
                    mm.then_inc(S["sa_done"], 1)
                    if not last:
                        for h in halves:
                            hs = slice(h, h + 64)
                            pe.matmul(DS[hs, :], kt[hs, n, :], vt[hs, n, :], start=True, stop=False)
                    hold(pe, S["sa_copied"], 12 * dd + s + 1)
                    if not last:
                        for h in halves:
                            hs = slice(h, h + 64)
                            mm = pe.matmul(DS[hs, :], bt[hs, n, :], sa[hs, :], start=False, stop=True)
                        mm.then_inc(S["ds_done"], 1)
                    for h in halves:
                        hs = slice(h, h + 64)
                        mm = pe.matmul(yc[hs, :], sa[hs, :], lt[hs, n, 1, :], start=False, stop=True)
                mm.then_inc(S["y_done"], 1)

            pe.wait_ge(S["constants"], 80)
            with pe.Fori(0, PAIRS) as i:
                hold(pe, S["pair_done"], i + 1)
                for j in range(3):
                    tile_products(k, pe, i, j, region(k, j), k.hn, TOK)
                hold(pe, S["sq_ready"], i + 1)
                summed(region(k, 1), t1).then_inc(S["norm_summed"], 1)
                hold(pe, S["mix_done"], i + 1)
                turned(region(k, 2), v).then_inc(S["vtok_done"], 1)
                for d in range(2):
                    dd = 2 * i + d
                    hold(pe, S["pair_landed"], 16 * i + 16)
                    hold(pe, S["y_read"], dd + 1)
                    ds_ = slice(64 * d, 64 * d + 64)
                    for reg, wt, src in ((3, w2, wd), (0, a2, ad)):
                        for a_, b_, _ in spans(TOK):
                            mm = pe.matmul(region(k, reg)[:, a_:b_], wt[ds_, :], src[ds_, a_:b_], start=True, stop=True)
                    mm.then_inc(S["lora_done"], 1)
                    hold(pe, S["qk_ready"], dd + 1)
                    turned(region(k, 0), flat(bb)).then_inc(S["tok_done"], 1)
                    hold(pe, S["vtok_copied"], i + 1)
                    for n in range(NCH):
                        for h in halves:
                            for j, w in enumerate((bb, kb)):
                                mm = pe.matmul(k.ps[h:h + 64, 2 + n // 2, (n % 2) * 256 + 128 * j:(n % 2) * 256 + 128 * j + 128],
                                               w[h:h + 64, n, :], qq[h:h + 64, n, :, :], start=True, stop=True)
                        if n % 2:
                            mm.then_inc(S["l_done"], 1)
                    hold(pe, S["tok_copied"], 2 * dd + 1)
                    turned(region(k, 0), flat(kb)).then_inc(S["tok_done"], 1)
                    hold(pe, S["lt_ready"], 6 * dd + 6)
                    invert(dd)
                    recur(dd, d)
                hold(pe, S["y_read"], 2 * i + 3)
                summed(region(k, 0), y).then_inc(S["mean_done"], 1)
                for a_, b_, _ in spans(TOK):
                    pe.matmul(region(k, 3)[:, a_:b_], g2, gd[:, a_:b_], start=True, stop=True)
                hold(pe, S["ysq_ready"], i + 1)
                summed(region(k, 1), t1)
                summed(region(k, 2), kds).then_inc(S["var_done"], 1)

        @st.block.scalar
        def _(act):
            with act.Fori(0, PAIRS) as i:
                act.wait_ge(S["padded"], i + 1)
                for j in range(3):
                    feed.wait_done(act, i, j)
                    act.activation(raw[:, j, 1:LAT + 1], region(k, j)[:, 0:LAT], ACT.Copy)
                    act.activation(raw[:, j, LAT + 2:TOK + 2], region(k, j)[:, LAT:TOK], ACT.Copy).then_inc(S["copied"], 1)
                act.wait_ge(S["kk_ready"], i + 1)
                act.activation(t1, kk[:, :], ACT.Square).then_inc(S["sq_ready"], 1)
                act.wait_ge(S["norm_summed"], i + 1)
                act.activation(t2, region(k, 1), ACT.Sqrt).then_inc(S["norm_root"], 1)
                act.wait_ge(S["vtok_done"], i + 1)
                act.activation(flat(vt), region(k, 2), ACT.Copy).then_inc(S["vtok_copied"], 1)
                for d in range(2):
                    dd = 2 * i + d
                    act.wait_ge(S["lora_done"], dd + 1)
                    act.activation(c[:, :], region(k, 3), ACT.Sigmoid, bias=par[f"w0_{d}"])
                    act.activation(a[:, :], region(k, 0), ACT.Sigmoid, bias=par[f"a0_{d}"]).then_inc(S["sig_done"], 1)
                    act.wait_ge(S["cum_ready"], dd + 1)
                    act.activation(mid[:, :, :], mid[:, :, :], ACT.Exp)
                    act.activation(em[:, :], em[:, :], ACT.Exp, scale=1.0 if d == 0 else -1.0)
                    act.activation(c[:, :], cm[:, :], ACT.Exp, scale=-1.0)
                    act.drain()
                    act.activation(cm[:, :], cm[:, :] if d == 0 else kd[:, :], ACT.Exp)
                    act.drain()
                    act.activation(zs[:, 0:1], mid[:, 0, 0:1], ACT.Copy).then_inc(S["exp_ready"], 1)
                    for j, dst in enumerate((bt, kt)):
                        act.wait_ge(S["tok_done"], 2 * dd + j + 1)
                        act.activation(flat(dst), region(k, 0), ACT.Copy).then_inc(S["tok_copied"], 1)
                    for l in range(1, LEVELS):
                        for gr in range(2):
                            if l >= 2:
                                act.wait_ge(S["u_done"], 10 * dd + 2 * (l - 2) + gr + 1)
                            act.wait_ge(S["g_done"], 12 * dd + 2 * l + gr + 1)
                            act.activation(g[:, GR * gr:GR * gr + GR, :].rearrange("p n c -> p (n c)"), k.ps[:, gr, 0:GR * RC],
                                           ACT.Copy).then_inc(S["g_copied"], 1)
                    for s in range(NCH):
                        act.wait_ge(S["z_done"], 12 * dd + s + 1)
                        act.activation(zs[:, :], k.ps[:, 0, 0:64], ACT.Copy).then_inc(S["z_copied"], 1)
                        act.wait_ge(S["sa_done"], 12 * dd + s + 1)
                        act.activation(sa[:, :], k.ps[:, 1, 0:64], ACT.Copy, scale=-1.0).then_inc(S["sa_copied"], 1)
                act.wait_ge(S["centred"], i + 1)
                act.activation(t1, y, ACT.Square).then_inc(S["ysq_ready"], 1)
                act.wait_ge(S["var_ready"], i + 1)
                act.activation(t2, t2, ACT.Sqrt).then_inc(S["var_root"], 1)

        @st.block.vector
        def _(dve):
            dve.sem_inc(S["pair_done"], 1)
            dve.sem_inc(S["y_read"], 1)
            dve.wait_ge(S["constants"], 80)
            with dve.Fori(0, PAIRS) as i:
                dve.wait_ge(S["pair_landed"], 16 * i + 16)
                dve.tensor_tensor(own[:, 0:3], pw[:, 0:3], pw[:, 3:6], ALU.add)
                dve.drain()
                dve.tensor_scalar(own[:, 0:3], own[:, 0:3], -1.0, 1.0, ALU.mult, ALU.add)
                dve.tensor_scalar(own[:, 3:4], par["k_a"], -1.0, 1.0, ALU.mult, ALU.add)
                dve.drain()
                for j, dst in enumerate((r, kf, v)):
                    dve.wait_ge(S["copied"], 3 * i + j + 1)
                    ins = shift_mix(dve, dst, raw[:, j, :], own[:, j:j + 1], pw[:, j:j + 1], pw[:, 3 + j:4 + j])
                ins.then_inc(S["mix_done"], 1)
                dve.tensor_scalar(kk[:, :], kf[:, :], par["k_k"], None, ALU.mult).then_inc(S["kk_ready"], 1)
                dve.wait_ge(S["norm_root"], i + 1)
                dve.tensor_scalar(t2, t2, 1e-12, None, ALU.max)
                dve.drain()
                dve.reciprocal(t2, t2)
                dve.drain()
                dve.tensor_tensor(kk[:, :], kk[:, :], t2, ALU.mult)
                for d in range(2):
                    dd = 2 * i + d
                    dve.wait_ge(S["sig_done"], dd + 1)
                    dve.tensor_scalar(c[:, :], c[:, :], -math.exp(-0.5), None, ALU.mult)
                    dve.drain()
                    dve.tensor_tensor_scan(cm[:, :], reset[:, :], c[:, :], 0.0, ALU.mult, ALU.add)
                    dve.drain()
                    dve.tensor_copy(mid[:, 0, :], chunked(cm[:, :])[:, :, RC // 2 - 1])
                    dve.tensor_tensor(em[:, :], cm[:, :], c[:, :], ALU.subtract)
                    dve.drain()
                    m = mid[:, 0, :].unsqueeze(2).to_broadcast([P, NCH, RC])
                    dve.tensor_tensor(mid[:, 1, :], chunked(cm[:, :])[:, :, RC - 1], mid[:, 0, :], ALU.subtract)
                    dve.tensor_tensor(chunked(em[:, :]), chunked(em[:, :]), m, ALU.subtract)
                    dve.drain()
                    dve.tensor_tensor(chunked(cm[:, :]), chunked(cm[:, :]), m, ALU.subtract)
                    if d == 1:
                        dve.tensor_copy(kd[:, :], em[:, :])
                    dve.drain()
                    dve.tensor_copy(own[:, 0:1], own[:, 0:1]).then_inc(S["cum_ready"], 1)
                    dve.tensor_scalar(t2, a[:, :], par["k_a"], own[:, 3:4], ALU.mult, ALU.add)
                    dve.drain()
                    dve.tensor_tensor(t2, t2, kf[:, :], ALU.mult)
                    dve.tensor_tensor(a[:, :], a[:, :], kk[:, :], ALU.mult)
                    dve.drain()
                    if d == 0:
                        dve.tensor_copy(kds[:, :], t2)
                    else:
                        dve.tensor_tensor(kds[:, :], kds[:, :], t2, ALU.add)
                    dve.wait_ge(S["exp_ready"], dd + 1)
                    ekk, er, eb = (em, cm, c) if d == 0 else (c, em, cm)
                    dve.tensor_tensor(qq[:, :, 0, :], chunked(kk[:, :]), chunked(ekk[:, :]), ALU.mult)
                    dve.tensor_tensor(qq[:, :, 1, :], chunked(r[:, :]), chunked(er[:, :]), ALU.mult)
                    dve.tensor_tensor(flat(bb), a[:, :], eb[:, :], ALU.mult)
                    dve.tensor_tensor(flat(kb), t2, eb[:, :], ALU.mult).then_inc(S["qk_ready"], 1)
                    start, end = (0, 1) if d == 0 else (1, 0)
                    for lo, hi in ((8, 12), (0, 8)):
                        if d == 0:
                            dve.tensor_tensor(factor[:, lo:hi - 1], mid[:, end, lo:hi - 1], mid[:, start, lo + 1:hi], ALU.mult)
                        else:
                            dve.tensor_tensor(factor[:, lo + 1:hi], mid[:, end, lo + 1:hi], mid[:, start, lo:hi - 1], ALU.mult)
                    seam_from, seam_to = (11, 0) if d == 0 else (8, 7)
                    dve.tensor_tensor(factor[:, seam_from:seam_from + 1], mid[:, end, seam_from:seam_from + 1],
                                      mid[:, start, seam_to:seam_to + 1], ALU.mult)
                    for b in range(6):
                        dve.wait_ge(S["l_done"], 6 * dd + b + 1)
                        dve.tensor_tensor(lt[:, 2 * b:2 * b + 2, :, :].rearrange("p n j c -> p n (j c)"),
                                          k.ps[:, 2 + b, :].rearrange("p (n w) -> p n w", n=2),
                                          lmask[:, d, :].unsqueeze(1).to_broadcast([P, 2, 256]), ALU.mult).then_inc(S["lt_ready"], 1)
                    for gr in range(2):
                        dve.wait_ge(S["g_done"], 12 * dd + gr + 1)
                        dve.scalar_tensor_tensor(out=x[:, GR * gr:GR * gr + GR, :], in0=k.ps[:, gr, 0:GR * RC].rearrange("p (n c) -> p n c", c=RC),
                                                 scalar=-1.0, in1=ident2[:, :].unsqueeze(1).to_broadcast([P, GR, RC]),
                                                 op0=ALU.mult, op1=ALU.add).then_inc(S["x_ready"], 1)
                    for l in range(1, LEVELS):
                        for gr in range(2):
                            dve.wait_ge(S["u_done"], 10 * dd + 2 * (l - 1) + gr + 1)
                            gs = slice(GR * gr, GR * gr + GR)
                            if l < LEVELS - 1:
                                xs = x[:, gs, :].rearrange("p n c -> p (n c)")
                                dve.tensor_tensor(xs, xs, k.ps[:, 2 + gr, 0:GR * RC], ALU.subtract)
                            xs = xt[:, gs, :].rearrange("p n c -> p (n c)")
                            dve.tensor_tensor(xs, xs, k.ps[:, 4 + gr, 0:GR * RC], ALU.subtract).then_inc(S["x_ready"], 1)
                    dve.memset(sm[:, 0, :], 0.0).then_inc(S["state_ready"], 1)
                    dve.drain()
                    for s, n in enumerate(order[d][:-1]):
                        f = factor[:, n:n + 1]
                        dve.tensor_scalar(sf[:, :], sm[:, s % 2, :], f, None, ALU.mult)
                        dve.drain()
                        dve.wait_ge(S["ds_done"], 11 * dd + s + 1)
                        dve.scalar_tensor_tensor(out=sm[:, (s + 1) % 2, :], in0=k.ps[:, 2, 0:64], scalar=f, in1=sf[:, :],
                                                 op0=ALU.mult, op1=ALU.add).then_inc(S["state_ready"], 1)
                        dve.drain()
                    dve.wait_ge(S["y_done"], dd + 1)
                    if d == 0:
                        dve.tensor_copy(y, region(k, 3)).then_inc(S["y_read"], 1)
                    else:
                        dve.scalar_tensor_tensor(out=kds[:, :], in0=r[:, :], scalar=par["r_k"], in1=kds[:, :], op0=ALU.mult, op1=ALU.mult)
                        dve.tensor_tensor(y, y, region(k, 3), ALU.add)
                        dve.drain()
                        dve.tensor_copy(own[:, 0:1], own[:, 0:1]).then_inc(S["y_read"], 1)
                dve.wait_ge(S["mean_done"], i + 1)
                dve.scalar_tensor_tensor(out=y, in0=region(k, 0), scalar=-1.0 / HEAD, in1=y, op0=ALU.mult, op1=ALU.add).then_inc(S["centred"], 1)
                dve.wait_ge(S["var_done"], i + 1)
                dve.tensor_scalar(t2, region(k, 1), 1.0 / HEAD, GN_EPS, ALU.mult, ALU.add).then_inc(S["var_ready"], 1)
                dve.tensor_tensor(t1, region(k, 2), v[:, :], ALU.mult)
                dve.wait_ge(S["var_root"], i + 1)
                dve.reciprocal(t2, t2)
                dve.drain()
                dve.tensor_tensor(y, y, t2, ALU.mult)
                dve.drain()
                dve.tensor_scalar(y, y, par["lnx_g"], par["lnx_b"], ALU.mult, ALU.add)
                dve.drain()
                dve.tensor_tensor(y, y, t1, ALU.add)
                dve.drain()
                dve.tensor_tensor(k.mo[:, bass.ds(i, 1), :].rearrange("p a t -> p (a t)"), y, region(k, 3), ALU.mult).then_inc(S["pair_done"], 1)
    feed.at += 1


def _tiles(w, kc=KC):
    w = w.reshape(kc, P, -1, P)
    return w.transpose(2, 1, 0, 3).reshape(-1, P, kc * P)


def _features(v):
    return v.reshape(-1, P).T


def _constants(np):
    c = {}
    c["ident"] = np.eye(P)
    pos = np.arange(LAT)
    nf = HEAD // 4
    inv = 10000.0 ** (-np.arange(nf, dtype=np.float32) / nf)
    ang = np.stack([(pos // GRID_W)[:, None] * inv, (pos % GRID_W)[:, None] * inv], axis=1).astype(np.float32)
    ang = np.broadcast_to(ang[:, :, None, :], (LAT, 2, 2, nf)).reshape(LAT, HEAD).T
    c["cos"], c["sin"] = np.tile(np.cos(ang), (2, 1)), np.tile(np.sin(ang), (2, 1))
    rot = np.zeros((P, P))
    for b in range(0, P, 32):
        for n in range(nf):
            rot[b + nf + n, b + n] = -1.0
            rot[b + n, b + nf + n] = 1.0
    c["rot"] = rot
    i, j = np.arange(P)[:, None], np.arange(P)[None, :]
    c["window_mask"] = np.concatenate([np.where(j >= i, 0.0, NEG), np.zeros((P, P + CTX)), np.where(j <= i, 0.0, NEG)], 1)
    start = np.clip(np.arange(GRID_W) - 8, 0, GRID_W - 16)[:, None]
    kc = np.arange(GRID_W)[None, :]
    c["column_mask"] = np.tile(np.where((kc >= start) & (kc < start + 16), 0.0, NEG), (2, 1))
    same = (i // RC) == (j // RC)
    c["bones"] = same.astype(np.float32)
    c["ident2"] = np.tile(np.eye(RC), (2, 1))
    c["reset"] = np.broadcast_to((np.arange(TOK) % RC != 0).astype(np.float32), (P, TOK))
    s, t = np.arange(RC)[:, None], np.arange(RC)[None, :]
    tri = [np.concatenate([s < t, s <= t, s < t, s <= t], 1), np.concatenate([s > t, s >= t, s > t, s >= t], 1)]
    c["tri_mask"] = np.tile(np.stack(tri, 1), (2, 1, 1))
    lev = [[((s >> (l + 1)) == (t >> (l + 1))) & ((s >> l) != (t >> l)) & ((s < t) if d == 0 else (s > t))
            for l in range(LEVELS)] for d in range(2)]
    c["level_mask"] = np.tile(np.array(lev).transpose(2, 0, 1, 3), (2, 1, 1, 1))
    inv = np.zeros((P, 2, TOK))
    for g, win in enumerate((2, 4, 8, 16)):
        for a, n in ((0, LAT), (LAT, CTX)):
            tt = np.arange(n)
            inv[64 * (g % 2):64 * (g % 2) + 64, g // 2, a:a + n] = 1.0 / (np.clip(tt + win // 2, 0, n) - np.clip(tt - win // 2, 0, n))
    c["pool_inv"] = inv
    return {n: np.ascontiguousarray(a, dtype=np.float32) for n, a in c.items()}


def _layout(np, x):
    a = _constants(np)
    both = np.concatenate([x["x"][0], x["ctx"][0]], 0)
    a["h0"] = both.T.reshape(KC, P, TOK).transpose(1, 0, 2)
    a["ctx2"] = x["ctx_2"][0].T.reshape(KC, P, CTX).transpose(1, 0, 2)
    for l in range(2):
        a[f"ada{l}"], a[f"ada{2 + l}"] = _tiles(x["ada_w"][l]), _tiles(x["ada_w_2"][l])
        a[f"ffn_g{l}"], a[f"ffn_u{l}"] = _tiles(x["ffn_w_in"][l][:, :FF]), _tiles(x["ffn_w_in"][l][:, FF:])
        a[f"ffn_g{2 + l}"], a[f"ffn_u{2 + l}"] = _tiles(x["ffn_w1_2"][l]), _tiles(x["ffn_w3_2"][l])
        for n, w in ((l, x["ffn_w_out"][l]), (2 + l, x["ffn_w2_2"][l])):
            a[f"ffn_d{n}"] = w.reshape(2, HALF, P, KC, P).transpose(3, 0, 2, 1, 4).reshape(2 * KC, P, HALF * P)
    a["even_in"], a["even_out"] = _tiles(x["even_w_in"][0]), _tiles(x["even_w_out"][0])
    w = x["odd_w_qkv"][0]
    order = [8 * c + 4 * s + j for c in range(2) for j in range(4) for s in range(2)]
    wq = w[:, :1024].reshape(D, 16, HEAD)[:, order].reshape(D, 1024)
    a["odd_in"] = _tiles(np.concatenate([wq, w[:, 1024:]], 1))
    a["odd_out"] = _tiles(x["odd_w_out"][0].reshape(16, HEAD, D)[order].reshape(1024, D))
    w = x["ev_w_in_2"][0]
    a["ev_in"], a["ev_out"] = _tiles(w), _tiles(x["ev_w_out_2"][0])
    a["od_in"], a["od_out"] = _tiles(x["od_w_in_2"][0]), _tiles(x["od_w_out_2"][0])
    mu = x["ev_shift_mu_2"][0]
    small = dict(c=x["c"][0], cc=x["c_ctx"], c2=x["c_2"][0], cc2=x["c_ctx_2"], ada_b=x["ada_b"], ada_b2=x["ada_b_2"],
                 norm1=x["norm1_g"], norm2=x["norm2_g"], final=x["final_g"], subln=x["diff_subln_g"], ln_g=x["ln_g_2"],
                 ln_b=x["ln_b_2"], mu_lora=mu[:, 2304:], pool_scale=x["ev_pool_scale_2"])
    a["small"] = np.concatenate([_features(small[n]) for n, _ in SMALL], 1)
    pair = [mu[d, 768 * j:768 * j + 768] for d in range(2) for j in range(3)]
    pair += [x["ev_w0_2"][0, 0], x["ev_w0_2"][0, 1], x["ev_a0_2"][0, 0], x["ev_a0_2"][0, 1], x["ev_k_k_2"][0],
             x["ev_k_a_2"][0], x["ev_r_k_2"][0].reshape(-1), x["ev_lnx_g_2"][0], x["ev_lnx_b_2"][0]]
    pair = np.stack(pair, 1).reshape(PAIRS, P, NPAIR)
    lora = np.stack([x["ev_w2_2"][0].reshape(P, -1), x["ev_a2_2"][0].reshape(P, -1), x["ev_g2_2"][0]], 0)
    lora = lora.reshape(3, P, PAIRS, P).transpose(2, 1, 0, 3).reshape(PAIRS, P, 3 * P)
    a["pair"] = np.concatenate([pair, lora], 2)
    a["pool_w"] = x["ev_pool_w_2"][0].reshape(2, 2, 64, 64).transpose(1, 2, 0, 3).reshape(P, 2, 64)
    a["rows"] = np.concatenate([x[n].reshape(-1) for n in ("diff_lq1", "diff_lk1", "diff_lq2", "diff_lk2", "odd_sink", "sgu_b")])
    a["sgu_wt"] = x["sgu_w"][0].transpose(2, 0, 1)
    a["rpb"] = x["od_rpb_2"][0].reshape(16 * DR, DCOL)
    return {n: np.ascontiguousarray(v) for n, v in a.items()}


def kernel(**inputs):
    import numpy as np
    import concourse.bacc as bacc
    from concourse.bass_utils import run_bass_kernel_spmd

    nc = bacc.Bacc("TRN2", target_bir_lowering=False, num_devices=1)
    arrays = _layout(np, {n: np.asarray(v) for n, v in inputs.items()})
    io = {n: nc.dram_tensor(f"in_{n}", v.shape, F32, kind="ExternalInput").ap() for n, v in arrays.items()}
    out = nc.dram_tensor("out", (P, KC, LAT), F32, kind="ExternalOutput").ap()
    program(nc, io, out)
    result = run_bass_kernel_spmd(nc, [{f"in_{n}": v for n, v in arrays.items()}], core_ids=[0])
    y = result.results[0]["out"]
    return y.transpose(2, 1, 0).reshape(1, LAT, D)
```

```python
import math
from contextlib import ExitStack

import concourse.bass as bass
from concourse import mybir

F32 = mybir.dt.float32
F32R = mybir.dt.float32r
ALU = mybir.AluOpType
ACT = mybir.ActivationFunctionType
AX = mybir.AxisListType

P = 128
D = 1024
KC = D // P
LAT, CTX = 512, 256
TOK = LAT + CTX
HEAD = 64
GRID_W = 64
FF = 2816
FC = FF // P
HALF = FC // 2
SIDE = 4
RING = 4
SLOT = HALF * P
EPS = 1e-6
GN_EPS = 64e-5
ALPHA = 4 ** 0.25
LAM_INIT = 0.8 - 0.6 * math.exp(-0.3 * 0)
SCALE = HEAD ** -0.5
RC = 64
NCH = TOK // RC
PAIRS = 6
RW = 21
NEG = -1e30
DR = 2 * 8 - 1
DCOL = 2 * 16 - 1
PADW = 2 * GRID_W - 1
LEVELS = 6

SMALL = [("c", 8), ("cc", 8), ("c2", 8), ("cc2", 8), ("ada_b", 96), ("ada_b2", 96), ("norm1", 16), ("norm2", 16),
         ("final", 8), ("subln", 1), ("ln_g", 32), ("ln_b", 32), ("mu_lora", 6), ("pool_scale", 2)]
COL = {}
for _name, _n in SMALL:
    COL[_name] = (sum(n for _, n in SMALL[:len(COL)]), _n)
NSMALL = sum(n for _, n in SMALL)
PAIRCOL = {n: c for c, n in enumerate(["mu0r", "mu0k", "mu0v", "mu1r", "mu1k", "mu1v", "w0_0", "w0_1", "a0_0", "a0_1",
                                       "k_k", "k_a", "r_k", "lnx_g", "lnx_b"])}
NPAIR = len(PAIRCOL)
ROWCOL = {"lam": 0, "sink": 256, "sgu_b": 272}
NROWS = 784


class Stage:

    def __init__(self, k, name):
        self.k, self.name = k, name

    def __enter__(self):
        k = self.k
        self.ids = list(k.sem_pools[k.stage_no % 2])
        self.clear = k.sem_pools[(k.stage_no + 1) % 2] if k.stage_no else None
        self.first = self.ids[0]
        self.mine = []
        self.stack = ExitStack()
        self.block = self.stack.enter_context(k.nc.Block(f"{self.name}_{k.stage_no}", no_gpsimd_drain=True))
        k.stage_no += 1
        return self

    def sem(self, name):
        s = self.k.nc.alloc_semaphore(f"{self.name}_{self.k.stage_no}_{name}", num=self.ids.pop(0))
        self.mine.append(s)
        return s

    def sb(self, name, shape, dtype=F32):
        return self.k.tmp.enter_context(self.k.nc.sbuf_tensor(f"{self.name}_{self.k.stage_no}_{name}", shape, dtype))

    def clear_last(self, pool):
        if self.clear:
            pool.drain()
            pool.sem_clear(range(self.clear[0], self.clear[-1] + 1))

    def __exit__(self, *a):
        self.stack.close()
        for s in self.mine:
            self.k.nc.release_semaphore(s)


class Feed:

    def __init__(self, k, plan, ring, name):
        self.plan, self.at = plan, 0
        self.ring = ring
        self.landed = [k.nc.alloc_semaphore(f"{name}_landed{s}") for s in range(RING)]
        self.used = [k.nc.alloc_semaphore(f"{name}_used{s}") for s in range(RING)]
        base = [0] * RING
        self.base = []
        for _, n, pattern in plan:
            self.base.append(list(base))
            for slot, *_ in pattern:
                base[slot] += n

    def count(self, stage, j):
        _, _, pattern = self.plan[stage]
        slot = pattern[j][0]
        before = self.base[stage][slot] + sum(1 for e in pattern[:j] if e[0] == slot)
        return slot, before, sum(1 for e in pattern if e[0] == slot)

    def issue(self, sp, stage, i, ahead=None):
        for j, (slot, src, mul, off) in enumerate(self.plan[stage][2]):
            slot, before, per = self.count(stage, j)
            if ahead is not None and ahead != (before == self.base[stage][slot]):
                continue
            if not (isinstance(i, int) and before + per * i == 0):
                sp.wait_ge(self.used[slot], per * i + before)
            w = src.shape[2]
            t = src[mul * i + off] if isinstance(i, int) else src[bass.ds(mul * i + off, 1)].rearrange("a p w -> (a p) w")
            sp.dma_start(self.ring[:, slot, 0:w], t).then_inc(self.landed[slot], 16)

    def program(self, sp, side=None):
        s = self.at
        n = self.plan[s][1]
        self.issue(sp, s, 0, ahead=False)
        if side:
            side.issue(sp, side.at, 0)
        if n > 1:
            with sp.Fori(1, n) as i:
                self.issue(sp, s, i)
                if side:
                    side.issue(sp, side.at, i)
        if s + 1 < len(self.plan):
            self.issue(sp, s + 1, 0, ahead=True)

    def wait(self, pe, i, j):
        slot, before, per = self.count(self.at, j)
        pe.wait_ge(self.landed[slot], 16 * per * i + 16 * (before + 1))
        return slot

    def done(self, matmul, j):
        matmul.then_inc(self.used[self.count(self.at, j)[0]], 1)

    def wait_done(self, eng, i, j):
        slot, before, per = self.count(self.at, j)
        eng.wait_ge(self.used[slot], per * i + before + 1)


class Split:

    def __init__(self, k, st, slots, width=KC * P):
        self.k, self.slots = k, slots
        self.high = st.sb("high", [P, slots, width], F32R)
        self.low = st.sb("low", [P, slots, width], F32R)
        self.products, self.high_ready = st.sem("products"), st.sem("high_ready")

    def start(self, pe):
        pe.sem_inc(self.products, self.slots)

    def entry(self, i, j, base):
        return len(self.k.feed.plan[self.k.feed.at][2]) * i + base + j

    def write_high(self, act, i, j, base=0):
        feed = self.k.feed
        slot, before, per = feed.count(feed.at, j)
        w = feed.plan[feed.at][2][j][1].shape[2]
        act.wait_ge(feed.landed[slot], 16 * per * i + 16 * (before + 1))
        act.wait_ge(self.products, self.entry(i, j, base) + 1)
        act.activation(self.high[:, j % self.slots, 0:w], feed.ring[:, slot, 0:w], ACT.Copy).then_inc(self.high_ready, 1)

    def write_low(self, pool, i, j, base=0):
        feed = self.k.feed
        slot, before, per = feed.count(feed.at, j)
        w = feed.plan[feed.at][2][j][1].shape[2]
        pool.wait_ge(self.high_ready, self.entry(i, j, base) + 1)
        pool.tensor_tensor(self.low[:, j % self.slots, 0:w], feed.ring[:, slot, 0:w],
                           self.high[:, j % self.slots, 0:w].bitcast(F32), ALU.subtract).then_inc(feed.used[slot], 1)

    def wait(self, pe, i, j):
        feed = self.k.feed
        slot, before, per = feed.count(feed.at, j)
        pe.wait_ge(feed.used[slot], per * i + before + 1)
        return j % self.slots

    def wait_done(self, eng, i, j, base=0):
        eng.wait_ge(self.products, self.entry(i, j, base) + 1 + self.slots)

    def products_of(self, pe, dst, weights, values, first=True, last=True):
        pairs = ((0, 0), (0, 1), (1, 0))
        for n, (a, b) in enumerate(pairs):
            mm = pe.matmul(dst, weights[a], values[b], start=first and n == 0, stop=last and n == 2)
        return mm


class SideModulation:

    def __init__(self, k, st, names):
        self.k, self.names = k, names
        self.vec = st.sb("side_vec", [P, KC, 2])
        self.ready = st.sem("side_vec_ready")
        self.done = st.sem("side_done")
        self.bank = k.ps[:, 6, 0:2 * 48]

    def scalar(self, act):
        for s, name in enumerate(self.names):
            ins = act.activation(self.vec[:, :, s], col(self.k, name, 0, KC), ACT.Silu)
        ins.then_inc(self.ready, 1)

    def tensor(self, pe, i, j, tile, signal=False):
        side = self.k.side
        slot = side.wait(pe, i, j)
        for c in range(KC):
            mm = pe.matmul(self.bank[:, bass.ds(2 * tile, 2)], side.ring[:, slot, c * P:(c + 1) * P], self.vec[:, c, :],
                           start=c == 0, stop=c == KC - 1)
        side.done(mm, j)

    def vector(self, dve, bias, last):
        self.k.side.wait_done(dve, *last)
        both = self.bank.rearrange("p (n s) -> p n s", s=2)
        for s in range(2):
            dve.tensor_tensor(self.k.mod_next[:, :, s], both[:, :, s], bias, ALU.add)


def spans(tokens):
    return [(0, LAT, 0), (LAT, TOK, 1)] if tokens == TOK else [(0, LAT, 0)]


class K:
    pass


def program(nc, io, out):
    k = K()
    k.nc = nc
    k.io = io
    k.stage_no = 0
    with ExitStack() as ctx:
        def sb(name, shape):
            return ctx.enter_context(nc.sbuf_tensor(name, shape, F32))

        k.h = sb("h", [P, KC, TOK])
        k.ring = sb("ring", [P, RING, SLOT])
        k.small = sb("small", [P, NSMALL])
        k.mod, k.mod_next = sb("mod_even", [P, 6 * KC, 2]), sb("mod_odd", [P, 6 * KC, 2])
        k.ident = sb("ident", [P, P])
        k.ones = sb("ones", [P, P])
        k.eps = sb("eps", [P, 2])
        k.ps = ctx.enter_context(nc.psum_tensor("ps", [P, 8, 512], F32))
        k.psf = k.ps[:, :, :].rearrange("p b n -> p (b n)")
        k.setup_sem = nc.alloc_semaphore("setup_sem")
        k.out_sem = nc.alloc_semaphore("out_sem")
        k.rows_sem = nc.alloc_semaphore("rows_sem")
        k.bias_sem = nc.alloc_semaphore("bias_sem")
        k.pair_landed = nc.alloc_semaphore("pair_landed")
        k.bias_landed = [nc.alloc_semaphore(f"bias_landed{j}") for j in range(4)]
        k.feed = Feed(k, weight_plan(io), k.ring, "weights")
        k.side = Feed(k, side_plan(io), None, "side")
        first = max(s.num for s in k.side.used) + 1
        k.sem_pools = [range(first, first + 40), range(first + 40, first + 80)]
        k.padded = nc.dram_tensor("padded_bias", (16 * DR, PADW), F32).ap()
        k.toeplitz = nc.dram_tensor("toeplitz_bias", (16, GRID_W, DR, GRID_W), F32).ap()

        load_inputs(k)
        modulation(k, "c", "cc", "ada_b", 0)
        with mixer(k, split=True):
            rms_modulate(k, TOK, 1, 0, "norm1", 0)
            with ExitStack() as k.tmp:
                gating_mlp(k)
            with ExitStack() as k.tmp:
                diff_attention(k)
        project_out(k, TOK, 2)
        with channel_mixer(k):
            rms_modulate(k, TOK, 4, 3, "norm2", 0)
            feed_forward(k, TOK, 5, ("c", "cc"), col(k, "ada_b", 48, 48))
        with mixer(k, split=True):
            rms_modulate(k, TOK, 1, 0, "norm1", 1)
            with ExitStack() as k.tmp:
                window_attention(k)
        project_out(k, LAT, 2)
        with channel_mixer(k):
            rms_modulate(k, LAT, 4, 3, "norm2", 1)
            feed_forward(k, LAT, 5, ("c2", "cc2"), col(k, "ada_b2", 0, 48))
        rms_modulate(k, LAT, None, None, "final", 0)
        with mixer(k, split=False):
            affine(k, TOK, 1, 0, load_context=True)
            with ExitStack() as k.tmp:
                rwkv(k)
        project_out(k, TOK, 2)
        layer_norm(k, TOK, 0)
        with channel_mixer(k):
            affine(k, TOK, 4, 3)
            feed_forward(k, TOK, 5, ("c2", "cc2"), col(k, "ada_b2", 48, 48))
        layer_norm(k, TOK, 1)
        with mixer(k, split=True):
            affine(k, TOK, 1, 0)
            with ExitStack() as k.tmp:
                neighbourhood_attention(k)
        project_out(k, LAT, 2)
        layer_norm(k, LAT, 2)
        with channel_mixer(k):
            affine(k, LAT, 4, 3)
            feed_forward(k, LAT, 5)
        layer_norm(k, LAT, 3)
        store(k, out)


class mixer:

    def __init__(self, k, split):
        self.k, self.split = k, split

    def __enter__(self):
        k = self.k
        k.mo_stack, self.stack = ExitStack(), ExitStack()
        k.mo = k.mo_stack.enter_context(k.nc.sbuf_tensor(f"mo{k.stage_no}", [P, KC, TOK], F32))
        stream_buffers(k, self.stack, self.split)

    def __exit__(self, *a):
        self.stack.close()


class channel_mixer(mixer):

    def __init__(self, k):
        self.k = k

    def __enter__(self):
        self.stack = ExitStack()
        stream_buffers(self.k, self.stack, True)


def stream_buffers(k, stack, split):
    new = lambda name, dt: stack.enter_context(k.nc.sbuf_tensor(f"{name}{k.stage_no}", [P, KC, TOK], dt))
    k.split = split
    k.hn = (new("hn_high", F32R), new("hn_low", F32R)) if split else new("hn", F32)


def weight_plan(io):
    def ada(w):
        return ("modulation", 12, [(s, w, 4, s) for s in range(4)])

    def out(w):
        return ("project_out", 2, [(s, w, 4, s) for s in range(4)])

    def ffn(g, u, d):
        return [part for h in range(2) for part in (
            ("feed_up_first", 1, [(0, g, 0, HALF * h), (1, u, 0, HALF * h)]),
            ("feed_up", HALF // 2, [((2 + 2 * p + m) % 4, w, 2, HALF * h + 1 + p) for p in range(2) for m, w in enumerate((g, u))]),
            ("feed_down", 2, [(s, d, 4, KC * h + s) for s in range(4)]))]

    ew, ow, rw, nw = io["even_in"], io["odd_in"], io["ev_in"], io["od_in"]
    return [
        ada(io["ada0"]),
        ("gating", 2, [(0, ew, 2, 0), (1, ew, 2, 4), (2, ew, 2, 1), (3, ew, 2, 5)]),
        ("diff", 4, [(0, ew, 1, 8), (1, ew, 1, 12), (2, ew, 1, 16)]),
        out(io["even_out"]), *ffn(io["ffn_g0"], io["ffn_u0"], io["ffn_d0"]),
        ("window", 2, [(0, ow, 1, 8), (1, ow, 1, 10)] + [((2 + j) % 4, ow, 4, j) for j in range(4)]),
        out(io["odd_out"]), *ffn(io["ffn_g1"], io["ffn_u1"], io["ffn_d1"]),
        ("lora", 1, [(j % 4, rw, 0, 18 + j) for j in range(5)]),
        ("rwkv", PAIRS, [(1, rw, 1, 0), (2, rw, 1, 6), (3, rw, 1, 12)]),
        out(io["ev_out"]), *ffn(io["ffn_g2"], io["ffn_u2"], io["ffn_d2"]),
        ("neighbour", 8, [(0, nw, 1, 0), (1, nw, 1, 8), (2, nw, 1, 16)]),
        out(io["od_out"]), *ffn(io["ffn_g3"], io["ffn_u3"], io["ffn_d3"]),
    ]


def side_plan(io):
    return [part for w in ("ada1", "ada2", "ada3") for h in range(2) for part in (
        ("up", HALF // 2, [(s, io[w], 4, 24 * h + s) for s in range(4)]),
        ("down", 2, [(s, io[w], 2, 24 * h + 20 + s) for s in range(2)]))]


def col(k, name, at=0, n=1):
    a = COL[name][0] + at
    return k.small[:, a:a + n]


def region(k, r, n=TOK):
    return k.psf[:, 1024 * r:1024 * r + n]


def load_inputs(k):
    with Stage(k, "load") as st:
        @st.block.sync
        def _(sp):
            for dst, src in ((k.small[:, :], k.io["small"]), (k.ident[:, :], k.io["ident"]),
                             (k.h[:, :, :], k.io["h0"])):
                sp.dma_start(dst, src).then_inc(k.setup_sem, 16)
            k.feed.issue(sp, 0, 0, ahead=True)
            sp.wait_ge(k.setup_sem, 48)

        @st.block.vector
        def _(dve):
            dve.memset(k.ones[:, :], 1.0)
            dve.memset(k.eps[:, 0:1], EPS)
            dve.memset(k.eps[:, 1:2], GN_EPS)


def store(k, out):
    with Stage(k, "store") as st:
        @st.block.sync
        def _(sp):
            sp.dma_start(out, k.h[:, :, 0:LAT]).then_inc(k.out_sem, 16)
            sp.wait_ge(k.out_sem, 16)


def modulation(k, c, cc, bias, layer):
    feed = k.feed
    with ExitStack() as k.tmp, Stage(k, "modulation") as st:
        vec = st.sb("vec", [P, KC, 2])
        silu_ready, products_read = st.sem("silu_ready"), st.sem("products_read")
        psum = k.ps[:, 0:RING, 0:2]

        @st.block.sync
        def _(sp):
            feed.program(sp)

        @st.block.gpsimd
        def _(pool):
            st.clear_last(pool)
            zeros = st.sb("zeros", [120, 2 * PADW])
            pool.memset(zeros[:, :], 0.0)
            pool.drain()
            pool.dma_start(k.padded.rearrange("(p r) c -> p (r c)", p=120), zeros[:, :]).then_inc(k.bias_sem, 16)
            pool.wait_ge(k.bias_sem, 16)
            left = (PADW - DCOL) // 2
            pool.dma_start(k.padded[:, left:left + DCOL], k.io["rpb"]).then_inc(k.bias_sem, 16)
            pool.wait_ge(k.bias_sem, 32)
            with pool.Fori(0, GRID_W) as q:
                pool.dma_start(k.toeplitz[:, bass.ds(q, 1), :, :].rearrange("h a r c -> (h a) r c"),
                               k.padded.rearrange("(h r) c -> h r c", h=16)[:, :, bass.ds(GRID_W - 1 - q, GRID_W)]).then_inc(k.bias_sem, 16)

        @st.block.scalar
        def _(act):
            act.activation(vec[:, :, 0], col(k, c, 0, KC), ACT.Silu)
            act.activation(vec[:, :, 1], col(k, cc, 0, KC), ACT.Silu).then_inc(silu_ready, 1)

        @st.block.tensor
        def _(pe):
            pe.wait_ge(silu_ready, 1)
            with pe.Fori(0, 12) as i:
                pe.wait_ge(products_read, i + 1)
                for j in range(RING):
                    slot = feed.wait(pe, i, j)
                    for c_ in range(KC):
                        mm = pe.matmul(psum[:, j, :], k.ring[:, slot, c_ * P:(c_ + 1) * P], vec[:, c_, :],
                                       start=c_ == 0, stop=c_ == KC - 1)
                    feed.done(mm, j)

        @st.block.vector
        def _(dve):
            b = col(k, bias, layer * 48, 48)
            dve.sem_inc(products_read, 1)
            with dve.Fori(0, 12) as i:
                feed.wait_done(dve, i, RING - 1)
                for s in range(2):
                    ins = dve.tensor_tensor(k.mod[:, bass.ds(4 * i, 4), s], psum[:, :, s], b[:, bass.ds(4 * i, 4)], ALU.add)
                ins.then_inc(products_read, 1)
    feed.at += 1


class StreamParts:

    def __init__(self, k, st, tokens):
        self.k, self.n = k, tokens
        self.whole = st.sb("whole", [P, 2, TOK])
        self.high_ready, self.low_ready = st.sem("stream_high"), st.sem("stream_low")

    def claim(self, act, c):
        if c >= 2:
            act.wait_ge(self.low_ready, c - 1)

    def scalar(self, act, c):
        act.drain()
        act.activation(self.k.hn[0][:, c, 0:self.n], self.whole[:, c % 2, 0:self.n], ACT.Copy).then_inc(self.high_ready, 1)

    def gpsimd(self, pool):
        for c in range(KC):
            pool.wait_ge(self.high_ready, c + 1)
            pool.tensor_tensor(self.k.hn[1][:, c, 0:self.n], self.whole[:, c % 2, 0:self.n],
                               self.k.hn[0][:, c, 0:self.n].bitcast(F32), ALU.subtract).then_inc(self.low_ready, 1)
        pool.drain()


def rms_modulate(k, tokens, scale_at, shift_at, gain, layer):
    final = scale_at is None
    dst = k.h if final else None if k.split else k.hn
    with ExitStack() as k.tmp, Stage(k, "rms") as st:
        sq = st.sb("sq", [P, 2, TOK])
        gains = st.sb("gains", [P, KC, 2])
        rstd = st.sb("rstd", [P, TOK])
        squared, summed, gains_ready = st.sem("squared"), st.sem("summed"), st.sem("gains_ready")
        var_ready, root_ready = st.sem("var_ready"), st.sem("root_ready")
        scaled, shifted = st.sem("scaled"), st.sem("shifted")
        acc = region(k, 0, tokens)
        parts = StreamParts(k, st, tokens) if dst is None else None

        @st.block.gpsimd
        def _(pool):
            st.clear_last(pool)
            if parts:
                parts.gpsimd(pool)

        @st.block.scalar
        def _(act):
            for c in range(KC):
                if c >= 2:
                    act.wait_ge(summed, c - 1)
                act.activation(sq[:, c % 2, 0:tokens], k.h[:, c, 0:tokens], ACT.Square).then_inc(squared, 1)
            act.wait_ge(var_ready, 1)
            act.activation(rstd[:, 0:tokens], rstd[:, 0:tokens], ACT.Sqrt).then_inc(root_ready, 1)
            act.wait_ge(gains_ready, 1)
            for c in range(KC):
                act.wait_ge(scaled, c + 1)
                for a, b, s in spans(tokens):
                    shift = 0.0 if final else k.mod[:, shift_at * KC + c, s:s + 1]
                    if parts and a == 0:
                        parts.claim(act, c)
                    ins = act.activation(parts.whole[:, c % 2, a:b] if parts else dst[:, c, a:b], sq[:, c % 2, a:b], ACT.Identity,
                                         scale=gains[:, c, s:s + 1], bias=shift)
                ins.then_inc(shifted, 1)
                if parts:
                    parts.scalar(act, c)

        @st.block.tensor
        def _(pe):
            for c in range(KC):
                pe.wait_ge(squared, c + 1)
                for a, b, _ in spans(tokens):
                    mm = pe.matmul(acc[:, a:b], k.ones[:, :], sq[:, c % 2, a:b], start=c == 0, stop=c == KC - 1)
                mm.then_inc(summed, 1)

        @st.block.vector
        def _(dve):
            g = col(k, gain, layer * KC, KC)
            for s in range(2):
                if final:
                    ins = dve.tensor_copy(gains[:, :, s], g)
                else:
                    ins = dve.scalar_tensor_tensor(out=gains[:, :, s], in0=k.mod[:, scale_at * KC:(scale_at + 1) * KC, s],
                                                   scalar=1.0, in1=g, op0=ALU.add, op1=ALU.mult)
            ins.then_inc(gains_ready, 1)
            dve.wait_ge(summed, KC)
            dve.tensor_scalar(rstd[:, 0:tokens], acc, 1.0 / D, EPS, ALU.mult, ALU.add).then_inc(var_ready, 1)
            dve.wait_ge(root_ready, 1)
            dve.reciprocal(rstd[:, 0:tokens], rstd[:, 0:tokens])
            dve.drain()
            for c in range(KC):
                if c >= 2:
                    dve.wait_ge(shifted, c - 1)
                dve.tensor_tensor(sq[:, c % 2, 0:tokens], k.h[:, c, 0:tokens], rstd[:, 0:tokens], ALU.mult).then_inc(scaled, 1)


def affine(k, tokens, scale_at, shift_at, load_context=False):
    with ExitStack() as k.tmp, Stage(k, "affine") as st:
        gains = st.sb("gains", [P, KC, 2])
        gains_ready, copied, context_landed = st.sem("gains_ready"), st.sem("copied"), st.sem("context_landed")

        parts = StreamParts(k, st, tokens) if k.split else None

        @st.block.sync
        def _(sp):
            if load_context:
                sp.dma_start(k.h[:, :, LAT:TOK], k.io["ctx2"]).then_inc(context_landed, 16)

        @st.block.gpsimd
        def _(pool):
            st.clear_last(pool)
            if parts:
                parts.gpsimd(pool)

        @st.block.scalar
        def _(act):
            act.wait_ge(gains_ready, 1)
            if load_context:
                act.wait_ge(context_landed, 16)
            for c in range(KC):
                for a, b, s in spans(tokens):
                    if parts and a == 0:
                        parts.claim(act, c)
                    ins = act.activation(parts.whole[:, c % 2, a:b] if parts else k.hn[:, c, a:b], k.h[:, c, a:b], ACT.Identity,
                                         scale=gains[:, c, s:s + 1], bias=k.mod[:, shift_at * KC + c, s:s + 1])
                ins.then_inc(copied, 1)
                if parts:
                    parts.scalar(act, c)

        @st.block.vector
        def _(dve):
            dve.tensor_scalar(gains[:, :, :], k.mod[:, scale_at * KC:(scale_at + 1) * KC, :], 1.0, None,
                              ALU.add).then_inc(gains_ready, 1)
            for c in range(KC):
                dve.wait_ge(copied, c + 1)
                dve.tensor_scalar(k.h[:, c, 0:tokens], k.h[:, c, 0:tokens], ALPHA, None, ALU.mult)


def layer_norm(k, tokens, which):
    with ExitStack() as k.tmp, Stage(k, "layernorm") as st:
        sq = st.sb("sq", [P, 2, TOK])
        rstd = st.sb("rstd", [P, TOK])
        mean_ready, centred, squared, summed = st.sem("mean_ready"), st.sem("centred"), st.sem("squared"), st.sem("summed")
        var_ready, root_ready, scaled = st.sem("var_ready"), st.sem("root_ready"), st.sem("scaled")
        total, acc = region(k, 0, tokens), region(k, 1, tokens)

        @st.block.gpsimd
        def _(pool):
            st.clear_last(pool)

        @st.block.tensor
        def _(pe):
            for c in range(KC):
                for a, b, _ in spans(tokens):
                    mm = pe.matmul(total[:, a:b], k.ones[:, :], k.h[:, c, a:b], start=c == 0, stop=c == KC - 1)
            mm.then_inc(mean_ready, 1)
            for c in range(KC):
                pe.wait_ge(squared, c + 1)
                for a, b, _ in spans(tokens):
                    mm = pe.matmul(acc[:, a:b], k.ones[:, :], sq[:, c % 2, a:b], start=c == 0, stop=c == KC - 1)
                mm.then_inc(summed, 1)

        @st.block.vector
        def _(dve):
            dve.wait_ge(mean_ready, 1)
            for c in range(KC):
                dve.scalar_tensor_tensor(out=k.h[:, c, 0:tokens], in0=total, scalar=-1.0 / D, in1=k.h[:, c, 0:tokens],
                                         op0=ALU.mult, op1=ALU.add).then_inc(centred, 1)
            dve.wait_ge(summed, KC)
            dve.tensor_scalar(rstd[:, 0:tokens], acc, 1.0 / D, EPS, ALU.mult, ALU.add).then_inc(var_ready, 1)
            dve.wait_ge(root_ready, 1)
            dve.reciprocal(rstd[:, 0:tokens], rstd[:, 0:tokens])
            dve.drain()
            for c in range(KC):
                dve.tensor_tensor(k.h[:, c, 0:tokens], k.h[:, c, 0:tokens], rstd[:, 0:tokens], ALU.mult).then_inc(scaled, 1)

        @st.block.scalar
        def _(act):
            for c in range(KC):
                act.wait_ge(centred, c + 1)
                if c >= 2:
                    act.wait_ge(summed, c - 1)
                act.activation(sq[:, c % 2, 0:tokens], k.h[:, c, 0:tokens], ACT.Square).then_inc(squared, 1)
            act.wait_ge(var_ready, 1)
            act.activation(rstd[:, 0:tokens], rstd[:, 0:tokens], ACT.Sqrt).then_inc(root_ready, 1)
            for c in range(KC):
                act.wait_ge(scaled, c + 1)
                act.activation(k.h[:, c, 0:tokens], k.h[:, c, 0:tokens], ACT.Identity,
                               scale=col(k, "ln_g", which * KC + c), bias=col(k, "ln_b", which * KC + c))


def tile_products(k, pe, i, j, dst, src, tokens, split=None, chunks=range(KC), first=True, last=True):
    slot = split.wait(pe, i, j) if split else k.feed.wait(pe, i, j)
    for a, b, _ in spans(tokens):
        for n, c in enumerate(chunks):
            lo, hi = first and n == 0, last and n == len(chunks) - 1
            cols = slice(n * P, (n + 1) * P)
            if split:
                mm = split.products_of(pe, dst[:, a:b], (split.high[:, slot, cols], split.low[:, slot, cols]),
                                       (src[0][:, c, a:b], src[1][:, c, a:b]), lo, hi)
            else:
                mm = pe.matmul(dst[:, a:b], k.ring[:, slot, cols], src[:, c, a:b], start=lo, stop=hi)
    if split:
        mm.then_inc(split.products, 1)
    else:
        k.feed.done(mm, j)


def token_products(k, pe, i, j, dst, src, tokens, split):
    slot = split.wait(pe, i, j)
    for t in range(tokens // P):
        ts = slice(t * P, (t + 1) * P)
        for c in range(KC):
            cols = slice(c * P, (c + 1) * P)
            mm = split.products_of(pe, dst[:, ts], (src[0][:, c, ts], src[1][:, c, ts]),
                                   (split.high[:, slot, cols], split.low[:, slot, cols]), c == 0, c == KC - 1)
    mm.then_inc(split.products, 1)


def project_out(k, tokens, gate_at):
    with ExitStack() as k.tmp, Stage(k, "project") as st:
        free = st.sem("psum_free")

        @st.block.sync
        def _(sp):
            k.feed.program(sp)

        @st.block.gpsimd
        def _(pool):
            st.clear_last(pool)

        @st.block.tensor
        def _(pe):
            with pe.Fori(0, 2) as i:
                for j in range(4):
                    pe.wait_ge(free, 4 * i + j + 1)
                    tile_products(k, pe, i, j, region(k, j, tokens), k.mo, tokens)

        @st.block.vector
        def _(dve):
            dve.sem_inc(free, 4)
            with dve.Fori(0, 2) as i:
                for j in range(4):
                    k.feed.wait_done(dve, i, j)
                    residual(k, dve, tokens, gate_at, 4 * i + j, j).then_inc(free, 1)
    k.feed.at += 1
    k.mo_stack.close()


def residual(k, dve, tokens, gate_at, n, r):
    for a, b, s in spans(tokens):
        hs = k.h[:, bass.ds(n, 1), a:b].rearrange("p a t -> p (a t)")
        ins = dve.scalar_tensor_tensor(out=hs, in0=region(k, r)[:, a:b], scalar=k.mod[:, bass.ds(n + gate_at * KC, 1), s],
                                       in1=hs, op0=ALU.mult, op1=ALU.add)
    return ins


def feed_forward(k, tokens, gate_at, next_c=None, next_bias=None):
    feed, side = k.feed, k.side
    FIRST, UP, DOWN = 2, 4 * (HALF // 2), 8
    with ExitStack() as k.tmp, Stage(k, "feed") as st:
        split = Split(k, st, 2, SLOT)
        hid = st.sb("hid_high", [P, HALF, tokens], F32R), st.sb("hid_low", [P, HALF, tokens], F32R)
        gate, whole = st.sb("gate", [P, tokens]), st.sb("whole", [P, tokens])
        gated, multiplied, hid_high_ready, hid_low_ready, y_free = (
            st.sem("gated"), st.sem("multiplied"), st.sem("hid_high_ready"), st.sem("hid_low_ready"), st.sem("y_free"))
        if next_c:
            side.ring = st.sb("side_ring", [P, SIDE, KC * P])
            sm = SideModulation(k, st, next_c)
        GATE, UPR = region(k, 0, tokens), region(k, 1, tokens)
        base, side_base = feed.at, side.at

        def sections(h):
            e = h * (FIRST + UP + DOWN)
            return (base + 3 * h, e), (base + 3 * h + 1, e + FIRST), (base + 3 * h + 2, e + FIRST + UP)

        @st.block.sync
        def _(sp):
            for h in range(2):
                for n, (at, _) in enumerate(sections(h)):
                    feed.at = at
                    side.at = side_base + 2 * h + (n == 2)
                    feed.program(sp, side if next_c and n != 0 else None)
            feed.at, side.at = base, side_base

        @st.block.gpsimd
        def _(pool):
            st.clear_last(pool)
            for h in range(2):
                for at, e in sections(h):
                    feed.at = at
                    if feed.plan[at][1] > 1:
                        with pool.Fori(0, feed.plan[at][1]) as i:
                            for j in range(4):
                                split.write_low(pool, i, j, e)
                    else:
                        for j in range(2):
                            split.write_low(pool, 0, j, e)
            feed.at = base

        @st.block.tensor
        def _(pe):
            split.start(pe)
            if next_c:
                pe.wait_ge(sm.ready, 1)
            for h in range(2):
                (first, _), (up, _), (down, _) = sections(h)

                def chunk(i, p, n):
                    pe.wait_ge(gated, n + (HALF * h + 1))
                    tile_products(k, pe, i, 2 * p, GATE, k.hn, tokens, split)
                    pe.wait_ge(multiplied, n + (HALF * h + 1))
                    tile_products(k, pe, i, 2 * p + 1, UPR, k.hn, tokens, split)

                feed.at = first
                if h:
                    pe.wait_ge(y_free, 8 * h + 2)
                chunk(0, 0, 0)
                feed.at, side.at = up, side_base + 2 * h
                with pe.Fori(0, HALF // 2) as i:
                    for p in range(2):
                        chunk(i, p, 2 * i + (p + 1))
                        if next_c:
                            for j in (2 * p, 2 * p + 1):
                                sm.tensor(pe, i, j, 4 * i + (24 * h + j))
                feed.at, side.at = down, side_base + 2 * h + 1
                pe.wait_ge(hid_low_ready, HALF * (h + 1))
                with pe.Fori(0, 2) as i:
                    for j in range(4):
                        pe.wait_ge(y_free, 4 * i + (8 * h + j + 1))
                        tile_products(k, pe, i, j, region(k, j % 2, tokens), hid, tokens, split, chunks=range(HALF))
                        if next_c and j < 2:
                            sm.tensor(pe, i, j, 2 * i + (24 * h + 20 + j))
            feed.at, side.at = base, side_base

        @st.block.scalar
        def _(act):
            if next_c:
                sm.scalar(act)
            act.sem_inc(gated, 1)
            for h in range(2):
                (first, e), (up, e1), (down, e2) = sections(h)

                def store_high(n):
                    act.wait_ge(multiplied, n + (HALF * h + 2))
                    act.activation(hid[0][:, bass.ds(n, 1), :].rearrange("p a t -> p (a t)"), whole[:, :],
                                   ACT.Copy).then_inc(hid_high_ready, 1)

                def gate_chunk(i, p, eb):
                    split.write_high(act, i, 2 * p + 1, eb)
                    split.wait_done(act, i, 2 * p, eb)
                    act.activation(gate[:, :], GATE, ACT.Silu).then_inc(gated, 1)

                feed.at = first
                split.write_high(act, 0, 0, e)
                gate_chunk(0, 0, e)
                feed.at = up
                with act.Fori(0, HALF // 2) as i:
                    for p in range(2):
                        split.write_high(act, i, 2 * p, e1)
                        store_high(2 * i + p)
                        gate_chunk(i, p, e1)
                feed.at = down
                split.write_high(act, 0, 0, e2)
                store_high(HALF - 1)
                for n in range(1, DOWN):
                    split.write_high(act, n // 4, n % 4, e2)
            feed.at = base

        @st.block.vector
        def _(dve):
            dve.sem_inc(multiplied, 1)
            dve.sem_inc(y_free, 2)
            for h in range(2):
                (first, e), (up, e1), (down, e2) = sections(h)

                def chunk(i, p, n, eb):
                    split.wait_done(dve, i, 2 * p + 1, eb)
                    dve.wait_ge(gated, n + (HALF * h + 2))
                    dve.tensor_tensor(whole[:, :], gate[:, :], UPR, ALU.mult).then_inc(multiplied, 1)
                    dve.wait_ge(hid_high_ready, n + (HALF * h + 1))
                    high = hid[0][:, bass.ds(n, 1), :].rearrange("p a t -> p (a t)").bitcast(F32)
                    dve.tensor_tensor(hid[1][:, bass.ds(n, 1), :].rearrange("p a t -> p (a t)"), whole[:, :], high,
                                      ALU.subtract).then_inc(hid_low_ready, 1)
                    dve.drain()

                feed.at = first
                chunk(0, 0, 0, e)
                feed.at = up
                with dve.Fori(0, HALF // 2) as i:
                    for p in range(2):
                        chunk(i, p, 2 * i + (p + 1), e1)
                feed.at = down
                with dve.Fori(0, 2) as i:
                    for j in range(4):
                        split.wait_done(dve, i, j, e2)
                        residual(k, dve, tokens, gate_at, 4 * i + j, j % 2).then_inc(y_free, 1)
            if next_c:
                side.at = side_base + 3
                sm.vector(dve, next_bias, (1, 1))
            feed.at, side.at = base, side_base
        feed.at = base + 6
        if next_c:
            side.at = side_base + 4
    if next_c:
        k.mod, k.mod_next = k.mod_next, k.mod


def constants(k, st, *names):
    return [st.sb(n, list(k.io[n].shape)) for n in names]


class Attention:

    def __init__(self, k, st, units, subs, scale, prepare=None, sinks=None, lam=None):
        self.k, self.st, self.units, self.subs, self.scale = k, st, units, subs, scale
        self.prepare, self.sinks, self.lam = prepare, sinks, lam
        self.probs = st.sb("probs", [P, 2, TOK])
        self.turned = st.sb("turned", [P, 2, TOK])
        self.scores = st.sb("scores", [P, 2, TOK]) if prepare else None
        self.mixed = st.sb("mixed", [P, TOK]) if subs == 2 else None
        self.negmax = st.sb("negmax", [P, 2])
        self.rowmax = st.sb("rowmax", [P, 2])
        self.sums = st.sb("sums", [P, 2])
        self.sinkexp = st.sb("sinkexp", [P, 2])
        self.recip = st.sb("recip", [P, 2])
        self.scores_ready = st.sem("scores_ready")
        self.max_ready = st.sem("max_ready")
        self.exp_done = st.sem("exp_done")
        self.probs_ready = st.sem("probs_ready")
        self.turn_done = st.sem("turn_done")
        self.turned_ready = st.sem("turned_ready")
        self.values_done = st.sem("values_done")

    def slot(self, u, s):
        return s if self.subs == 2 else u % 2

    def tensor(self, pe, i, lo, hi, between=None):
        U = len(self.units)
        ahead = 2 if self.subs == 1 else 1

        def scores(u):
            for s, products in enumerate(self.units[u]["scores"]):
                if self.subs == 2 and u > 0:
                    pe.wait_ge(self.exp_done, i * U + u)
                if self.subs == 1 and u > 1:
                    pe.wait_ge(self.max_ready, i * U + u - 1)
                for q, key, c, n in products:
                    mm = pe.matmul(region(self.k, 1 + self.slot(u, s))[:, c:c + n], q, key, start=True, stop=True)
                mm.then_inc(self.scores_ready, 1)

        def turn(u):
            pe.wait_ge(self.probs_ready, i * U + u + 1)
            if u > 0:
                pe.wait_ge(self.turned_ready, i * U + u)
            src = self.mixed[:, :] if self.subs == 2 else self.probs[:, u % 2, :]
            for b in range(self.units[u]["n"] // P):
                mm = pe.transpose(region(self.k, 3)[:, b * P:(b + 1) * P], src[:, b * P:(b + 1) * P], self.k.ident[:, :])
            mm.then_inc(self.turn_done, 1)

        def values(u):
            pe.wait_ge(self.turned_ready, i * U + u + 1)
            v = self.units[u]["values"]
            for b, val in enumerate(v):
                mm = pe.matmul(self.units[u]["out"], val, self.turned[:, u % 2, b * P:(b + 1) * P],
                               start=b == 0, stop=b == len(v) - 1)
            mm.then_inc(self.values_done, 1)

        for u in range(lo, lo + ahead):
            scores(u)
        for u in range(lo, hi):
            if u + ahead < hi:
                scores(u + ahead)
            if between:
                between(u)
            turn(u)
            if u > lo:
                values(u - 1)
        values(hi - 1)

    def vector(self, dve, i, lo, hi, between=None):
        U, S = len(self.units), self.subs

        def maxima(u):
            n = self.units[u]["n"]
            if S == 1 and u > 1:
                dve.wait_ge(self.exp_done, i * U + u - 1)
            for s in range(S):
                r = self.slot(u, s)
                dve.wait_ge(self.scores_ready, i * (U * S) + u * S + s + 1)
                src = region(self.k, 1 + r, n)
                if self.prepare:
                    self.prepare(dve, self.units[u], src, self.scores[:, r, 0:n])
                    dve.drain()
                    src = self.scores[:, r, 0:n]
                dve.tensor_reduce(self.rowmax[:, r:r + 1], src, AX.X, ALU.max)
                dve.drain()
                if self.sinks is not None:
                    sink = self.sinks[:, self.units[u]["sink"]:self.units[u]["sink"] + 1]
                    dve.tensor_scalar(self.rowmax[:, r:r + 1], self.rowmax[:, r:r + 1], self.scale, sink, ALU.mult, ALU.max)
                    dve.drain()
                    dve.tensor_scalar(self.negmax[:, r:r + 1], self.rowmax[:, r:r + 1], -1.0, None, ALU.mult).then_inc(self.max_ready, 1)
                else:
                    dve.tensor_scalar(self.negmax[:, r:r + 1], self.rowmax[:, r:r + 1], -self.scale, None, ALU.mult).then_inc(self.max_ready, 1)

        def finish(u):
            n = self.units[u]["n"]
            dve.wait_ge(self.exp_done, i * U + u + 1)
            if S == 2:
                dve.reciprocal(self.recip[:, :], self.sums[:, :])
                dve.drain()
                dve.tensor_tensor(self.recip[:, 1:2], self.recip[:, 1:2], self.lam, ALU.mult)
                dve.drain()
                if u > 0:
                    dve.wait_ge(self.turn_done, i * U + u)
                dve.tensor_scalar(self.probs[:, 1, 0:n], self.probs[:, 1, 0:n], self.recip[:, 1:2], None, ALU.mult)
                dve.drain()
                dve.scalar_tensor_tensor(out=self.mixed[:, 0:n], in0=self.probs[:, 0, 0:n], scalar=self.recip[:, 0:1],
                                         in1=self.probs[:, 1, 0:n], op0=ALU.mult, op1=ALU.subtract).then_inc(self.probs_ready, 1)
            else:
                r = u % 2
                total = self.sums[:, r:r + 1]
                if self.sinks is not None:
                    dve.tensor_tensor(total, total, self.sinkexp[:, r:r + 1], ALU.add)
                    dve.drain()
                dve.reciprocal(self.recip[:, r:r + 1], total)
                dve.drain()
                dve.tensor_scalar(self.probs[:, r, 0:n], self.probs[:, r, 0:n], self.recip[:, r:r + 1], None,
                                  ALU.mult).then_inc(self.probs_ready, 1)

        for u in range(lo, hi):
            maxima(u)
            if u > lo:
                finish(u - 1)
            if between:
                between(u)
        finish(hi - 1)

    def scalar(self, act, i, lo, hi, between=None):
        U, S = len(self.units), self.subs

        def exps(u):
            n = self.units[u]["n"]
            if S == 2 and u > 0:
                act.wait_ge(self.probs_ready, i * U + u)
            if S == 1 and u > 1:
                act.wait_ge(self.turn_done, i * U + u - 1)
            for s in range(S):
                r = self.slot(u, s)
                act.wait_ge(self.max_ready, i * (U * S) + u * S + s + 1)
                if self.sinks is not None:
                    sink = self.sinks[:, self.units[u]["sink"]:self.units[u]["sink"] + 1]
                    act.activation(self.sinkexp[:, r:r + 1], sink, ACT.Exp, bias=self.negmax[:, r:r + 1])
                src = self.scores[:, r, 0:n] if self.prepare else region(self.k, 1 + r, n)
                ins = act.activation(self.probs[:, r, 0:n], src, ACT.Exp, bias=self.negmax[:, r:r + 1], scale=self.scale,
                                     accum_out=self.sums[:, r:r + 1])
            ins.then_inc(self.exp_done, 1)

        def copy(u):
            n = self.units[u]["n"]
            act.wait_ge(self.turn_done, i * U + u + 1)
            if u > 1:
                act.wait_ge(self.values_done, i * U + u - 1)
            act.activation(self.turned[:, u % 2, 0:n], region(self.k, 3, n), ACT.Copy).then_inc(self.turned_ready, 1)

        for u in range(lo, hi):
            exps(u)
            if u > lo:
                copy(u - 1)
            if between:
                between(u)
        copy(hi - 1)


def gating_mlp(k):
    nc, feed = k.nc, k.feed
    T = TOK // P
    with Stage(k, "gating") as st:
        split = Split(k, st, 2)
        u = st.sb("u", [P, 2, TOK])
        v = st.sb("v", [P, 2, T, P])
        wst = st.sb("wst", [P, 4, P])
        rows = st.sb("rows", [P, NROWS])
        stats = st.sb("stats", [P, 4, T, 6])
        mv = st.sb("mv", [P, 4, T, 2])
        rstd = st.sb("rstd", [P, 4, T])
        landed = st.sem("constants_landed")
        u_ready, v_ready, var_ready, root_ready = st.sem("u_ready"), st.sem("v_ready"), st.sem("var_ready"), st.sem("root_ready")
        normed, mixed, done = st.sem("normed"), st.sem("mixed"), st.sem("gated")

        @st.block.sync
        def _(sp):
            sp.dma_start(wst[:, :, :], k.io["sgu_wt"]).then_inc(landed, 16)
            sp.dma_start(rows[:, :], k.io["rows"].partition_broadcast(P)).then_inc(landed, 16)
            feed.program(sp)

        @st.block.gpsimd
        def _(pool):
            st.clear_last(pool)
            for g in range(4):
                for j in range(2):
                    split.write_low(pool, g // 2, 2 * (g % 2) + j)

        @st.block.tensor
        def _(pe):
            def mix(g):
                b = g % 2
                pe.wait_ge(normed, g + 1)
                for t in range(T):
                    mm = pe.matmul(region(k, 2 * b + 1)[:, t * P:(t + 1) * P], v[:, g % 2, t, :], wst[:, g, :], start=True, stop=True)
                mm.then_inc(mixed, 1)

            split.start(pe)
            pe.wait_ge(landed, 32)
            for g in range(4):
                i, b = divmod(g, 2)
                if g >= 2:
                    pe.wait_ge(u_ready, g - 1)
                    pe.wait_ge(done, g - 1)
                tile_products(k, pe, i, 2 * b, region(k, 2 * b), k.hn, TOK, split)
                token_products(k, pe, i, 2 * b + 1, region(k, 2 * b + 1), k.hn, TOK, split)
                if g > 0:
                    mix(g - 1)
            mix(3)

        @st.block.scalar
        def _(act):
            for j in range(2):
                split.write_high(act, 0, j)
            for g in range(4):
                i, b = divmod(g, 2)
                if g >= 2:
                    act.wait_ge(done, g - 1)
                split.wait_done(act, i, 2 * b)
                if g < 3:
                    split.write_high(act, (g + 1) // 2, 2 * ((g + 1) % 2))
                act.activation(u[:, g % 2, :], region(k, 2 * b), ACT.Gelu).then_inc(u_ready, 1)
                split.wait_done(act, i, 2 * b + 1)
                if g < 3:
                    split.write_high(act, (g + 1) // 2, 2 * ((g + 1) % 2) + 1)
                act.activation(v[:, g % 2, :, :].rearrange("p t c -> p (t c)"), region(k, 2 * b + 1), ACT.Gelu).then_inc(v_ready, 1)
                act.wait_ge(var_ready, g + 1)
                act.activation(rstd[:, g, :], mv[:, g, :, 1], ACT.Sqrt, bias=k.eps[:, 0:1]).then_inc(root_ready, 1)

        @st.block.vector
        def _(dve):
            for g in range(4):
                b = g % 2
                dve.wait_ge(v_ready, g + 1)
                for t in range(T):
                    dve.bn_stats(stats[:, g, t, :], v[:, g % 2, t, :])
                dve.drain()
                for t in range(T):
                    ins = dve.bn_aggr(mv[:, g, t, :], stats[:, g, t, :])
                ins.then_inc(var_ready, 1)
                dve.wait_ge(root_ready, g + 1)
                dve.reciprocal(rstd[:, g, :], rstd[:, g, :])
                dve.drain()
                for t in range(T):
                    ins = dve.tensor_scalar(v[:, g % 2, t, :], v[:, g % 2, t, :], mv[:, g, t, 0:1], rstd[:, g, t:t + 1], ALU.subtract, ALU.mult)
                ins.then_inc(normed, 1)
                dve.wait_ge(mixed, g + 1)
                bias = rows[:, ROWCOL["sgu_b"] + g * P:ROWCOL["sgu_b"] + (g + 1) * P]
                mo = k.mo[:, g, :]
                dve.tensor_tensor(mo.rearrange("p (t c) -> p t c", t=T), region(k, 2 * b + 1).rearrange("p (t c) -> p t c", t=T),
                                  bias.unsqueeze(1).to_broadcast([P, T, P]), ALU.add)
                dve.drain()
                dve.wait_ge(u_ready, g + 1)
                dve.tensor_tensor(mo, mo, u[:, g % 2, :], ALU.mult).then_inc(done, 1)
    feed.at += 1


def rope(k, dve, x, rotated, cos, sin, tmp):
    dve.tensor_tensor(tmp, rotated, sin, ALU.mult)
    dve.tensor_tensor(x, x, cos, ALU.mult)
    dve.drain()
    return dve.tensor_tensor(x, x, tmp, ALU.add)


def diff_attention(k):
    nc, feed = k.nc, k.feed
    T = TOK // P
    with Stage(k, "diff") as st:
        split = Split(k, st, 3)
        q, key, v = st.sb("q", [P, TOK]), st.sb("key", [P, TOK]), st.sb("v", [P, T, P])
        tmp = st.sb("tmp", [P, LAT])
        rot, cos, sin = constants(k, st, "rot", "cos", "sin")
        rows = st.sb("rows", [P, NROWS])
        dots, lam, gain = st.sb("dots", [P, 2]), st.sb("lam", [P, 1]), st.sb("gain", [P, 1])
        junk = st.sb("junk", [P, HEAD])
        rstd, sq = st.sb("rstd", [P, TOK]), st.sb("sq", [P, TOK])
        landed, dots_ready, lam_exp = st.sem("constants_landed"), st.sem("dots_ready"), st.sem("lam_exp")
        copied, rotated, roped = st.sem("copied"), st.sem("rotated"), st.sem("roped")
        squared, summed, var_ready, root_ready, head_done = (st.sem("squared"), st.sem("summed"), st.sem("var_ready"),
                                                             st.sem("root_ready"), st.sem("head_done"))
        units = []
        for t in range(T):
            keys = [(0, 512), (512, 256)] if t < LAT // P else [(512, 256)]
            off = keys[0][0]
            units.append(dict(
                n=TOK - off, out=region(k, 0)[:, t * P:(t + 1) * P], values=[v[:, b, :] for b in range(off // P, T)],
                scores=[[(q[64 * s:64 * s + 64, t * P:(t + 1) * P], key[64 * s:64 * s + 64, a:a + n], a - off, n)
                         for a, n in keys] for s in range(2)]))
        att = Attention(k, st, units, 2, SCALE, lam=lam[:, :])
        U = len(units)

        @st.block.sync
        def _(sp):
            for dst, name in ((rot, "rot"), (cos, "cos"), (sin, "sin")):
                sp.dma_start(dst[:, :], k.io[name]).then_inc(landed, 16)
            sp.dma_start(rows[:, :], k.io["rows"].partition_broadcast(P)).then_inc(landed, 16)
            feed.program(sp)

        @st.block.gpsimd
        def _(pool):
            st.clear_last(pool)
            with pool.Fori(0, 4) as i:
                for j in range(3):
                    split.write_low(pool, i, j)

        @st.block.tensor
        def _(pe):
            split.start(pe)
            pe.wait_ge(landed, 64)
            with pe.Fori(0, 4) as i:
                pe.wait_ge(head_done, i + 1)
                tile_products(k, pe, i, 0, region(k, 0), k.hn, TOK, split)
                tile_products(k, pe, i, 1, region(k, 1), k.hn, TOK, split)
                token_products(k, pe, i, 2, region(k, 2), k.hn, TOK, split)
                pe.wait_ge(copied, 3 * i + 1)
                pe.matmul(region(k, 3, LAT), rot[:, :], q[:, 0:LAT], start=True, stop=True).then_inc(rotated, 1)
                pe.wait_ge(copied, 3 * i + 2)
                pe.matmul(region(k, 0, LAT), rot[:, :], key[:, 0:LAT], start=True, stop=True).then_inc(rotated, 1)
                pe.wait_ge(copied, 3 * i + 3)
                pe.wait_ge(roped, 2 * i + 2)
                att.tensor(pe, i, 0, U)
                pe.wait_ge(squared, i + 1)
                for a, b, _ in spans(TOK):
                    mm = pe.matmul(region(k, 1)[:, a:b], k.ones[:, :], sq[:, a:b], start=True, stop=True)
                mm.then_inc(summed, 1)

        @st.block.scalar
        def _(act):
            act.wait_ge(dots_ready, 1)
            act.activation(dots[:, :], dots[:, :], ACT.Exp).then_inc(lam_exp, 1)
            with act.Fori(0, 4) as i:
                for j in range(3):
                    split.write_high(act, i, j)
                for j, dst in enumerate((q[:, :], key[:, :], v[:, :, :].rearrange("p t c -> p (t c)"))):
                    split.wait_done(act, i, j)
                    act.activation(dst, region(k, j), ACT.Copy).then_inc(copied, 1)
                att.scalar(act, i, 0, U)
                act.wait_ge(att.values_done, U * i + U)
                act.activation(sq[:, :], region(k, 0), ACT.Square).then_inc(squared, 1)
                act.wait_ge(var_ready, i + 1)
                act.activation(rstd[:, :], rstd[:, :], ACT.Sqrt).then_inc(root_ready, 1)

        @st.block.vector
        def _(dve):
            dve.sem_inc(head_done, 1)
            dve.wait_ge(landed, 64)
            for j in range(2):
                ins = dve.tensor_tensor_reduce(junk[:, :], rows[:, 128 * j:128 * j + 64], rows[:, 128 * j + 64:128 * j + 128],
                                               1.0, 0.0, ALU.mult, ALU.add, dots[:, j:j + 1])
                dve.drain()
            dve.tensor_scalar(gain[:, :], col(k, "subln"), 1.0 - LAM_INIT, None, ALU.mult).then_inc(dots_ready, 1)
            dve.wait_ge(lam_exp, 1)
            dve.scalar_tensor_tensor(out=lam[:, :], in0=dots[:, 0:1], scalar=LAM_INIT, in1=dots[:, 1:2],
                                     op0=ALU.add, op1=ALU.subtract)
            dve.drain()
            with dve.Fori(0, 4) as i:
                for j, (x, r) in enumerate(((q, 3), (key, 0))):
                    dve.wait_ge(rotated, 2 * i + j + 1)
                    rope(k, dve, x[:, 0:LAT], region(k, r, LAT), cos[:, :], sin[:, :], tmp[:, :]).then_inc(roped, 1)
                    dve.drain()
                att.vector(dve, i, 0, U)
                dve.wait_ge(summed, i + 1)
                dve.tensor_scalar(rstd[:, :], region(k, 1), 1.0 / P, EPS, ALU.mult, ALU.add).then_inc(var_ready, 1)
                dve.wait_ge(root_ready, i + 1)
                dve.reciprocal(rstd[:, :], rstd[:, :])
                dve.drain()
                dve.scalar_tensor_tensor(out=k.mo[:, bass.ds(i + 4, 1), :].rearrange("p a t -> p (a t)"), in0=region(k, 0),
                                         scalar=gain[:, :], in1=rstd[:, :], op0=ALU.mult, op1=ALU.mult).then_inc(head_done, 1)
    feed.at += 1


def window_attention(k):
    nc, feed = k.nc, k.feed
    T = TOK // P
    with Stage(k, "window") as st:
        split = Split(k, st, 3)
        q, key, v = st.sb("q", [P, LAT]), st.sb("key", [P, TOK]), st.sb("v", [P, T, P])
        tmp = st.sb("tmp", [P, LAT])
        rot, cos, sin, mask = constants(k, st, "rot", "cos", "sin", "window_mask")
        rows, sinks = st.sb("rows", [P, NROWS]), st.sb("sinks", [P, 8])
        landed = st.sem("constants_landed")
        kv_copied, q_copied, rotated, roped, chunk_done = (st.sem("kv_copied"), st.sem("q_copied"), st.sem("rotated"),
                                                           st.sem("roped"), st.sem("chunk_done"))
        units = []
        for j in range(4):
            for s in range(2):
                for t in range(4):
                    qt = q[64 * s:64 * s + 64, t * P:(t + 1) * P]
                    kt = key[64 * s:64 * s + 64, :]
                    left = P if t > 0 else 0
                    products = [(qt, kt[:, t * P - left:(t + 1) * P], 0, left + P), (qt, kt[:, LAT:TOK], left + P, CTX)]
                    tiles = ([t - 1] if left else []) + [t, 4, 5]
                    n = left + P + CTX
                    if t < 3:
                        products.append((qt, kt[:, (t + 1) * P:(t + 2) * P], n, P))
                        tiles.append(t + 1)
                        n += P
                    units.append(dict(n=n, scores=[products], values=[v[:, b, 64 * s:64 * s + 64] for b in tiles],
                                      out=region(k, 0)[64 * s:64 * s + 64, t * P:(t + 1) * P], sink=4 * s + j,
                                      mask=0 if left else P))

        def prepare(dve, unit, src, dst):
            dve.tensor_tensor(dst, src, mask[:, unit["mask"]:unit["mask"] + unit["n"]], ALU.add)

        att = Attention(k, st, units, 1, SCALE, prepare=prepare, sinks=sinks)
        U = len(units)

        @st.block.sync
        def _(sp):
            for dst, name in ((rot, "rot"), (cos, "cos"), (sin, "sin"), (mask, "window_mask")):
                sp.dma_start(dst[:, :], k.io[name]).then_inc(landed, 16)
            sp.dma_start(rows[:, :], k.io["rows"].partition_broadcast(P)).then_inc(landed, 16)
            feed.program(sp)

        @st.block.gpsimd
        def _(pool):
            st.clear_last(pool)
            with pool.Fori(0, 2) as i:
                for j in range(6):
                    split.write_low(pool, i, j)

        @st.block.tensor
        def _(pe):
            split.start(pe)
            pe.wait_ge(landed, 80)
            with pe.Fori(0, 2) as i:
                pe.wait_ge(chunk_done, 4 * i + 1)
                tile_products(k, pe, i, 0, region(k, 1), k.hn, TOK, split)
                token_products(k, pe, i, 1, region(k, 2), k.hn, TOK, split)
                pe.wait_ge(kv_copied, 2 * i + 1)
                pe.matmul(region(k, 3, LAT), rot[:, :], key[:, 0:LAT], start=True, stop=True).then_inc(rotated, 1)
                for j in range(4):
                    pe.wait_ge(chunk_done, 4 * i + j + 1)
                    tile_products(k, pe, i, 2 + j, region(k, 0), k.hn, LAT, split)
                    pe.wait_ge(q_copied, 4 * i + j + 1)
                    pe.wait_ge(roped, 5 * i + j + 1)
                    pe.matmul(region(k, 3, LAT), rot[:, :], q[:, 0:LAT], start=True, stop=True).then_inc(rotated, 1)
                    pe.wait_ge(roped, 5 * i + j + 2)
                    pe.wait_ge(kv_copied, 2 * i + 2)
                    att.tensor(pe, i, 8 * j, 8 * j + 8)

        @st.block.scalar
        def _(act):
            with act.Fori(0, 2) as i:
                for j in range(3):
                    split.write_high(act, i, j)
                split.wait_done(act, i, 0)
                act.activation(key[:, :], region(k, 1), ACT.Copy).then_inc(kv_copied, 1)
                split.wait_done(act, i, 1)
                act.activation(v[:, :, :].rearrange("p t c -> p (t c)"), region(k, 2), ACT.Copy).then_inc(kv_copied, 1)
                for j in range(4):
                    if j < 3:
                        split.write_high(act, i, 3 + j)
                    split.wait_done(act, i, 2 + j)
                    act.activation(q[:, :], region(k, 0, LAT), ACT.Copy).then_inc(q_copied, 1)
                    att.scalar(act, i, 8 * j, 8 * j + 8)

        @st.block.vector
        def _(dve):
            dve.sem_inc(chunk_done, 1)
            dve.wait_ge(landed, 80)
            with dve.Fori(0, 2) as i:
                dve.wait_ge(rotated, 5 * i + 1)
                rope(k, dve, key[:, 0:LAT], region(k, 3, LAT), cos[:, :], sin[:, :], tmp[:, :]).then_inc(roped, 1)
                dve.tensor_copy(sinks[:, :], rows[:, bass.ds(8 * i + ROWCOL["sink"], 8)])
                dve.drain()
                for j in range(4):
                    dve.wait_ge(rotated, 5 * i + j + 2)
                    rope(k, dve, q[:, 0:LAT], region(k, 3, LAT), cos[:, :], sin[:, :], tmp[:, :]).then_inc(roped, 1)
                    dve.drain()
                    att.vector(dve, i, 8 * j, 8 * j + 8)
                    dve.wait_ge(att.values_done, i * U + 8 * j + 8)
                    dve.tensor_copy(k.mo[:, bass.ds(4 * i + j, 1), 0:LAT].rearrange("p a t -> p (a t)"),
                                    region(k, 0, LAT)).then_inc(chunk_done, 1)
    feed.at += 1


def neighbourhood_attention(k):
    nc, feed = k.nc, k.feed
    T = TOK // P
    NB = (DR - 1) * GRID_W
    with Stage(k, "neighbour") as st:
        split = Split(k, st, 3)
        q, key, v = st.sb("q", [P, LAT]), st.sb("key", [P, TOK]), st.sb("v", [P, T, P])
        mask, = constants(k, st, "column_mask")
        bias = st.sb("bias", [P, 2, NB])
        landed, bias_landed, bias_ready, bias_free = (st.sem("mask_landed"), k.bias_landed,
                                                      st.sem("bias_ready"), st.sem("bias_free"))
        copied, pair_done = st.sem("copied"), st.sem("pair_done")
        units = []
        for s in range(2):
            for t in range(4):
                qt = q[64 * s:64 * s + 64, t * P:(t + 1) * P]
                kt = key[64 * s:64 * s + 64, :]
                units.append(dict(n=TOK, scores=[[(qt, kt[:, 0:LAT], 0, LAT), (qt, kt[:, LAT:TOK], LAT, CTX)]],
                                  values=[v[:, b, 64 * s:64 * s + 64] for b in range(T)],
                                  out=region(k, 0)[64 * s:64 * s + 64, t * P:(t + 1) * P],
                                  bias=bias[:, s, (6 - 2 * t) * GRID_W:(6 - 2 * t) * GRID_W + LAT]))

        def prepare(dve, unit, src, dst):
            dve.scalar_tensor_tensor(out=dst[:, 0:LAT], in0=src[:, 0:LAT], scalar=SCALE, in1=unit["bias"],
                                     op0=ALU.mult, op1=ALU.add)
            dve.tensor_scalar(dst[:, LAT:TOK], src[:, LAT:TOK], SCALE, None, ALU.mult)

        att = Attention(k, st, units, 1, 1.0, prepare=prepare)
        U = len(units)

        @st.block.sync
        def _(sp):
            sp.dma_start(mask[:, :], k.io["column_mask"]).then_inc(landed, 16)
            feed.program(sp)

        @st.block.gpsimd
        def _(pool):
            st.clear_last(pool)
            pool.wait_ge(k.bias_sem, 16 * (2 + GRID_W))
            with pool.Fori(0, 8) as i:
                for j in range(3):
                    split.write_low(pool, i, j)
                pool.wait_ge(bias_free, i + 1)
                for s in range(2):
                    for half in range(2):
                        src = k.toeplitz[bass.ds(2 * i + s, 1), :, 1 - half:DR - half, :]
                        pool.dma_start(bias[64 * half:64 * half + 64, s, :],
                                       src.rearrange("a q r c -> (a q) (r c)")).then_inc(bias_landed[2 * s + half], 16)

        @st.block.tensor
        def _(pe):
            split.start(pe)
            with pe.Fori(0, 8) as i:
                pe.wait_ge(pair_done, i + 1)
                tile_products(k, pe, i, 0, region(k, 0), k.hn, LAT, split)
                tile_products(k, pe, i, 1, region(k, 1), k.hn, TOK, split)
                token_products(k, pe, i, 2, region(k, 2), k.hn, TOK, split)
                pe.wait_ge(copied, 3 * i + 3)
                att.tensor(pe, i, 0, U)

        @st.block.scalar
        def _(act):
            with act.Fori(0, 8) as i:
                for j in range(3):
                    split.write_high(act, i, j)
                for j, (dst, n) in enumerate(((q[:, :], LAT), (key[:, :], TOK), (v[:, :, :].rearrange("p t c -> p (t c)"), TOK))):
                    split.wait_done(act, i, j)
                    act.activation(dst, region(k, j, n), ACT.Copy).then_inc(copied, 1)
                att.scalar(act, i, 0, U)

        @st.block.vector
        def _(dve):
            dve.sem_inc(pair_done, 1)
            dve.sem_inc(bias_free, 1)
            dve.wait_ge(landed, 16)
            with dve.Fori(0, 8) as i:
                for s in range(4):
                    dve.wait_ge(bias_landed[s], 16 * i + 16)
                for s in range(2):
                    b3 = bias[:, s, :].rearrange("p (r c) -> p r c", c=GRID_W)
                    dve.tensor_tensor(b3, b3, mask[:, :].unsqueeze(1).to_broadcast([P, DR - 1, GRID_W]), ALU.add)
                dve.drain()
                att.vector(dve, i, 0, U)
                dve.sem_inc(bias_free, 1)
                dve.wait_ge(att.values_done, i * U + U)
                dve.tensor_copy(k.mo[:, bass.ds(i, 1), 0:LAT].rearrange("p a t -> p (a t)"),
                                region(k, 0, LAT)).then_inc(pair_done, 1)
    feed.at += 1


def shift_mix(dve, dst, raw, own, before, after):
    for op in range(3):
        for a, n, off in ((0, LAT, 1), (LAT, CTX, LAT + 2)):
            d = dst[:, a:a + n]
            if op == 0:
                ins = dve.tensor_scalar(d, raw[:, off:off + n], own, None, ALU.mult)
            else:
                o = off - 1 if op == 1 else off + 1
                ins = dve.scalar_tensor_tensor(out=d, in0=raw[:, o:o + n], scalar=before if op == 1 else after, in1=d,
                                               op0=ALU.mult, op1=ALU.add)
        if op < 2:
            dve.drain()
    return ins


RAWW = TOK + 3
POOLW = 8 + LAT + 8 + CTX + 8


def rwkv(k):
    keep = k.tmp
    new = lambda name, n: keep.enter_context(k.nc.sbuf_tensor(f"rwkv_{name}", [P, n], F32))
    wd, ad, gd = new("wd", TOK), new("ad", TOK), new("gd", TOK)
    with ExitStack() as k.tmp:
        lora_and_pooling(k, wd, ad, gd)
    with ExitStack() as k.tmp:
        rwkv_pairs(k, wd, ad, gd)


def lora_and_pooling(k, wd, ad, gd):
    feed = k.feed
    with Stage(k, "lora") as st:
        raw = st.sb("raw", [P, 3, RAWW])
        own = st.sb("own", [P, 3])
        pads = [st.sb(f"pooled{j}", [P, 2, POOLW]) for j in range(5)]
        pooled = st.sb("pooled", [P, 2, TOK])
        invc, poolw = constants(k, st, "pool_inv", "pool_w")
        zeroed, copied, mixed, landed, pooled_ready, products = (st.sem("zeroed"), st.sem("copied"), st.sem("mixed"),
                                                                 st.sem("landed"), st.sem("pooled_ready"), st.sem("pool_products"))
        seqs = ((0, LAT, 8), (LAT, CTX, 16 + LAT))

        @st.block.sync
        def _(sp):
            sp.dma_start(invc[:, :, :], k.io["pool_inv"]).then_inc(landed, 16)
            sp.dma_start(poolw[:, :, :], k.io["pool_w"]).then_inc(landed, 16)
            feed.program(sp)

        @st.block.gpsimd
        def _(pool):
            st.clear_last(pool)
            pool.memset(raw[:, :, :], 0.0)
            pool.memset(pads[0][:, :, :], 0.0).then_inc(zeroed, 1)

        @st.block.tensor
        def _(pe):
            for j in range(4):
                tile_products(k, pe, 0, j, region(k, j), k.hn, TOK)
            pe.wait_ge(copied, 1)
            tile_products(k, pe, 0, 4, region(k, 0), k.hn, TOK)
            pe.wait_ge(landed, 32)
            pe.wait_ge(pooled_ready, 1)
            pe.wait_ge(copied, 4)
            for j in range(2):
                for h in range(2):
                    for a, b, _ in spans(TOK):
                        mm = pe.matmul(region(k, 2 + j)[64 * h:64 * h + 64, a:b], poolw[64 * h:64 * h + 64, j, :],
                                       pooled[64 * h:64 * h + 64, j, a:b], start=True, stop=True)
            mm.then_inc(products, 1)

        @st.block.scalar
        def _(act):
            act.wait_ge(zeroed, 1)
            for j in range(5):
                feed.wait_done(act, 0, j)
                for a, n, off in (((0, LAT, 1), (LAT, CTX, LAT + 2)) if j < 3 else seqs):
                    dst = raw[:, j, off:off + n] if j < 3 else pads[0][:, j - 3, off:off + n]
                    ins = act.activation(dst, region(k, j % 4)[:, a:a + n], ACT.Copy)
                ins.then_inc(copied, 1)
            act.wait_ge(mixed, 3)
            act.activation(wd[:, :], wd[:, :], ACT.Tanh)
            act.activation(gd[:, :], gd[:, :], ACT.Sigmoid)
            act.wait_ge(products, 1)
            for j in range(2):
                act.activation(k.mo[:, 6 + j, :], region(k, 2 + j), ACT.Identity, scale=col(k, "pool_scale", j))

        @st.block.vector
        def _(dve):
            mu = lambda d, j: col(k, "mu_lora", 3 * d + j)
            dve.tensor_tensor(own[:, :], col(k, "mu_lora", 0, 3), col(k, "mu_lora", 3, 3), ALU.add)
            dve.drain()
            dve.tensor_scalar(own[:, :], own[:, :], -1.0, 1.0, ALU.mult, ALU.add)
            dve.drain()
            for j, dst in enumerate((wd, ad, gd)):
                dve.wait_ge(copied, j + 1)
                shift_mix(dve, dst, raw[:, j, :], own[:, j:j + 1], mu(0, j), mu(1, j)).then_inc(mixed, 1)
            dve.wait_ge(copied, 5)
            for n, (left, right) in enumerate(((1, 0), (1, 1), (2, 2), (4, 4))):
                a, b = pads[n], pads[n + 1]
                if n == 0:
                    dve.memset(b[:, :, 0:1], 0.0)
                edge = (1, 2, 4, 8)[n]
                m = POOLW - 2 * edge
                dve.tensor_tensor(b[:, :, edge:edge + m], a[:, :, edge - left:edge - left + m],
                                  a[:, :, edge + right:edge + right + m], ALU.add)
                dve.drain()
            dve.wait_ge(landed, 32)
            for a, n, off in seqs:
                for j in range(2):
                    for h in range(2):
                        dve.tensor_tensor(pooled[64 * h:64 * h + 64, j, a:a + n], pads[1 + 2 * j + h][64 * h:64 * h + 64, j, off:off + n],
                                          invc[64 * h:64 * h + 64, j, a:a + n], ALU.mult)
            dve.drain()
            for a, n, off in seqs:
                ins = dve.tensor_tensor(pooled[:, :, a:a + n], pooled[:, :, a:a + n], pads[0][:, :, off:off + n], ALU.subtract)
            ins.then_inc(pooled_ready, 1)
    feed.at += 1


def rwkv_pairs(k, wd, ad, gd):
    feed = k.feed
    GR = NCH // 2
    with Stage(k, "rwkv") as st:
        pw = st.sb("pair_weights", [P, NPAIR + 3 * P])
        bones, ident2, reset, lmask, levels = constants(k, st, "bones", "ident2", "reset", "tri_mask", "level_mask")
        own = st.sb("own", [P, 4])
        raw = st.sb("raw", [P, 3, RAWW])
        y, t1, t2 = (raw[:, j, 0:TOK] for j in range(3))
        r, kf, v, kk = (st.sb(n, [P, TOK]) for n in ("r", "kf", "v", "kk"))
        c, cm, em = (st.sb(n, [P, TOK]) for n in ("c", "cm", "em"))
        a, kd, kds = (st.sb(n, [P, TOK]) for n in ("a", "kd", "kds"))
        mid = st.sb("mid", [P, 2, NCH])
        factor = st.sb("factor", [P, NCH])
        qq = st.sb("qq", [P, NCH, 2, RC])
        bb, kb = st.sb("bb", [P, NCH, RC]), st.sb("kb", [P, NCH, RC])
        vt, bt, kt = (st.sb(n, [P, NCH, RC]) for n in ("vt", "bt", "kt"))
        lt = st.sb("lt", [P, NCH, 4, RC])
        x, xt, g = (st.sb(n, [P, NCH, RC]) for n in ("x", "xt", "g"))
        ct = st.sb("ct", [P, 2, NCH, RC])
        sm, sf = st.sb("sm", [P, 2, HEAD]), st.sb("sf", [P, HEAD])
        zs, sa = st.sb("zs", [P, HEAD]), st.sb("sa", [P, HEAD])
        par = {n: pw[:, i:i + 1] for n, i in PAIRCOL.items()}
        w2, a2, g2 = (pw[:, NPAIR + P * j:NPAIR + P * (j + 1)] for j in range(3))
        S = {n: st.sem(n) for n in (
            "constants", "padded", "pair_done", "copied", "kk_ready", "sq_ready", "norm_summed", "norm_root",
            "mix_done", "vtok_done", "vtok_copied", "lora_done", "sig_done", "cum_ready", "exp_ready", "qk_ready",
            "tok_done", "tok_copied", "l_done", "lt_ready", "ct_ready", "g_done", "g_copied", "u_done", "x_ready",
            "state_ready", "z_done", "z_copied", "sa_done", "sa_copied", "ds_done", "y_done", "y_read")}
        S.update({n: st.sem(n) for n in ("mean_done", "centred", "ysq_ready", "var_done", "var_ready", "var_root")})
        S["pair_landed"] = k.pair_landed
        halves = (0, 64)
        order = [list(range(8, 12)) + list(range(8)), list(range(11, 7, -1)) + list(range(7, -1, -1))]
        def flat(t):
            return t[:, :, :].rearrange("p n c -> p (n c)")

        def chunked(t):
            return t.rearrange("p (n c) -> p n c", c=RC)

        def hold(eng, sem, value):
            eng.wait_ge(sem, value)
            eng.nop(nofuse=True)

        @st.block.sync
        def _(sp):
            for dst, name in ((bones, "bones"), (ident2, "ident2"), (reset, "reset"), (lmask, "tri_mask"), (levels, "level_mask")):
                sp.dma_start(dst[:], k.io[name]).then_inc(S["constants"], 16)
            feed.program(sp)

        @st.block.gpsimd
        def _(pool):
            st.clear_last(pool)
            pool.wait_ge(S["constants"], 80)
            with pool.Fori(0, PAIRS) as i:
                hold(pool, S["pair_done"], i + 1)
                pool.memset(raw[:, :, 0:1], 0.0)
                pool.memset(raw[:, :, LAT + 1:LAT + 2], 0.0)
                pool.memset(raw[:, :, TOK + 2:TOK + 3], 0.0).then_inc(S["padded"], 1)
                pool.dma_start(pw[:, :], k.io["pair"][bass.ds(i, 1)].rearrange("a p w -> (a p) w")).then_inc(S["pair_landed"], 16)
                for d in range(2):
                    dd = 2 * i + d
                    for l in range(LEVELS):
                        for gr in range(2):
                            ns = slice(GR * gr, GR * gr + GR)
                            if l == 0:
                                pool.wait_ge(S["lt_ready"], 6 * dd + 3 * gr + 3)
                            if l >= 2:
                                pool.wait_ge(S["g_done"], 12 * dd + 2 * (l - 2) + gr + 1)
                            ins = pool.tensor_tensor(ct[:, l % 2, ns, :], lt[:, ns, 0, :],
                                                     levels[:, d, l, :].unsqueeze(1).to_broadcast([P, GR, RC]), ALU.mult)
                            if l == 0:
                                pool.drain()
                                ins = pool.tensor_tensor(xt[:, ns, :], ident2[:, :].unsqueeze(1).to_broadcast([P, GR, RC]),
                                                         ct[:, 0, ns, :], ALU.subtract)
                            ins.then_inc(S["ct_ready"], 1)

        @st.block.tensor
        def _(pe):
            def turned(dst, src):
                for n in range(NCH):
                    for h in halves:
                        mm = pe.matmul(dst[h:h + 64, n * RC:(n + 1) * RC], src[h:h + 64, n * RC:(n + 1) * RC], ident2[h:h + 64, :],
                                       start=True, stop=True)
                return mm

            def summed(dst, src):
                for a_, b_, _ in spans(TOK):
                    mm = pe.matmul(dst[:, a_:b_], bones[:, :], src[:, a_:b_], start=True, stop=True)
                return mm

            def invert(dd):
                hold(pe, S["tok_copied"], 2 * dd + 2)
                for l in range(LEVELS):
                    for gr in range(2):
                        hold(pe, S["ct_ready"], 12 * dd + 2 * l + gr + 1)
                        if l > 0:
                            hold(pe, S["x_ready"], 12 * dd + 2 * (l - 1) + gr + 1)
                        for n in range(GR * gr, GR * gr + GR):
                            for h in halves:
                                rhs = x[h:h + 64, n, :] if l else ident2[h:h + 64, :]
                                mm = pe.matmul(k.ps[h:h + 64, gr, (n - GR * gr) * RC:(n - GR * gr + 1) * RC],
                                               ct[h:h + 64, l % 2, n, :], rhs, start=True, stop=True)
                        mm.then_inc(S["g_done"], 1)
                    if l == 0:
                        continue
                    for gr in range(2):
                        hold(pe, S["g_copied"], 10 * dd + 2 * (l - 1) + gr + 1)
                        for n in range(GR * gr, GR * gr + GR):
                            cols = slice((n - GR * gr) * RC, (n - GR * gr + 1) * RC)
                            for h in halves:
                                if l < LEVELS - 1:
                                    pe.matmul(k.ps[h:h + 64, 2 + gr, cols], xt[h:h + 64, n, :], g[h:h + 64, n, :], start=True, stop=True)
                                mm = pe.matmul(k.ps[h:h + 64, 4 + gr, cols], g[h:h + 64, n, :], xt[h:h + 64, n, :], start=True, stop=True)
                        mm.then_inc(S["u_done"], 1)

            def recur(dd, d):
                hold(pe, S["x_ready"], 12 * dd + 12)
                Z, A, DS, Y = k.ps[:, 0, 0:64], k.ps[:, 1, 0:64], k.ps[:, 2, 0:64], region(k, 3)
                for s, n in enumerate(order[d]):
                    last = s == NCH - 1
                    state = sm[:, s % 2, :]
                    yc = Y[:, n * RC:(n + 1) * RC]
                    hold(pe, S["state_ready"], 12 * dd + s + 1)
                    for h in halves:
                        hs = slice(h, h + 64)
                        pe.matmul(Z[hs, :], qq[hs, n, 0, :], state[hs, :], start=True, stop=False)
                        mm = pe.matmul(Z[hs, :], lt[hs, n, 2, :], vt[hs, n, :], start=False, stop=True)
                    mm.then_inc(S["z_done"], 1)
                    for h in halves:
                        hs = slice(h, h + 64)
                        pe.matmul(yc[hs, :], state[hs, :], qq[hs, n, 1, :], start=True, stop=False)
                        pe.matmul(yc[hs, :], vt[hs, n, :], lt[hs, n, 3, :], start=False, stop=False)
                    hold(pe, S["z_copied"], 12 * dd + s + 1)
                    for h in halves:
                        hs = slice(h, h + 64)
                        mm = pe.matmul(A[hs, :], xt[hs, n, :], zs[hs, :], start=True, stop=True)
                    mm.then_inc(S["sa_done"], 1)
                    if not last:
                        for h in halves:
                            hs = slice(h, h + 64)
                            pe.matmul(DS[hs, :], kt[hs, n, :], vt[hs, n, :], start=True, stop=False)
                    hold(pe, S["sa_copied"], 12 * dd + s + 1)
                    if not last:
                        for h in halves:
                            hs = slice(h, h + 64)
                            mm = pe.matmul(DS[hs, :], bt[hs, n, :], sa[hs, :], start=False, stop=True)
                        mm.then_inc(S["ds_done"], 1)
                    for h in halves:
                        hs = slice(h, h + 64)
                        mm = pe.matmul(yc[hs, :], sa[hs, :], lt[hs, n, 1, :], start=False, stop=True)
                mm.then_inc(S["y_done"], 1)

            pe.wait_ge(S["constants"], 80)
            with pe.Fori(0, PAIRS) as i:
                hold(pe, S["pair_done"], i + 1)
                for j in range(3):
                    tile_products(k, pe, i, j, region(k, j), k.hn, TOK)
                hold(pe, S["sq_ready"], i + 1)
                summed(region(k, 1), t1).then_inc(S["norm_summed"], 1)
                hold(pe, S["mix_done"], i + 1)
                turned(region(k, 2), v).then_inc(S["vtok_done"], 1)
                for d in range(2):
                    dd = 2 * i + d
                    hold(pe, S["pair_landed"], 16 * i + 16)
                    hold(pe, S["y_read"], dd + 1)
                    ds_ = slice(64 * d, 64 * d + 64)
                    for reg, wt, src in ((3, w2, wd), (0, a2, ad)):
                        for a_, b_, _ in spans(TOK):
                            mm = pe.matmul(region(k, reg)[:, a_:b_], wt[ds_, :], src[ds_, a_:b_], start=True, stop=True)
                    mm.then_inc(S["lora_done"], 1)
                    hold(pe, S["qk_ready"], dd + 1)
                    turned(region(k, 0), flat(bb)).then_inc(S["tok_done"], 1)
                    hold(pe, S["vtok_copied"], i + 1)
                    for n in range(NCH):
                        for h in halves:
                            for j, w in enumerate((bb, kb)):
                                mm = pe.matmul(k.ps[h:h + 64, 2 + n // 2, (n % 2) * 256 + 128 * j:(n % 2) * 256 + 128 * j + 128],
                                               w[h:h + 64, n, :], qq[h:h + 64, n, :, :], start=True, stop=True)
                        if n % 2:
                            mm.then_inc(S["l_done"], 1)
                    hold(pe, S["tok_copied"], 2 * dd + 1)
                    turned(region(k, 0), flat(kb)).then_inc(S["tok_done"], 1)
                    hold(pe, S["lt_ready"], 6 * dd + 6)
                    invert(dd)
                    recur(dd, d)
                hold(pe, S["y_read"], 2 * i + 3)
                summed(region(k, 0), y).then_inc(S["mean_done"], 1)
                for a_, b_, _ in spans(TOK):
                    pe.matmul(region(k, 3)[:, a_:b_], g2, gd[:, a_:b_], start=True, stop=True)
                hold(pe, S["ysq_ready"], i + 1)
                summed(region(k, 1), t1)
                summed(region(k, 2), kds).then_inc(S["var_done"], 1)

        @st.block.scalar
        def _(act):
            with act.Fori(0, PAIRS) as i:
                act.wait_ge(S["padded"], i + 1)
                for j in range(3):
                    feed.wait_done(act, i, j)
                    act.activation(raw[:, j, 1:LAT + 1], region(k, j)[:, 0:LAT], ACT.Copy)
                    act.activation(raw[:, j, LAT + 2:TOK + 2], region(k, j)[:, LAT:TOK], ACT.Copy).then_inc(S["copied"], 1)
                act.wait_ge(S["kk_ready"], i + 1)
                act.activation(t1, kk[:, :], ACT.Square).then_inc(S["sq_ready"], 1)
                act.wait_ge(S["norm_summed"], i + 1)
                act.activation(t2, region(k, 1), ACT.Sqrt).then_inc(S["norm_root"], 1)
                act.wait_ge(S["vtok_done"], i + 1)
                act.activation(flat(vt), region(k, 2), ACT.Copy).then_inc(S["vtok_copied"], 1)
                for d in range(2):
                    dd = 2 * i + d
                    act.wait_ge(S["lora_done"], dd + 1)
                    act.activation(c[:, :], region(k, 3), ACT.Sigmoid, bias=par[f"w0_{d}"])
                    act.activation(a[:, :], region(k, 0), ACT.Sigmoid, bias=par[f"a0_{d}"]).then_inc(S["sig_done"], 1)
                    act.wait_ge(S["cum_ready"], dd + 1)
                    act.activation(mid[:, :, :], mid[:, :, :], ACT.Exp)
                    act.activation(em[:, :], em[:, :], ACT.Exp, scale=1.0 if d == 0 else -1.0)
                    act.activation(c[:, :], cm[:, :], ACT.Exp, scale=-1.0)
                    act.drain()
                    act.activation(cm[:, :], cm[:, :] if d == 0 else kd[:, :], ACT.Exp)
                    act.drain()
                    act.activation(zs[:, 0:1], mid[:, 0, 0:1], ACT.Copy).then_inc(S["exp_ready"], 1)
                    for j, dst in enumerate((bt, kt)):
                        act.wait_ge(S["tok_done"], 2 * dd + j + 1)
                        act.activation(flat(dst), region(k, 0), ACT.Copy).then_inc(S["tok_copied"], 1)
                    for l in range(1, LEVELS):
                        for gr in range(2):
                            if l >= 2:
                                act.wait_ge(S["u_done"], 10 * dd + 2 * (l - 2) + gr + 1)
                            act.wait_ge(S["g_done"], 12 * dd + 2 * l + gr + 1)
                            act.activation(g[:, GR * gr:GR * gr + GR, :].rearrange("p n c -> p (n c)"), k.ps[:, gr, 0:GR * RC],
                                           ACT.Copy).then_inc(S["g_copied"], 1)
                    for s in range(NCH):
                        act.wait_ge(S["z_done"], 12 * dd + s + 1)
                        act.activation(zs[:, :], k.ps[:, 0, 0:64], ACT.Copy).then_inc(S["z_copied"], 1)
                        act.wait_ge(S["sa_done"], 12 * dd + s + 1)
                        act.activation(sa[:, :], k.ps[:, 1, 0:64], ACT.Copy, scale=-1.0).then_inc(S["sa_copied"], 1)
                act.wait_ge(S["centred"], i + 1)
                act.activation(t1, y, ACT.Square).then_inc(S["ysq_ready"], 1)
                act.wait_ge(S["var_ready"], i + 1)
                act.activation(t2, t2, ACT.Sqrt).then_inc(S["var_root"], 1)

        @st.block.vector
        def _(dve):
            dve.sem_inc(S["pair_done"], 1)
            dve.sem_inc(S["y_read"], 1)
            dve.wait_ge(S["constants"], 80)
            with dve.Fori(0, PAIRS) as i:
                dve.wait_ge(S["pair_landed"], 16 * i + 16)
                dve.tensor_tensor(own[:, 0:3], pw[:, 0:3], pw[:, 3:6], ALU.add)
                dve.drain()
                dve.tensor_scalar(own[:, 0:3], own[:, 0:3], -1.0, 1.0, ALU.mult, ALU.add)
                dve.tensor_scalar(own[:, 3:4], par["k_a"], -1.0, 1.0, ALU.mult, ALU.add)
                dve.drain()
                for j, dst in enumerate((r, kf, v)):
                    dve.wait_ge(S["copied"], 3 * i + j + 1)
                    ins = shift_mix(dve, dst, raw[:, j, :], own[:, j:j + 1], pw[:, j:j + 1], pw[:, 3 + j:4 + j])
                ins.then_inc(S["mix_done"], 1)
                dve.tensor_scalar(kk[:, :], kf[:, :], par["k_k"], None, ALU.mult).then_inc(S["kk_ready"], 1)
                dve.wait_ge(S["norm_root"], i + 1)
                dve.tensor_scalar(t2, t2, 1e-12, None, ALU.max)
                dve.drain()
                dve.reciprocal(t2, t2)
                dve.drain()
                dve.tensor_tensor(kk[:, :], kk[:, :], t2, ALU.mult)
                for d in range(2):
                    dd = 2 * i + d
                    dve.wait_ge(S["sig_done"], dd + 1)
                    dve.tensor_scalar(c[:, :], c[:, :], -math.exp(-0.5), None, ALU.mult)
                    dve.drain()
                    dve.tensor_tensor_scan(cm[:, :], reset[:, :], c[:, :], 0.0, ALU.mult, ALU.add)
                    dve.drain()
                    dve.tensor_copy(mid[:, 0, :], chunked(cm[:, :])[:, :, RC // 2 - 1])
                    dve.tensor_tensor(em[:, :], cm[:, :], c[:, :], ALU.subtract)
                    dve.drain()
                    m = mid[:, 0, :].unsqueeze(2).to_broadcast([P, NCH, RC])
                    dve.tensor_tensor(mid[:, 1, :], chunked(cm[:, :])[:, :, RC - 1], mid[:, 0, :], ALU.subtract)
                    dve.tensor_tensor(chunked(em[:, :]), chunked(em[:, :]), m, ALU.subtract)
                    dve.drain()
                    dve.tensor_tensor(chunked(cm[:, :]), chunked(cm[:, :]), m, ALU.subtract)
                    if d == 1:
                        dve.tensor_copy(kd[:, :], em[:, :])
                    dve.drain()
                    dve.tensor_copy(own[:, 0:1], own[:, 0:1]).then_inc(S["cum_ready"], 1)
                    dve.tensor_scalar(t2, a[:, :], par["k_a"], own[:, 3:4], ALU.mult, ALU.add)
                    dve.drain()
                    dve.tensor_tensor(t2, t2, kf[:, :], ALU.mult)
                    dve.tensor_tensor(a[:, :], a[:, :], kk[:, :], ALU.mult)
                    dve.drain()
                    if d == 0:
                        dve.tensor_copy(kds[:, :], t2)
                    else:
                        dve.tensor_tensor(kds[:, :], kds[:, :], t2, ALU.add)
                    dve.wait_ge(S["exp_ready"], dd + 1)
                    ekk, er, eb = (em, cm, c) if d == 0 else (c, em, cm)
                    dve.tensor_tensor(qq[:, :, 0, :], chunked(kk[:, :]), chunked(ekk[:, :]), ALU.mult)
                    dve.tensor_tensor(qq[:, :, 1, :], chunked(r[:, :]), chunked(er[:, :]), ALU.mult)
                    dve.tensor_tensor(flat(bb), a[:, :], eb[:, :], ALU.mult)
                    dve.tensor_tensor(flat(kb), t2, eb[:, :], ALU.mult).then_inc(S["qk_ready"], 1)
                    start, end = (0, 1) if d == 0 else (1, 0)
                    for lo, hi in ((8, 12), (0, 8)):
                        if d == 0:
                            dve.tensor_tensor(factor[:, lo:hi - 1], mid[:, end, lo:hi - 1], mid[:, start, lo + 1:hi], ALU.mult)
                        else:
                            dve.tensor_tensor(factor[:, lo + 1:hi], mid[:, end, lo + 1:hi], mid[:, start, lo:hi - 1], ALU.mult)
                    seam_from, seam_to = (11, 0) if d == 0 else (8, 7)
                    dve.tensor_tensor(factor[:, seam_from:seam_from + 1], mid[:, end, seam_from:seam_from + 1],
                                      mid[:, start, seam_to:seam_to + 1], ALU.mult)
                    for b in range(6):
                        dve.wait_ge(S["l_done"], 6 * dd + b + 1)
                        dve.tensor_tensor(lt[:, 2 * b:2 * b + 2, :, :].rearrange("p n j c -> p n (j c)"),
                                          k.ps[:, 2 + b, :].rearrange("p (n w) -> p n w", n=2),
                                          lmask[:, d, :].unsqueeze(1).to_broadcast([P, 2, 256]), ALU.mult).then_inc(S["lt_ready"], 1)
                    for gr in range(2):
                        dve.wait_ge(S["g_done"], 12 * dd + gr + 1)
                        dve.scalar_tensor_tensor(out=x[:, GR * gr:GR * gr + GR, :], in0=k.ps[:, gr, 0:GR * RC].rearrange("p (n c) -> p n c", c=RC),
                                                 scalar=-1.0, in1=ident2[:, :].unsqueeze(1).to_broadcast([P, GR, RC]),
                                                 op0=ALU.mult, op1=ALU.add).then_inc(S["x_ready"], 1)
                    for l in range(1, LEVELS):
                        for gr in range(2):
                            dve.wait_ge(S["u_done"], 10 * dd + 2 * (l - 1) + gr + 1)
                            gs = slice(GR * gr, GR * gr + GR)
                            if l < LEVELS - 1:
                                xs = x[:, gs, :].rearrange("p n c -> p (n c)")
                                dve.tensor_tensor(xs, xs, k.ps[:, 2 + gr, 0:GR * RC], ALU.subtract)
                            xs = xt[:, gs, :].rearrange("p n c -> p (n c)")
                            dve.tensor_tensor(xs, xs, k.ps[:, 4 + gr, 0:GR * RC], ALU.subtract).then_inc(S["x_ready"], 1)
                    dve.memset(sm[:, 0, :], 0.0).then_inc(S["state_ready"], 1)
                    dve.drain()
                    for s, n in enumerate(order[d][:-1]):
                        f = factor[:, n:n + 1]
                        dve.tensor_scalar(sf[:, :], sm[:, s % 2, :], f, None, ALU.mult)
                        dve.drain()
                        dve.wait_ge(S["ds_done"], 11 * dd + s + 1)
                        dve.scalar_tensor_tensor(out=sm[:, (s + 1) % 2, :], in0=k.ps[:, 2, 0:64], scalar=f, in1=sf[:, :],
                                                 op0=ALU.mult, op1=ALU.add).then_inc(S["state_ready"], 1)
                        dve.drain()
                    dve.wait_ge(S["y_done"], dd + 1)
                    if d == 0:
                        dve.tensor_copy(y, region(k, 3)).then_inc(S["y_read"], 1)
                    else:
                        dve.scalar_tensor_tensor(out=kds[:, :], in0=r[:, :], scalar=par["r_k"], in1=kds[:, :], op0=ALU.mult, op1=ALU.mult)
                        dve.tensor_tensor(y, y, region(k, 3), ALU.add)
                        dve.drain()
                        dve.tensor_copy(own[:, 0:1], own[:, 0:1]).then_inc(S["y_read"], 1)
                dve.wait_ge(S["mean_done"], i + 1)
                dve.scalar_tensor_tensor(out=y, in0=region(k, 0), scalar=-1.0 / HEAD, in1=y, op0=ALU.mult, op1=ALU.add).then_inc(S["centred"], 1)
                dve.wait_ge(S["var_done"], i + 1)
                dve.tensor_scalar(t2, region(k, 1), 1.0 / HEAD, GN_EPS, ALU.mult, ALU.add).then_inc(S["var_ready"], 1)
                dve.tensor_tensor(t1, region(k, 2), v[:, :], ALU.mult)
                dve.wait_ge(S["var_root"], i + 1)
                dve.reciprocal(t2, t2)
                dve.drain()
                dve.tensor_tensor(y, y, t2, ALU.mult)
                dve.drain()
                dve.tensor_scalar(y, y, par["lnx_g"], par["lnx_b"], ALU.mult, ALU.add)
                dve.drain()
                dve.tensor_tensor(y, y, t1, ALU.add)
                dve.drain()
                dve.tensor_tensor(k.mo[:, bass.ds(i, 1), :].rearrange("p a t -> p (a t)"), y, region(k, 3), ALU.mult).then_inc(S["pair_done"], 1)
    feed.at += 1


def _tiles(w, kc=KC):
    w = w.reshape(kc, P, -1, P)
    return w.transpose(2, 1, 0, 3).reshape(-1, P, kc * P)


def _features(v):
    return v.reshape(-1, P).T


def _constants(np):
    c = {}
    c["ident"] = np.eye(P)
    pos = np.arange(LAT)
    nf = HEAD // 4
    inv = 10000.0 ** (-np.arange(nf, dtype=np.float32) / nf)
    ang = np.stack([(pos // GRID_W)[:, None] * inv, (pos % GRID_W)[:, None] * inv], axis=1).astype(np.float32)
    ang = np.broadcast_to(ang[:, :, None, :], (LAT, 2, 2, nf)).reshape(LAT, HEAD).T
    c["cos"], c["sin"] = np.tile(np.cos(ang), (2, 1)), np.tile(np.sin(ang), (2, 1))
    rot = np.zeros((P, P))
    for b in range(0, P, 32):
        for n in range(nf):
            rot[b + nf + n, b + n] = -1.0
            rot[b + n, b + nf + n] = 1.0
    c["rot"] = rot
    i, j = np.arange(P)[:, None], np.arange(P)[None, :]
    c["window_mask"] = np.concatenate([np.where(j >= i, 0.0, NEG), np.zeros((P, P + CTX)), np.where(j <= i, 0.0, NEG)], 1)
    start = np.clip(np.arange(GRID_W) - 8, 0, GRID_W - 16)[:, None]
    kc = np.arange(GRID_W)[None, :]
    c["column_mask"] = np.tile(np.where((kc >= start) & (kc < start + 16), 0.0, NEG), (2, 1))
    same = (i // RC) == (j // RC)
    c["bones"] = same.astype(np.float32)
    c["ident2"] = np.tile(np.eye(RC), (2, 1))
    c["reset"] = np.broadcast_to((np.arange(TOK) % RC != 0).astype(np.float32), (P, TOK))
    s, t = np.arange(RC)[:, None], np.arange(RC)[None, :]
    tri = [np.concatenate([s < t, s <= t, s < t, s <= t], 1), np.concatenate([s > t, s >= t, s > t, s >= t], 1)]
    c["tri_mask"] = np.tile(np.stack(tri, 1), (2, 1, 1))
    lev = [[((s >> (l + 1)) == (t >> (l + 1))) & ((s >> l) != (t >> l)) & ((s < t) if d == 0 else (s > t))
            for l in range(LEVELS)] for d in range(2)]
    c["level_mask"] = np.tile(np.array(lev).transpose(2, 0, 1, 3), (2, 1, 1, 1))
    inv = np.zeros((P, 2, TOK))
    for g, win in enumerate((2, 4, 8, 16)):
        for a, n in ((0, LAT), (LAT, CTX)):
            tt = np.arange(n)
            inv[64 * (g % 2):64 * (g % 2) + 64, g // 2, a:a + n] = 1.0 / (np.clip(tt + win // 2, 0, n) - np.clip(tt - win // 2, 0, n))
    c["pool_inv"] = inv
    return {n: np.ascontiguousarray(a, dtype=np.float32) for n, a in c.items()}


def _layout(np, x):
    a = _constants(np)
    both = np.concatenate([x["x"][0], x["ctx"][0]], 0)
    a["h0"] = both.T.reshape(KC, P, TOK).transpose(1, 0, 2)
    a["ctx2"] = x["ctx_2"][0].T.reshape(KC, P, CTX).transpose(1, 0, 2)
    for l in range(2):
        a[f"ada{l}"], a[f"ada{2 + l}"] = _tiles(x["ada_w"][l]), _tiles(x["ada_w_2"][l])
        a[f"ffn_g{l}"], a[f"ffn_u{l}"] = _tiles(x["ffn_w_in"][l][:, :FF]), _tiles(x["ffn_w_in"][l][:, FF:])
        a[f"ffn_g{2 + l}"], a[f"ffn_u{2 + l}"] = _tiles(x["ffn_w1_2"][l]), _tiles(x["ffn_w3_2"][l])
        for n, w in ((l, x["ffn_w_out"][l]), (2 + l, x["ffn_w2_2"][l])):
            a[f"ffn_d{n}"] = w.reshape(2, HALF, P, KC, P).transpose(0, 3, 2, 1, 4).reshape(2 * KC, P, HALF * P)
    a["even_in"], a["even_out"] = _tiles(x["even_w_in"][0]), _tiles(x["even_w_out"][0])
    w = x["odd_w_qkv"][0]
    order = [8 * c + 4 * s + j for c in range(2) for j in range(4) for s in range(2)]
    wq = w[:, :1024].reshape(D, 16, HEAD)[:, order].reshape(D, 1024)
    a["odd_in"] = _tiles(np.concatenate([wq, w[:, 1024:]], 1))
    a["odd_out"] = _tiles(x["odd_w_out"][0].reshape(16, HEAD, D)[order].reshape(1024, D))
    w = x["ev_w_in_2"][0]
    a["ev_in"], a["ev_out"] = _tiles(w), _tiles(x["ev_w_out_2"][0])
    a["od_in"], a["od_out"] = _tiles(x["od_w_in_2"][0]), _tiles(x["od_w_out_2"][0])
    mu = x["ev_shift_mu_2"][0]
    small = dict(c=x["c"][0], cc=x["c_ctx"], c2=x["c_2"][0], cc2=x["c_ctx_2"], ada_b=x["ada_b"], ada_b2=x["ada_b_2"],
                 norm1=x["norm1_g"], norm2=x["norm2_g"], final=x["final_g"], subln=x["diff_subln_g"], ln_g=x["ln_g_2"],
                 ln_b=x["ln_b_2"], mu_lora=mu[:, 2304:], pool_scale=x["ev_pool_scale_2"])
    a["small"] = np.concatenate([_features(small[n]) for n, _ in SMALL], 1)
    pair = [mu[d, 768 * j:768 * j + 768] for d in range(2) for j in range(3)]
    pair += [x["ev_w0_2"][0, 0], x["ev_w0_2"][0, 1], x["ev_a0_2"][0, 0], x["ev_a0_2"][0, 1], x["ev_k_k_2"][0],
             x["ev_k_a_2"][0], x["ev_r_k_2"][0].reshape(-1), x["ev_lnx_g_2"][0], x["ev_lnx_b_2"][0]]
    pair = np.stack(pair, 1).reshape(PAIRS, P, NPAIR)
    lora = np.stack([x["ev_w2_2"][0].reshape(P, -1), x["ev_a2_2"][0].reshape(P, -1), x["ev_g2_2"][0]], 0)
    lora = lora.reshape(3, P, PAIRS, P).transpose(2, 1, 0, 3).reshape(PAIRS, P, 3 * P)
    a["pair"] = np.concatenate([pair, lora], 2)
    a["pool_w"] = x["ev_pool_w_2"][0].reshape(2, 2, 64, 64).transpose(1, 2, 0, 3).reshape(P, 2, 64)
    a["rows"] = np.concatenate([x[n].reshape(-1) for n in ("diff_lq1", "diff_lk1", "diff_lq2", "diff_lk2", "odd_sink", "sgu_b")])
    a["sgu_wt"] = x["sgu_w"][0].transpose(2, 0, 1)
    a["rpb"] = x["od_rpb_2"][0].reshape(16 * DR, DCOL)
    return {n: np.ascontiguousarray(v) for n, v in a.items()}


def kernel(**inputs):
    import numpy as np
    import concourse.bacc as bacc
    from concourse.bass_utils import run_bass_kernel_spmd

    nc = bacc.Bacc("TRN2", target_bir_lowering=False, num_devices=1)
    arrays = _layout(np, {n: np.asarray(v) for n, v in inputs.items()})
    io = {n: nc.dram_tensor(f"in_{n}", v.shape, F32, kind="ExternalInput").ap() for n, v in arrays.items()}
    out = nc.dram_tensor("out", (P, KC, LAT), F32, kind="ExternalOutput").ap()
    program(nc, io, out)
    result = run_bass_kernel_spmd(nc, [{f"in_{n}": v for n, v in arrays.items()}], core_ids=[0])
    y = result.results[0]["out"]
    return y.transpose(2, 1, 0).reshape(1, LAT, D)
```

```python
import math
from contextlib import ExitStack

import concourse.bass as bass
from concourse import mybir

F32 = mybir.dt.float32
F32R = mybir.dt.float32r
ALU = mybir.AluOpType
ACT = mybir.ActivationFunctionType
AX = mybir.AxisListType

P = 128
D = 1024
KC = D // P
LAT, CTX = 512, 256
TOK = LAT + CTX
HEAD = 64
GRID_W = 64
FF = 2816
FC = FF // P
HALF = FC // 2
SIDE = 4
RING = 4
SLOT = HALF * P
EPS = 1e-6
GN_EPS = 64e-5
ALPHA = 4 ** 0.25
LAM_INIT = 0.8 - 0.6 * math.exp(-0.3 * 0)
SCALE = HEAD ** -0.5
RC = 64
NCH = TOK // RC
PAIRS = 6
RW = 21
NEG = -1e30
DR = 2 * 8 - 1
DCOL = 2 * 16 - 1
PADW = 2 * GRID_W - 1
LEVELS = 6

SMALL = [("c", 8), ("cc", 8), ("c2", 8), ("cc2", 8), ("ada_b", 96), ("ada_b2", 96), ("norm1", 16), ("norm2", 16),
         ("final", 8), ("subln", 1), ("ln_g", 32), ("ln_b", 32), ("mu_lora", 6), ("pool_scale", 2)]
COL = {}
for _name, _n in SMALL:
    COL[_name] = (sum(n for _, n in SMALL[:len(COL)]), _n)
NSMALL = sum(n for _, n in SMALL)
PAIRCOL = {n: c for c, n in enumerate(["mu0r", "mu0k", "mu0v", "mu1r", "mu1k", "mu1v", "w0_0", "w0_1", "a0_0", "a0_1",
                                       "k_k", "k_a", "r_k", "lnx_g", "lnx_b"])}
NPAIR = len(PAIRCOL)
ROWCOL = {"lam": 0, "sink": 256, "sgu_b": 272}
NROWS = 784


class Stage:

    def __init__(self, k, name):
        self.k, self.name = k, name

    def __enter__(self):
        k = self.k
        self.ids = list(k.sem_pools[k.stage_no % 2])
        self.clear = k.sem_pools[(k.stage_no + 1) % 2] if k.stage_no else None
        self.first = self.ids[0]
        self.mine = []
        self.stack = ExitStack()
        self.block = self.stack.enter_context(k.nc.Block(f"{self.name}_{k.stage_no}", no_gpsimd_drain=True))
        k.stage_no += 1
        return self

    def sem(self, name):
        s = self.k.nc.alloc_semaphore(f"{self.name}_{self.k.stage_no}_{name}", num=self.ids.pop(0))
        self.mine.append(s)
        return s

    def sb(self, name, shape, dtype=F32):
        return self.k.tmp.enter_context(self.k.nc.sbuf_tensor(f"{self.name}_{self.k.stage_no}_{name}", shape, dtype))

    def clear_last(self, pool):
        if self.clear:
            pool.drain()
            pool.sem_clear(range(self.clear[0], self.clear[-1] + 1))

    def __exit__(self, *a):
        self.stack.close()
        for s in self.mine:
            self.k.nc.release_semaphore(s)


class Feed:

    def __init__(self, k, plan, ring, name):
        self.plan, self.at = plan, 0
        self.ring = ring
        self.landed = [k.nc.alloc_semaphore(f"{name}_landed{s}") for s in range(RING)]
        self.used = [k.nc.alloc_semaphore(f"{name}_used{s}") for s in range(RING)]
        base = [0] * RING
        self.base = []
        for _, n, pattern in plan:
            self.base.append(list(base))
            for slot, *_ in pattern:
                base[slot] += n

    def count(self, stage, j):
        _, _, pattern = self.plan[stage]
        slot = pattern[j][0]
        before = self.base[stage][slot] + sum(1 for e in pattern[:j] if e[0] == slot)
        return slot, before, sum(1 for e in pattern if e[0] == slot)

    def issue(self, sp, stage, i, ahead=None):
        for j, (slot, src, mul, off) in enumerate(self.plan[stage][2]):
            slot, before, per = self.count(stage, j)
            if ahead is not None and ahead != (before == self.base[stage][slot]):
                continue
            if not (isinstance(i, int) and before + per * i == 0):
                sp.wait_ge(self.used[slot], per * i + before)
            w = src.shape[2]
            t = src[mul * i + off] if isinstance(i, int) else src[bass.ds(mul * i + off, 1)].rearrange("a p w -> (a p) w")
            sp.dma_start(self.ring[:, slot, 0:w], t).then_inc(self.landed[slot], 16)

    def program(self, sp, side=None):
        s = self.at
        n = self.plan[s][1]
        self.issue(sp, s, 0, ahead=False)
        if n > 1:
            if side:
                side.issue(sp, side.at, 0)
            with sp.Fori(1, n) as i:
                self.issue(sp, s, i)
                if side:
                    side.issue(sp, side.at, i)
        if s + 1 < len(self.plan):
            self.issue(sp, s + 1, 0, ahead=True)
        if side and n == 1:
            side.issue(sp, side.at, 0)

    def wait(self, pe, i, j):
        slot, before, per = self.count(self.at, j)
        pe.wait_ge(self.landed[slot], 16 * per * i + 16 * (before + 1))
        return slot

    def done(self, matmul, j):
        matmul.then_inc(self.used[self.count(self.at, j)[0]], 1)

    def wait_done(self, eng, i, j):
        slot, before, per = self.count(self.at, j)
        eng.wait_ge(self.used[slot], per * i + before + 1)


class Split:

    def __init__(self, k, st, slots, width=KC * P):
        self.k, self.slots = k, slots
        self.high = st.sb("high", [P, slots, width], F32R)
        self.low = st.sb("low", [P, slots, width], F32R)
        self.products, self.high_ready = st.sem("products"), st.sem("high_ready")

    def start(self, pe):
        pe.sem_inc(self.products, self.slots)

    def entry(self, i, j, base):
        return len(self.k.feed.plan[self.k.feed.at][2]) * i + base + j

    def write_high(self, act, i, j, base=0):
        feed = self.k.feed
        slot, before, per = feed.count(feed.at, j)
        w = feed.plan[feed.at][2][j][1].shape[2]
        act.wait_ge(feed.landed[slot], 16 * per * i + 16 * (before + 1))
        act.wait_ge(self.products, self.entry(i, j, base) + 1)
        act.activation(self.high[:, j % self.slots, 0:w], feed.ring[:, slot, 0:w], ACT.Copy).then_inc(self.high_ready, 1)

    def write_low(self, pool, i, j, base=0):
        feed = self.k.feed
        slot, before, per = feed.count(feed.at, j)
        w = feed.plan[feed.at][2][j][1].shape[2]
        pool.wait_ge(self.high_ready, self.entry(i, j, base) + 1)
        pool.tensor_tensor(self.low[:, j % self.slots, 0:w], feed.ring[:, slot, 0:w],
                           self.high[:, j % self.slots, 0:w].bitcast(F32), ALU.subtract).then_inc(feed.used[slot], 1)

    def wait(self, pe, i, j):
        feed = self.k.feed
        slot, before, per = feed.count(feed.at, j)
        pe.wait_ge(feed.used[slot], per * i + before + 1)
        return j % self.slots

    def wait_done(self, eng, i, j, base=0):
        eng.wait_ge(self.products, self.entry(i, j, base) + 1 + self.slots)

    def products_of(self, pe, dst, weights, values, first=True, last=True):
        pairs = ((0, 0), (0, 1), (1, 0))
        for n, (a, b) in enumerate(pairs):
            mm = pe.matmul(dst, weights[a], values[b], start=first and n == 0, stop=last and n == 2)
        return mm


class SideModulation:

    GROUPS = 6 * D // 512

    def __init__(self, k, st, names):
        self.k, self.names = k, names
        self.vec = st.sb("side_vec", [P, KC, 2])
        self.acc = st.sb("side_acc", [P, 2, 512])
        self.ready = st.sem("side_vec_ready")
        self.chunks_summed, self.summed = st.sem("side_chunks_summed"), st.sem("side_summed")
        self.bank = k.ps[:, 6, 0:2 * 48]

    def scalar(self, act):
        for s, name in enumerate(self.names):
            ins = act.activation(self.vec[:, :, s], col(self.k, name, 0, KC), ACT.Silu)
        ins.then_inc(self.ready, 1)

    def vector(self, dve, i, j, group):
        side = self.k.side
        if j == 0 and not (isinstance(group, int) and group == 0):
            dve.wait_ge(self.summed, group)
        slot = side.wait(dve, i, j)
        for b in range(2):
            w = side.ring[:, slot, 512 * b:512 * b + 512]
            for s in range(2):
                scale = self.vec[:, 2 * j + b, s:s + 1]
                if j == 0 and b == 0:
                    ins = dve.tensor_scalar(self.acc[:, s, :], w, scale, None, ALU.mult)
                else:
                    ins = dve.scalar_tensor_tensor(out=self.acc[:, s, :], in0=w, scalar=scale, in1=self.acc[:, s, :],
                                                   op0=ALU.mult, op1=ALU.add)
            if b == 1:
                side.done(ins, j)
            dve.drain()
        if j == 3:
            dve.sem_inc(self.chunks_summed, 1)

    def tensor(self, pe, group):
        pe.wait_ge(self.chunks_summed, group + 1)
        for n in range(4):
            for s in range(2):
                mm = pe.matmul(self.bank[:, bass.ds(8 * group + (2 * n + s), 1)], self.acc[:, s, n * P:(n + 1) * P],
                               self.k.ones[:, 0:1], start=True, stop=True)
        mm.then_inc(self.summed, 1)

    def finish(self, dve, bias):
        dve.wait_ge(self.summed, self.GROUPS)
        both = self.bank.rearrange("p (n s) -> p n s", s=2)
        for s in range(2):
            dve.tensor_tensor(self.k.mod_next[:, :, s], both[:, :, s], bias, ALU.add)


def spans(tokens):
    return [(0, LAT, 0), (LAT, TOK, 1)] if tokens == TOK else [(0, LAT, 0)]


class K:
    pass


def program(nc, io, out):
    k = K()
    k.nc = nc
    k.io = io
    k.stage_no = 0
    with ExitStack() as ctx:
        def sb(name, shape):
            return ctx.enter_context(nc.sbuf_tensor(name, shape, F32))

        k.h = sb("h", [P, KC, TOK])
        k.ring = sb("ring", [P, RING, SLOT])
        k.small = sb("small", [P, NSMALL])
        k.mod, k.mod_next = sb("mod_even", [P, 6 * KC, 2]), sb("mod_odd", [P, 6 * KC, 2])
        k.ones = sb("ones", [P, P])
        k.eps = sb("eps", [P, 2])
        k.ps = ctx.enter_context(nc.psum_tensor("ps", [P, 8, 512], F32))
        k.psf = k.ps[:, :, :].rearrange("p b n -> p (b n)")
        k.setup_sem = nc.alloc_semaphore("setup_sem")
        k.out_sem = nc.alloc_semaphore("out_sem")
        k.rows_sem = nc.alloc_semaphore("rows_sem")
        k.bias_sem = nc.alloc_semaphore("bias_sem")
        k.pair_landed = nc.alloc_semaphore("pair_landed")
        k.bias_landed = [nc.alloc_semaphore(f"bias_landed{j}") for j in range(4)]
        k.feed = Feed(k, weight_plan(io), k.ring, "weights")
        k.side = Feed(k, side_plan(io), None, "side")
        first = max(s.num for s in k.side.used) + 1
        k.sem_pools = [range(first, first + 40), range(first + 40, first + 80)]
        k.padded = nc.dram_tensor("padded_bias", (16 * DR, PADW), F32).ap()
        k.saved_h = nc.dram_tensor("saved_h", (P, KC, TOK), F32).ap()
        k.toeplitz = nc.dram_tensor("toeplitz_bias", (16, GRID_W, DR, GRID_W), F32).ap()

        load_inputs(k)
        modulation(k, "c", "cc", "ada_b", 0)
        with mixer(k, split=True):
            rms_modulate(k, TOK, 1, 0, "norm1", 0)
            with ExitStack() as k.tmp:
                gating_mlp(k)
            with ExitStack() as k.tmp:
                diff_attention(k)
        project_out(k, TOK, 2)
        with channel_mixer(k):
            rms_modulate(k, TOK, 4, 3, "norm2", 0)
            feed_forward(k, TOK, 5, ("c", "cc"), col(k, "ada_b", 48, 48))
        with mixer(k, split=True):
            rms_modulate(k, TOK, 1, 0, "norm1", 1)
            with ExitStack() as k.tmp:
                window_attention(k)
        project_out(k, LAT, 2)
        with channel_mixer(k):
            rms_modulate(k, LAT, 4, 3, "norm2", 1)
            feed_forward(k, LAT, 5, ("c2", "cc2"), col(k, "ada_b2", 0, 48))
        rms_modulate(k, LAT, None, None, "final", 0)
        with mixer(k, split=False):
            affine(k, TOK, 1, 0, load_context=True)
            with ExitStack() as k.tmp:
                rwkv(k)
        project_out(k, TOK, 2, restore=True)
        layer_norm(k, TOK, 0)
        with channel_mixer(k):
            affine(k, TOK, 4, 3)
            feed_forward(k, TOK, 5, ("c2", "cc2"), col(k, "ada_b2", 48, 48))
        layer_norm(k, TOK, 1)
        with mixer(k, split=True):
            affine(k, TOK, 1, 0)
            with ExitStack() as k.tmp:
                neighbourhood_attention(k)
        project_out(k, LAT, 2)
        layer_norm(k, LAT, 2)
        with channel_mixer(k):
            affine(k, LAT, 4, 3)
            feed_forward(k, LAT, 5)
        layer_norm(k, LAT, 3)
        store(k, out)


class mixer:

    def __init__(self, k, split):
        self.k, self.split = k, split

    def __enter__(self):
        k = self.k
        k.mo_stack, self.stack = ExitStack(), ExitStack()
        k.mo = k.mo_stack.enter_context(k.nc.sbuf_tensor(f"mo{k.stage_no}", [P, KC, TOK], F32))
        stream_buffers(k, self.stack, self.split)

    def __exit__(self, *a):
        self.stack.close()


class channel_mixer(mixer):

    def __init__(self, k):
        self.k = k

    def __enter__(self):
        self.stack = ExitStack()
        stream_buffers(self.k, self.stack, True)


def stream_buffers(k, stack, split):
    new = lambda name, dt: stack.enter_context(k.nc.sbuf_tensor(f"{name}{k.stage_no}", [P, KC, TOK], dt))
    k.split = split
    k.hn = (new("hn_high", F32R), new("hn_low", F32R)) if split else new("hn", F32)


def weight_plan(io):
    def ada(w):
        return ("modulation", 12, [(s, w, 4, s) for s in range(4)])

    def out(w):
        return ("project_out", 2, [(s, w, 4, s) for s in range(4)])

    def ffn(g, u, d):
        return [part for h in range(2) for part in (
            ("feed_up_first", 1, [(0, g, 0, HALF * h), (1, u, 0, HALF * h)]),
            ("feed_up", HALF // 2, [((2 + 2 * p + m) % 4, w, 2, HALF * h + 1 + p) for p in range(2) for m, w in enumerate((g, u))]),
            ("feed_down", 2, [(s, d, 4, KC * h + s) for s in range(4)]))]

    ew, ow, rw, nw = io["even_in"], io["odd_in"], io["ev_in"], io["od_in"]
    return [
        ada(io["ada0"]),
        ("gating", 2, [(0, ew, 2, 0), (1, ew, 2, 4), (2, ew, 2, 1), (3, ew, 2, 5)]),
        ("diff", 4, [(0, ew, 1, 8), (1, ew, 1, 12), (2, ew, 1, 16)]),
        out(io["even_out"]), *ffn(io["ffn_g0"], io["ffn_u0"], io["ffn_d0"]),
        ("window", 2, [(0, ow, 1, 8), (1, ow, 1, 10)] + [((2 + j) % 4, ow, 4, j) for j in range(4)]),
        out(io["odd_out"]), *ffn(io["ffn_g1"], io["ffn_u1"], io["ffn_d1"]),
        ("lora", 1, [(j % 4, rw, 0, 18 + j) for j in range(5)]),
        ("rwkv", PAIRS, [(1, rw, 1, 0), (2, rw, 1, 6), (3, rw, 1, 12)]),
        out(io["ev_out"]), *ffn(io["ffn_g2"], io["ffn_u2"], io["ffn_d2"]),
        ("neighbour_first", 1, [(s, nw, 0, KC * s) for s in range(3)]),
        ("neighbour", KC - 1, [(s, nw, 1, KC * s + 1) for s in range(3)]),
        out(io["od_out"]), *ffn(io["ffn_g3"], io["ffn_u3"], io["ffn_d3"]),
    ]


def side_plan(io):
    return [part for w in ("ada1", "ada2", "ada3") for h in range(2) for part in (
        ("first", 1, [(s % SIDE, io[w], 0, 24 * h + s) for s in range(4)]),
        ("up", HALF // 2, [(s % SIDE, io[w], 4, 24 * h + 4 + s) for s in range(4)]))]


def col(k, name, at=0, n=1):
    a = COL[name][0] + at
    return k.small[:, a:a + n]


def region(k, r, n=TOK):
    return k.psf[:, 1024 * r:1024 * r + n]


def load_inputs(k):
    with Stage(k, "load") as st:
        @st.block.sync
        def _(sp):
            for dst, src in ((k.small[:, :], k.io["small"]), (k.h[:, :, :], k.io["h0"])):
                sp.dma_start(dst, src).then_inc(k.setup_sem, 16)
            k.feed.issue(sp, 0, 0, ahead=True)
            sp.wait_ge(k.setup_sem, 32)

        @st.block.vector
        def _(dve):
            dve.memset(k.ones[:, :], 1.0)
            dve.memset(k.eps[:, 0:1], EPS)
            dve.memset(k.eps[:, 1:2], GN_EPS)


def store(k, out):
    with Stage(k, "store") as st:
        @st.block.sync
        def _(sp):
            sp.dma_start(out, k.h[:, :, 0:LAT]).then_inc(k.out_sem, 16)
            sp.wait_ge(k.out_sem, 16)


def modulation(k, c, cc, bias, layer):
    feed = k.feed
    with ExitStack() as k.tmp, Stage(k, "modulation") as st:
        vec = st.sb("vec", [P, KC, 2])
        silu_ready, products_read = st.sem("silu_ready"), st.sem("products_read")
        psum = k.ps[:, 0:RING, 0:2]

        @st.block.sync
        def _(sp):
            feed.program(sp)

        @st.block.gpsimd
        def _(pool):
            st.clear_last(pool)
            zeros = st.sb("zeros", [120, 2 * PADW])
            pool.memset(zeros[:, :], 0.0)
            pool.drain()
            pool.dma_start(k.padded.rearrange("(p r) c -> p (r c)", p=120), zeros[:, :]).then_inc(k.bias_sem, 16)
            pool.wait_ge(k.bias_sem, 16)
            left = (PADW - DCOL) // 2
            pool.dma_start(k.padded[:, left:left + DCOL], k.io["rpb"]).then_inc(k.bias_sem, 16)
            pool.wait_ge(k.bias_sem, 32)
            with pool.Fori(0, GRID_W) as q:
                pool.dma_start(k.toeplitz[:, bass.ds(q, 1), :, :].rearrange("h a r c -> (h a) r c"),
                               k.padded.rearrange("(h r) c -> h r c", h=16)[:, :, bass.ds(GRID_W - 1 - q, GRID_W)]).then_inc(k.bias_sem, 16)

        @st.block.scalar
        def _(act):
            act.activation(vec[:, :, 0], col(k, c, 0, KC), ACT.Silu)
            act.activation(vec[:, :, 1], col(k, cc, 0, KC), ACT.Silu).then_inc(silu_ready, 1)

        @st.block.tensor
        def _(pe):
            pe.wait_ge(silu_ready, 1)
            with pe.Fori(0, 12) as i:
                pe.wait_ge(products_read, i + 1)
                for j in range(RING):
                    slot = feed.wait(pe, i, j)
                    for c_ in range(KC):
                        mm = pe.matmul(psum[:, j, :], k.ring[:, slot, c_ * P:(c_ + 1) * P], vec[:, c_, :],
                                       start=c_ == 0, stop=c_ == KC - 1)
                    feed.done(mm, j)

        @st.block.vector
        def _(dve):
            b = col(k, bias, layer * 48, 48)
            dve.sem_inc(products_read, 1)
            with dve.Fori(0, 12) as i:
                feed.wait_done(dve, i, RING - 1)
                for s in range(2):
                    ins = dve.tensor_tensor(k.mod[:, bass.ds(4 * i, 4), s], psum[:, :, s], b[:, bass.ds(4 * i, 4)], ALU.add)
                ins.then_inc(products_read, 1)
    feed.at += 1


class StreamParts:

    def __init__(self, k, st, tokens):
        self.k, self.n = k, tokens
        self.whole = st.sb("whole", [P, 2, TOK])
        self.high_ready = st.sem("stream_high")
        self.low_ready = st.sem("stream_low_even"), st.sem("stream_low_odd")

    def claim(self, act, c):
        if c >= 2:
            act.wait_ge(self.low_ready[c % 2], c // 2)

    def scalar(self, act, c):
        act.drain()
        act.activation(self.k.hn[0][:, c, 0:self.n], self.whole[:, c % 2, 0:self.n], ACT.Copy).then_inc(self.high_ready, 1)

    def low(self, eng, c):
        eng.wait_ge(self.high_ready, c + 1)
        eng.tensor_tensor(self.k.hn[1][:, c, 0:self.n], self.whole[:, c % 2, 0:self.n],
                          self.k.hn[0][:, c, 0:self.n].bitcast(F32), ALU.subtract).then_inc(self.low_ready[c % 2], 1)

    def gpsimd(self, pool):
        for c in range(0, KC, 2):
            self.low(pool, c)
        pool.drain()


def rms_modulate(k, tokens, scale_at, shift_at, gain, layer):
    final = scale_at is None
    dst = k.h if final else None if k.split else k.hn
    with ExitStack() as k.tmp, Stage(k, "rms") as st:
        sq = st.sb("sq", [P, 2, TOK])
        gains = st.sb("gains", [P, KC, 2])
        rstd = st.sb("rstd", [P, TOK])
        squared, summed, gains_ready = st.sem("squared"), st.sem("summed"), st.sem("gains_ready")
        var_ready, root_ready = st.sem("var_ready"), st.sem("root_ready")
        scaled, shifted = st.sem("scaled"), st.sem("shifted")
        acc = region(k, 0, tokens)
        parts = StreamParts(k, st, tokens) if dst is None else None

        @st.block.gpsimd
        def _(pool):
            st.clear_last(pool)
            if parts:
                parts.gpsimd(pool)

        @st.block.scalar
        def _(act):
            for c in range(KC):
                if c >= 2:
                    act.wait_ge(summed, c - 1)
                act.activation(sq[:, c % 2, 0:tokens], k.h[:, c, 0:tokens], ACT.Square).then_inc(squared, 1)
            act.wait_ge(var_ready, 1)
            act.activation(rstd[:, 0:tokens], rstd[:, 0:tokens], ACT.Sqrt).then_inc(root_ready, 1)
            act.wait_ge(gains_ready, 1)
            for c in range(KC):
                act.wait_ge(scaled, c + 1)
                for a, b, s in spans(tokens):
                    shift = 0.0 if final else k.mod[:, shift_at * KC + c, s:s + 1]
                    if parts and a == 0:
                        parts.claim(act, c)
                    ins = act.activation(parts.whole[:, c % 2, a:b] if parts else dst[:, c, a:b], sq[:, c % 2, a:b], ACT.Identity,
                                         scale=gains[:, c, s:s + 1], bias=shift)
                ins.then_inc(shifted, 1)
                if parts:
                    parts.scalar(act, c)

        @st.block.tensor
        def _(pe):
            for c in range(KC):
                pe.wait_ge(squared, c + 1)
                for a, b, _ in spans(tokens):
                    mm = pe.matmul(acc[:, a:b], k.ones[:, :], sq[:, c % 2, a:b], start=c == 0, stop=c == KC - 1)
                mm.then_inc(summed, 1)

        @st.block.vector
        def _(dve):
            g = col(k, gain, layer * KC, KC)
            for s in range(2):
                if final:
                    ins = dve.tensor_copy(gains[:, :, s], g)
                else:
                    ins = dve.scalar_tensor_tensor(out=gains[:, :, s], in0=k.mod[:, scale_at * KC:(scale_at + 1) * KC, s],
                                                   scalar=1.0, in1=g, op0=ALU.add, op1=ALU.mult)
            ins.then_inc(gains_ready, 1)
            dve.wait_ge(summed, KC)
            dve.tensor_scalar(rstd[:, 0:tokens], acc, 1.0 / D, EPS, ALU.mult, ALU.add).then_inc(var_ready, 1)
            dve.wait_ge(root_ready, 1)
            dve.reciprocal(rstd[:, 0:tokens], rstd[:, 0:tokens])
            dve.drain()
            for c in range(KC):
                if c >= 2:
                    dve.wait_ge(shifted, c - 1)
                dve.tensor_tensor(sq[:, c % 2, 0:tokens], k.h[:, c, 0:tokens], rstd[:, 0:tokens], ALU.mult).then_inc(scaled, 1)
                if parts and c % 2 == 0 and c > 0:
                    parts.low(dve, c - 1)
            if parts:
                parts.low(dve, KC - 1)


def affine(k, tokens, scale_at, shift_at, load_context=False):
    with ExitStack() as k.tmp, Stage(k, "affine") as st:
        gains = st.sb("gains", [P, KC, 2])
        gains_ready, copied, context_landed = st.sem("gains_ready"), st.sem("copied"), st.sem("context_landed")

        parts = StreamParts(k, st, tokens) if k.split else None

        @st.block.sync
        def _(sp):
            if load_context:
                sp.dma_start(k.h[:, :, LAT:TOK], k.io["ctx2"]).then_inc(context_landed, 16)

        @st.block.gpsimd
        def _(pool):
            st.clear_last(pool)
            if parts:
                parts.gpsimd(pool)

        @st.block.scalar
        def _(act):
            act.wait_ge(gains_ready, 1)
            if load_context:
                act.wait_ge(context_landed, 16)
            for c in range(KC):
                for a, b, s in spans(tokens):
                    if parts and a == 0:
                        parts.claim(act, c)
                    ins = act.activation(parts.whole[:, c % 2, a:b] if parts else k.hn[:, c, a:b], k.h[:, c, a:b], ACT.Identity,
                                         scale=gains[:, c, s:s + 1], bias=k.mod[:, shift_at * KC + c, s:s + 1])
                ins.then_inc(copied, 1)
                if parts:
                    parts.scalar(act, c)

        @st.block.vector
        def _(dve):
            dve.tensor_scalar(gains[:, :, :], k.mod[:, scale_at * KC:(scale_at + 1) * KC, :], 1.0, None,
                              ALU.add).then_inc(gains_ready, 1)
            for c in range(KC):
                dve.wait_ge(copied, c + 1)
                dve.tensor_scalar(k.h[:, c, 0:tokens], k.h[:, c, 0:tokens], ALPHA, None, ALU.mult)
                if parts and c % 2:
                    parts.low(dve, c)


def layer_norm(k, tokens, which):
    with ExitStack() as k.tmp, Stage(k, "layernorm") as st:
        sq = st.sb("sq", [P, 2, TOK])
        rstd = st.sb("rstd", [P, TOK])
        mean_ready, centred, squared, summed = st.sem("mean_ready"), st.sem("centred"), st.sem("squared"), st.sem("summed")
        var_ready, root_ready, scaled = st.sem("var_ready"), st.sem("root_ready"), st.sem("scaled")
        total, acc = region(k, 0, tokens), region(k, 1, tokens)

        @st.block.gpsimd
        def _(pool):
            st.clear_last(pool)

        @st.block.tensor
        def _(pe):
            for c in range(KC):
                for a, b, _ in spans(tokens):
                    mm = pe.matmul(total[:, a:b], k.ones[:, :], k.h[:, c, a:b], start=c == 0, stop=c == KC - 1)
            mm.then_inc(mean_ready, 1)
            for c in range(KC):
                pe.wait_ge(squared, c + 1)
                for a, b, _ in spans(tokens):
                    mm = pe.matmul(acc[:, a:b], k.ones[:, :], sq[:, c % 2, a:b], start=c == 0, stop=c == KC - 1)
                mm.then_inc(summed, 1)

        @st.block.vector
        def _(dve):
            dve.wait_ge(mean_ready, 1)
            for c in range(KC):
                dve.scalar_tensor_tensor(out=k.h[:, c, 0:tokens], in0=total, scalar=-1.0 / D, in1=k.h[:, c, 0:tokens],
                                         op0=ALU.mult, op1=ALU.add).then_inc(centred, 1)
            dve.wait_ge(summed, KC)
            dve.tensor_scalar(rstd[:, 0:tokens], acc, 1.0 / D, EPS, ALU.mult, ALU.add).then_inc(var_ready, 1)
            dve.wait_ge(root_ready, 1)
            dve.reciprocal(rstd[:, 0:tokens], rstd[:, 0:tokens])
            dve.drain()
            for c in range(KC):
                dve.tensor_tensor(k.h[:, c, 0:tokens], k.h[:, c, 0:tokens], rstd[:, 0:tokens], ALU.mult).then_inc(scaled, 1)

        @st.block.scalar
        def _(act):
            for c in range(KC):
                act.wait_ge(centred, c + 1)
                if c >= 2:
                    act.wait_ge(summed, c - 1)
                act.activation(sq[:, c % 2, 0:tokens], k.h[:, c, 0:tokens], ACT.Square).then_inc(squared, 1)
            act.wait_ge(var_ready, 1)
            act.activation(rstd[:, 0:tokens], rstd[:, 0:tokens], ACT.Sqrt).then_inc(root_ready, 1)
            for c in range(KC):
                act.wait_ge(scaled, c + 1)
                act.activation(k.h[:, c, 0:tokens], k.h[:, c, 0:tokens], ACT.Identity,
                               scale=col(k, "ln_g", which * KC + c), bias=col(k, "ln_b", which * KC + c))


def tile_products(k, pe, i, j, dst, src, tokens, split=None, chunks=range(KC), first=True, last=True):
    slot = split.wait(pe, i, j) if split else k.feed.wait(pe, i, j)
    for a, b, _ in spans(tokens):
        for n, c in enumerate(chunks):
            lo, hi = first and n == 0, last and n == len(chunks) - 1
            cols = slice(n * P, (n + 1) * P)
            if split:
                mm = split.products_of(pe, dst[:, a:b], (split.high[:, slot, cols], split.low[:, slot, cols]),
                                       (src[0][:, c, a:b], src[1][:, c, a:b]), lo, hi)
            else:
                mm = pe.matmul(dst[:, a:b], k.ring[:, slot, cols], src[:, c, a:b], start=lo, stop=hi)
    if split:
        mm.then_inc(split.products, 1)
    else:
        k.feed.done(mm, j)


def token_products(k, pe, i, j, dst, src, tokens, split):
    slot = split.wait(pe, i, j)
    for t in range(tokens // P):
        ts = slice(t * P, (t + 1) * P)
        for c in range(KC):
            cols = slice(c * P, (c + 1) * P)
            mm = split.products_of(pe, dst[:, ts], (src[0][:, c, ts], src[1][:, c, ts]),
                                   (split.high[:, slot, cols], split.low[:, slot, cols]), c == 0, c == KC - 1)
    mm.then_inc(split.products, 1)


def project_out(k, tokens, gate_at, restore=False):
    with ExitStack() as k.tmp, Stage(k, "project") as st:
        free = st.sem("psum_free")
        restored = st.sem("stream_restored")

        @st.block.sync
        def _(sp):
            if restore:
                sp.dma_start(k.h[:, :, :], k.saved_h).then_inc(restored, 16)
            k.feed.program(sp)

        @st.block.gpsimd
        def _(pool):
            st.clear_last(pool)

        @st.block.tensor
        def _(pe):
            with pe.Fori(0, 2) as i:
                for j in range(4):
                    pe.wait_ge(free, 4 * i + j + 1)
                    tile_products(k, pe, i, j, region(k, j, tokens), k.mo, tokens)

        @st.block.vector
        def _(dve):
            dve.sem_inc(free, 4)
            if restore:
                dve.wait_ge(restored, 16)
            with dve.Fori(0, 2) as i:
                for j in range(4):
                    k.feed.wait_done(dve, i, j)
                    residual(k, dve, tokens, gate_at, 4 * i + j, j).then_inc(free, 1)
    k.feed.at += 1
    k.mo_stack.close()


def residual(k, dve, tokens, gate_at, n, r):
    for a, b, s in spans(tokens):
        hs = k.h[:, bass.ds(n, 1), a:b].rearrange("p a t -> p (a t)")
        ins = dve.scalar_tensor_tensor(out=hs, in0=region(k, r)[:, a:b], scalar=k.mod[:, bass.ds(n + gate_at * KC, 1), s],
                                       in1=hs, op0=ALU.mult, op1=ALU.add)
    return ins


def feed_forward(k, tokens, gate_at, next_c=None, next_bias=None):
    feed, side = k.feed, k.side
    FIRST, UP, DOWN = 2, 4 * (HALF // 2), 8
    with ExitStack() as k.tmp, Stage(k, "feed") as st:
        split = Split(k, st, 2, SLOT)
        hid = st.sb("hid_high", [P, HALF, tokens], F32R), st.sb("hid_low", [P, HALF, tokens], F32R)
        gate, whole = st.sb("gate", [P, tokens])[:, :], region(k, 2, tokens)
        gated, multiplied, hid_high_ready, hid_low_ready, y_free = (
            st.sem("gated"), st.sem("multiplied"), st.sem("hid_high_ready"), st.sem("hid_low_ready"), st.sem("y_free"))
        if next_c:
            side.ring = st.sb("side_ring", [P, SIDE, KC * P])
            sm = SideModulation(k, st, next_c)
        GATE, UPR = region(k, 0, tokens), region(k, 1, tokens)
        base, side_base = feed.at, side.at

        def sections(h):
            e = h * (FIRST + UP + DOWN)
            return (base + 3 * h, e), (base + 3 * h + 1, e + FIRST), (base + 3 * h + 2, e + FIRST + UP)

        @st.block.sync
        def _(sp):
            for h in range(2):
                for n, (at, _) in enumerate(sections(h)):
                    feed.at = at
                    side.at = side_base + 2 * h + n
                    feed.program(sp, side if next_c and n < 2 else None)
            feed.at, side.at = base, side_base

        @st.block.gpsimd
        def _(pool):
            st.clear_last(pool)
            for h in range(2):
                for at, e in sections(h):
                    feed.at = at
                    if feed.plan[at][1] > 1:
                        with pool.Fori(0, feed.plan[at][1]) as i:
                            for j in range(4):
                                split.write_low(pool, i, j, e)
                    else:
                        for j in range(2):
                            split.write_low(pool, 0, j, e)
            feed.at = base

        @st.block.tensor
        def _(pe):
            split.start(pe)
            for h in range(2):
                (first, _), (up, _), (down, _) = sections(h)

                def chunk(i, p, n):
                    pe.wait_ge(gated, n + (HALF * h + 1))
                    tile_products(k, pe, i, 2 * p, GATE, k.hn, tokens, split)
                    pe.wait_ge(multiplied, n + (HALF * h + 1))
                    tile_products(k, pe, i, 2 * p + 1, UPR, k.hn, tokens, split)
                    if next_c and p == 0 and not isinstance(i, int):
                        sm.tensor(pe, i + 6 * h)

                feed.at = first
                if h:
                    pe.wait_ge(y_free, 8 * h + 2)
                chunk(0, 0, 0)
                feed.at = up
                with pe.Fori(0, HALF // 2) as i:
                    for p in range(2):
                        chunk(i, p, 2 * i + (p + 1))
                feed.at = down
                if next_c:
                    sm.tensor(pe, 6 * h + 5)
                pe.wait_ge(hid_low_ready, HALF * (h + 1))
                with pe.Fori(0, 2) as i:
                    for j in range(4):
                        pe.wait_ge(y_free, 4 * i + (8 * h + j + 1))
                        tile_products(k, pe, i, j, region(k, j % 2, tokens), hid, tokens, split, chunks=range(HALF))
            feed.at = base

        @st.block.scalar
        def _(act):
            if next_c:
                sm.scalar(act)
            act.sem_inc(gated, 1)
            for h in range(2):
                (first, e), (up, e1), (down, e2) = sections(h)

                def store_high(n):
                    act.wait_ge(multiplied, n + (HALF * h + 2))
                    act.activation(hid[0][:, bass.ds(n, 1), :].rearrange("p a t -> p (a t)"), whole,
                                   ACT.Copy).then_inc(hid_high_ready, 1)

                def gate_chunk(i, p, eb):
                    split.write_high(act, i, 2 * p + 1, eb)
                    split.wait_done(act, i, 2 * p, eb)
                    act.activation(gate, GATE, ACT.Silu).then_inc(gated, 1)

                feed.at = first
                split.write_high(act, 0, 0, e)
                gate_chunk(0, 0, e)
                feed.at = up
                with act.Fori(0, HALF // 2) as i:
                    for p in range(2):
                        split.write_high(act, i, 2 * p, e1)
                        store_high(2 * i + p)
                        gate_chunk(i, p, e1)
                feed.at = down
                split.write_high(act, 0, 0, e2)
                store_high(HALF - 1)
                for n in range(1, DOWN):
                    split.write_high(act, n // 4, n % 4, e2)
            feed.at = base

        @st.block.vector
        def _(dve):
            dve.sem_inc(multiplied, 1)
            dve.sem_inc(y_free, 2)
            if next_c:
                dve.wait_ge(sm.ready, 1)
            for h in range(2):
                (first, e), (up, e1), (down, e2) = sections(h)

                def chunk(i, p, n, eb):
                    split.wait_done(dve, i, 2 * p + 1, eb)
                    dve.wait_ge(gated, n + (HALF * h + 2))
                    dve.tensor_tensor(whole, gate, UPR, ALU.mult).then_inc(multiplied, 1)
                    dve.wait_ge(hid_high_ready, n + (HALF * h + 1))
                    high = hid[0][:, bass.ds(n, 1), :].rearrange("p a t -> p (a t)").bitcast(F32)
                    dve.tensor_tensor(hid[1][:, bass.ds(n, 1), :].rearrange("p a t -> p (a t)"), whole, high,
                                      ALU.subtract).then_inc(hid_low_ready, 1)
                    dve.drain()

                feed.at, side.at = first, side_base + 2 * h
                chunk(0, 0, 0, e)
                if next_c:
                    for j in range(4):
                        sm.vector(dve, 0, j, 6 * h)
                feed.at, side.at = up, side_base + 2 * h + 1
                with dve.Fori(0, HALF // 2) as i:
                    for p in range(2):
                        chunk(i, p, 2 * i + (p + 1), e1)
                        if next_c:
                            for j in (2 * p, 2 * p + 1):
                                sm.vector(dve, i, j, i + (6 * h + 1))
                feed.at = down
                with dve.Fori(0, 2) as i:
                    for j in range(4):
                        split.wait_done(dve, i, j, e2)
                        residual(k, dve, tokens, gate_at, 4 * i + j, j % 2).then_inc(y_free, 1)
            if next_c:
                sm.finish(dve, next_bias)
            feed.at, side.at = base, side_base
        feed.at = base + 6
        if next_c:
            side.at = side_base + 4
    if next_c:
        k.mod, k.mod_next = k.mod_next, k.mod


def constants(k, st, *names):
    return [st.sb(n, list(k.io[n].shape)) for n in names]


class Attention:

    def __init__(self, k, st, units, subs, scale, prepare=None, sinks=None, lam=None):
        self.k, self.st, self.units, self.subs, self.scale = k, st, units, subs, scale
        self.prepare, self.sinks, self.lam = prepare, sinks, lam
        self.ident, self.ident_landed = st.sb("ident", [P, P]), st.sem("ident_landed")
        self.probs = st.sb("probs", [P, 2 * subs, TOK])
        self.turned = st.sb("turned", [P, 2, TOK])
        self.scores = st.sb("scores", [P, 2, TOK]) if prepare else None
        self.mixed = st.sb("mixed", [P, TOK]) if subs == 2 else None
        self.negmax = st.sb("negmax", [P, 2 * subs])
        self.rowmax = st.sb("rowmax", [P, 2 * subs])
        self.sums = st.sb("sums", [P, 2 * subs])
        self.sinkexp = st.sb("sinkexp", [P, 2 * subs])
        self.recip = st.sb("recip", [P, 2 * subs])
        self.scores_ready = st.sem("scores_ready")
        self.max_ready = st.sem("max_ready")
        self.exp_done = st.sem("exp_done")
        self.probs_ready = st.sem("probs_ready")
        self.turn_done = st.sem("turn_done")
        self.turned_ready = st.sem("turned_ready")
        self.values_done = st.sem("values_done")

    def load(self, sp):
        sp.dma_start(self.ident[:, :], self.k.io["ident"]).then_inc(self.ident_landed, 16)

    def slot(self, u, s):
        return s if self.subs == 2 else u % 2

    def buf(self, u, s):
        return self.subs * (u % 2) + s

    def tensor(self, pe, i, lo, hi, between=None):
        U = len(self.units)
        ahead = 2 if self.subs == 1 else 1

        def scores(u):
            for s, products in enumerate(self.units[u]["scores"]):
                if self.subs == 2 and u > 0:
                    pe.wait_ge(self.exp_done, i * (2 * U) + 2 * u + s - 1)
                if self.subs == 1 and u > 1:
                    pe.wait_ge(self.max_ready, i * U + u - 1)
                for q, key, c, n in products:
                    mm = pe.matmul(region(self.k, 1 + self.slot(u, s))[:, c:c + n], q, key, start=True, stop=True)
                mm.then_inc(self.scores_ready, 1)

        def turn(u):
            pe.wait_ge(self.probs_ready, i * U + u + 1)
            if u > 0:
                pe.wait_ge(self.turned_ready, i * U + u)
            src = self.mixed[:, :] if self.subs == 2 else self.probs[:, u % 2, :]
            for b in range(self.units[u]["n"] // P):
                mm = pe.transpose(region(self.k, 3)[:, b * P:(b + 1) * P], src[:, b * P:(b + 1) * P], self.ident[:, :])
            mm.then_inc(self.turn_done, 1)

        def values(u):
            pe.wait_ge(self.turned_ready, i * U + u + 1)
            v = self.units[u]["values"]
            for b, val in enumerate(v):
                mm = pe.matmul(self.units[u]["out"], val, self.turned[:, u % 2, b * P:(b + 1) * P],
                               start=b == 0, stop=b == len(v) - 1)
            mm.then_inc(self.values_done, 1)

        for u in range(lo, lo + ahead):
            scores(u)
        for u in range(lo, hi):
            if u + ahead < hi:
                scores(u + ahead)
            if between:
                between(u)
            turn(u)
            if u > lo:
                values(u - 1)
        values(hi - 1)

    def vector(self, dve, i, lo, hi, between=None):
        U, S = len(self.units), self.subs

        def maxima(u):
            n = self.units[u]["n"]
            if S == 1 and u > 1:
                dve.wait_ge(self.exp_done, i * U + u - 1)
            if S == 2 and u > 1:
                dve.wait_ge(self.exp_done, i * (2 * U) + 2 * u - 2)
            for s in range(S):
                r, m = self.slot(u, s), self.buf(u, s)
                dve.wait_ge(self.scores_ready, i * (U * S) + u * S + s + 1)
                src = region(self.k, 1 + r, n)
                if self.prepare:
                    self.prepare(dve, self.units[u], src, self.scores[:, r, 0:n])
                    dve.drain()
                    src = self.scores[:, r, 0:n]
                dve.tensor_reduce(self.rowmax[:, m:m + 1], src, AX.X, ALU.max)
                dve.drain()
                if self.sinks is not None:
                    sink = self.sinks[:, self.units[u]["sink"]:self.units[u]["sink"] + 1]
                    dve.tensor_scalar(self.rowmax[:, m:m + 1], self.rowmax[:, m:m + 1], self.scale, sink, ALU.mult, ALU.max)
                    dve.drain()
                    dve.tensor_scalar(self.negmax[:, m:m + 1], self.rowmax[:, m:m + 1], -1.0, None, ALU.mult).then_inc(self.max_ready, 1)
                else:
                    dve.tensor_scalar(self.negmax[:, m:m + 1], self.rowmax[:, m:m + 1], -self.scale, None, ALU.mult).then_inc(self.max_ready, 1)

        def finish(u):
            n = self.units[u]["n"]
            dve.wait_ge(self.exp_done, i * (S * U) + S * (u + 1))
            if S == 2:
                m = self.buf(u, 0)
                dve.reciprocal(self.recip[:, m:m + 2], self.sums[:, m:m + 2])
                dve.drain()
                dve.tensor_tensor(self.recip[:, m + 1:m + 2], self.recip[:, m + 1:m + 2], self.lam, ALU.mult)
                dve.drain()
                if u > 0:
                    dve.wait_ge(self.turn_done, i * U + u)
                dve.tensor_scalar(self.probs[:, m + 1, 0:n], self.probs[:, m + 1, 0:n], self.recip[:, m + 1:m + 2], None, ALU.mult)
                dve.drain()
                dve.scalar_tensor_tensor(out=self.mixed[:, 0:n], in0=self.probs[:, m, 0:n], scalar=self.recip[:, m:m + 1],
                                         in1=self.probs[:, m + 1, 0:n], op0=ALU.mult, op1=ALU.subtract).then_inc(self.probs_ready, 1)
            else:
                r = u % 2
                total = self.sums[:, r:r + 1]
                if self.sinks is not None:
                    dve.tensor_tensor(total, total, self.sinkexp[:, r:r + 1], ALU.add)
                    dve.drain()
                dve.reciprocal(self.recip[:, r:r + 1], total)
                dve.drain()
                dve.tensor_scalar(self.probs[:, r, 0:n], self.probs[:, r, 0:n], self.recip[:, r:r + 1], None,
                                  ALU.mult).then_inc(self.probs_ready, 1)

        for u in range(lo, hi):
            maxima(u)
            if u > lo:
                finish(u - 1)
            if between:
                between(u)
        finish(hi - 1)

    def scalar(self, act, i, lo, hi, between=None):
        U, S = len(self.units), self.subs

        def exps(u):
            n = self.units[u]["n"]
            if S == 2 and u > 1:
                act.wait_ge(self.probs_ready, i * U + u - 1)
            if S == 1 and u > 1:
                act.wait_ge(self.turn_done, i * U + u - 1)
            for s in range(S):
                r, m = self.slot(u, s), self.buf(u, s)
                act.wait_ge(self.max_ready, i * (U * S) + u * S + s + 1)
                if self.sinks is not None:
                    sink = self.sinks[:, self.units[u]["sink"]:self.units[u]["sink"] + 1]
                    act.activation(self.sinkexp[:, m:m + 1], sink, ACT.Exp, bias=self.negmax[:, m:m + 1])
                src = self.scores[:, r, 0:n] if self.prepare else region(self.k, 1 + r, n)
                act.activation(self.probs[:, m, 0:n], src, ACT.Exp, bias=self.negmax[:, m:m + 1], scale=self.scale,
                                     accum_out=self.sums[:, m:m + 1]).then_inc(self.exp_done, 1)

        def copy(u):
            n = self.units[u]["n"]
            act.wait_ge(self.turn_done, i * U + u + 1)
            if u > 1:
                act.wait_ge(self.values_done, i * U + u - 1)
            act.activation(self.turned[:, u % 2, 0:n], region(self.k, 3, n), ACT.Copy).then_inc(self.turned_ready, 1)

        for u in range(lo, hi):
            exps(u)
            if u > lo:
                copy(u - 1)
            if between:
                between(u)
        copy(hi - 1)


def gating_mlp(k):
    nc, feed = k.nc, k.feed
    T = TOK // P
    with Stage(k, "gating") as st:
        split = Split(k, st, 2)
        u = st.sb("u", [P, 2, TOK])
        v = st.sb("v", [P, 2, T, P])
        wst = st.sb("wst", [P, 4, P])
        rows = st.sb("rows", [P, NROWS])
        stats = st.sb("stats", [P, 4, T, 6])
        mv = st.sb("mv", [P, 4, T, 2])
        rstd = st.sb("rstd", [P, 4, T])
        landed = st.sem("constants_landed")
        u_ready, v_ready, var_ready, root_ready = st.sem("u_ready"), st.sem("v_ready"), st.sem("var_ready"), st.sem("root_ready")
        normed, mixed, done = st.sem("normed"), st.sem("mixed"), st.sem("gated")

        @st.block.sync
        def _(sp):
            sp.dma_start(wst[:, :, :], k.io["sgu_wt"]).then_inc(landed, 16)
            sp.dma_start(rows[:, :], k.io["rows"].partition_broadcast(P)).then_inc(landed, 16)
            feed.program(sp)

        @st.block.gpsimd
        def _(pool):
            st.clear_last(pool)
            for g in range(4):
                for j in range(2):
                    split.write_low(pool, g // 2, 2 * (g % 2) + j)

        @st.block.tensor
        def _(pe):
            def mix(g):
                b = g % 2
                pe.wait_ge(normed, g + 1)
                for t in range(T):
                    mm = pe.matmul(region(k, 2 * b + 1)[:, t * P:(t + 1) * P], v[:, g % 2, t, :], wst[:, g, :], start=True, stop=True)
                mm.then_inc(mixed, 1)

            split.start(pe)
            pe.wait_ge(landed, 32)
            for g in range(4):
                i, b = divmod(g, 2)
                if g >= 2:
                    pe.wait_ge(u_ready, g - 1)
                    pe.wait_ge(done, g - 1)
                tile_products(k, pe, i, 2 * b, region(k, 2 * b), k.hn, TOK, split)
                token_products(k, pe, i, 2 * b + 1, region(k, 2 * b + 1), k.hn, TOK, split)
                if g > 0:
                    mix(g - 1)
            mix(3)

        @st.block.scalar
        def _(act):
            for j in range(2):
                split.write_high(act, 0, j)
            for g in range(4):
                i, b = divmod(g, 2)
                if g >= 2:
                    act.wait_ge(done, g - 1)
                split.wait_done(act, i, 2 * b)
                if g < 3:
                    split.write_high(act, (g + 1) // 2, 2 * ((g + 1) % 2))
                act.activation(u[:, g % 2, :], region(k, 2 * b), ACT.Gelu).then_inc(u_ready, 1)
                split.wait_done(act, i, 2 * b + 1)
                if g < 3:
                    split.write_high(act, (g + 1) // 2, 2 * ((g + 1) % 2) + 1)
                act.activation(v[:, g % 2, :, :].rearrange("p t c -> p (t c)"), region(k, 2 * b + 1), ACT.Gelu).then_inc(v_ready, 1)
                act.wait_ge(var_ready, g + 1)
                act.activation(rstd[:, g, :], mv[:, g, :, 1], ACT.Sqrt, bias=k.eps[:, 0:1]).then_inc(root_ready, 1)

        @st.block.vector
        def _(dve):
            for g in range(4):
                b = g % 2
                dve.wait_ge(v_ready, g + 1)
                for t in range(T):
                    dve.bn_stats(stats[:, g, t, :], v[:, g % 2, t, :])
                dve.drain()
                for t in range(T):
                    ins = dve.bn_aggr(mv[:, g, t, :], stats[:, g, t, :])
                ins.then_inc(var_ready, 1)
                dve.wait_ge(root_ready, g + 1)
                dve.reciprocal(rstd[:, g, :], rstd[:, g, :])
                dve.drain()
                for t in range(T):
                    ins = dve.tensor_scalar(v[:, g % 2, t, :], v[:, g % 2, t, :], mv[:, g, t, 0:1], rstd[:, g, t:t + 1], ALU.subtract, ALU.mult)
                ins.then_inc(normed, 1)
                dve.wait_ge(mixed, g + 1)
                bias = rows[:, ROWCOL["sgu_b"] + g * P:ROWCOL["sgu_b"] + (g + 1) * P]
                mo = k.mo[:, g, :]
                dve.tensor_tensor(mo.rearrange("p (t c) -> p t c", t=T), region(k, 2 * b + 1).rearrange("p (t c) -> p t c", t=T),
                                  bias.unsqueeze(1).to_broadcast([P, T, P]), ALU.add)
                dve.drain()
                dve.wait_ge(u_ready, g + 1)
                dve.tensor_tensor(mo, mo, u[:, g % 2, :], ALU.mult).then_inc(done, 1)
    feed.at += 1


def rope(k, dve, x, rotated, cos, sin, tmp):
    dve.tensor_tensor(tmp, rotated, sin, ALU.mult)
    dve.tensor_tensor(x, x, cos, ALU.mult)
    dve.drain()
    return dve.tensor_tensor(x, x, tmp, ALU.add)


def diff_attention(k):
    nc, feed = k.nc, k.feed
    T = TOK // P
    with Stage(k, "diff") as st:
        split = Split(k, st, 3)
        q, key, v = st.sb("q", [P, TOK]), st.sb("key", [P, TOK]), st.sb("v", [P, T, P])
        tmp = st.sb("tmp", [P, LAT])
        rot, cos, sin = constants(k, st, "rot", "cos", "sin")
        rows = st.sb("rows", [P, NROWS])
        dots, lam, gain = st.sb("dots", [P, 2]), st.sb("lam", [P, 1]), st.sb("gain", [P, 1])
        junk = st.sb("junk", [P, HEAD])
        rstd, sq = st.sb("rstd", [P, TOK]), st.sb("sq", [P, TOK])
        landed, dots_ready, lam_exp = st.sem("constants_landed"), st.sem("dots_ready"), st.sem("lam_exp")
        copied, rotated, roped = st.sem("copied"), st.sem("rotated"), st.sem("roped")
        squared, summed, var_ready, root_ready, head_done = (st.sem("squared"), st.sem("summed"), st.sem("var_ready"),
                                                             st.sem("root_ready"), st.sem("head_done"))
        units = []
        for t in range(T):
            keys = [(0, 512), (512, 256)] if t < LAT // P else [(512, 256)]
            off = keys[0][0]
            units.append(dict(
                n=TOK - off, out=region(k, 0)[:, t * P:(t + 1) * P], values=[v[:, b, :] for b in range(off // P, T)],
                scores=[[(q[64 * s:64 * s + 64, t * P:(t + 1) * P], key[64 * s:64 * s + 64, a:a + n], a - off, n)
                         for a, n in keys] for s in range(2)]))
        att = Attention(k, st, units, 2, SCALE, lam=lam[:, :])
        U = len(units)

        @st.block.sync
        def _(sp):
            for dst, name in ((rot, "rot"), (cos, "cos"), (sin, "sin")):
                sp.dma_start(dst[:, :], k.io[name]).then_inc(landed, 16)
            sp.dma_start(rows[:, :], k.io["rows"].partition_broadcast(P)).then_inc(landed, 16)
            att.load(sp)
            feed.program(sp)

        @st.block.gpsimd
        def _(pool):
            st.clear_last(pool)
            with pool.Fori(0, 4) as i:
                for j in range(3):
                    split.write_low(pool, i, j)

        @st.block.tensor
        def _(pe):
            split.start(pe)
            pe.wait_ge(landed, 64)
            pe.wait_ge(att.ident_landed, 16)
            with pe.Fori(0, 4) as i:
                pe.wait_ge(head_done, i + 1)
                tile_products(k, pe, i, 0, region(k, 0), k.hn, TOK, split)
                tile_products(k, pe, i, 1, region(k, 1), k.hn, TOK, split)
                token_products(k, pe, i, 2, region(k, 2), k.hn, TOK, split)
                pe.wait_ge(copied, 3 * i + 1)
                pe.matmul(region(k, 3, LAT), rot[:, :], q[:, 0:LAT], start=True, stop=True).then_inc(rotated, 1)
                pe.wait_ge(copied, 3 * i + 2)
                pe.matmul(region(k, 0, LAT), rot[:, :], key[:, 0:LAT], start=True, stop=True).then_inc(rotated, 1)
                pe.wait_ge(copied, 3 * i + 3)
                pe.wait_ge(roped, 2 * i + 2)
                att.tensor(pe, i, 0, U)
                pe.wait_ge(squared, i + 1)
                for a, b, _ in spans(TOK):
                    mm = pe.matmul(region(k, 1)[:, a:b], k.ones[:, :], sq[:, a:b], start=True, stop=True)
                mm.then_inc(summed, 1)

        @st.block.scalar
        def _(act):
            act.wait_ge(dots_ready, 1)
            act.activation(dots[:, :], dots[:, :], ACT.Exp).then_inc(lam_exp, 1)
            with act.Fori(0, 4) as i:
                for j in range(3):
                    split.write_high(act, i, j)
                for j, dst in enumerate((q[:, :], key[:, :], v[:, :, :].rearrange("p t c -> p (t c)"))):
                    split.wait_done(act, i, j)
                    act.activation(dst, region(k, j), ACT.Copy).then_inc(copied, 1)
                att.scalar(act, i, 0, U)
                act.wait_ge(att.values_done, U * i + U)
                act.activation(sq[:, :], region(k, 0), ACT.Square).then_inc(squared, 1)
                act.wait_ge(var_ready, i + 1)
                act.activation(rstd[:, :], rstd[:, :], ACT.Sqrt).then_inc(root_ready, 1)

        @st.block.vector
        def _(dve):
            dve.sem_inc(head_done, 1)
            dve.wait_ge(landed, 64)
            for j in range(2):
                ins = dve.tensor_tensor_reduce(junk[:, :], rows[:, 128 * j:128 * j + 64], rows[:, 128 * j + 64:128 * j + 128],
                                               1.0, 0.0, ALU.mult, ALU.add, dots[:, j:j + 1])
                dve.drain()
            dve.tensor_scalar(gain[:, :], col(k, "subln"), 1.0 - LAM_INIT, None, ALU.mult).then_inc(dots_ready, 1)
            dve.wait_ge(lam_exp, 1)
            dve.scalar_tensor_tensor(out=lam[:, :], in0=dots[:, 0:1], scalar=LAM_INIT, in1=dots[:, 1:2],
                                     op0=ALU.add, op1=ALU.subtract)
            dve.drain()
            with dve.Fori(0, 4) as i:
                for j, (x, r) in enumerate(((q, 3), (key, 0))):
                    dve.wait_ge(rotated, 2 * i + j + 1)
                    rope(k, dve, x[:, 0:LAT], region(k, r, LAT), cos[:, :], sin[:, :], tmp[:, :]).then_inc(roped, 1)
                    dve.drain()
                att.vector(dve, i, 0, U)
                dve.wait_ge(summed, i + 1)
                dve.tensor_scalar(rstd[:, :], region(k, 1), 1.0 / P, EPS, ALU.mult, ALU.add).then_inc(var_ready, 1)
                dve.wait_ge(root_ready, i + 1)
                dve.reciprocal(rstd[:, :], rstd[:, :])
                dve.drain()
                dve.scalar_tensor_tensor(out=k.mo[:, bass.ds(i + 4, 1), :].rearrange("p a t -> p (a t)"), in0=region(k, 0),
                                         scalar=gain[:, :], in1=rstd[:, :], op0=ALU.mult, op1=ALU.mult).then_inc(head_done, 1)
    feed.at += 1


def window_attention(k):
    nc, feed = k.nc, k.feed
    T = TOK // P
    with Stage(k, "window") as st:
        split = Split(k, st, 3)
        q, key, v = st.sb("q", [P, LAT]), st.sb("key", [P, TOK]), st.sb("v", [P, T, P])
        tmp = st.sb("tmp", [P, LAT])
        rot, cos, sin, mask = constants(k, st, "rot", "cos", "sin", "window_mask")
        rows, sinks = st.sb("rows", [P, NROWS]), st.sb("sinks", [P, 8])
        landed = st.sem("constants_landed")
        kv_copied, q_copied, rotated, roped, chunk_done = (st.sem("kv_copied"), st.sem("q_copied"), st.sem("rotated"),
                                                           st.sem("roped"), st.sem("chunk_done"))
        units = []
        for j in range(4):
            for s in range(2):
                for t in range(4):
                    qt = q[64 * s:64 * s + 64, t * P:(t + 1) * P]
                    kt = key[64 * s:64 * s + 64, :]
                    left = P if t > 0 else 0
                    products = [(qt, kt[:, t * P - left:(t + 1) * P], 0, left + P), (qt, kt[:, LAT:TOK], left + P, CTX)]
                    tiles = ([t - 1] if left else []) + [t, 4, 5]
                    n = left + P + CTX
                    if t < 3:
                        products.append((qt, kt[:, (t + 1) * P:(t + 2) * P], n, P))
                        tiles.append(t + 1)
                        n += P
                    units.append(dict(n=n, scores=[products], values=[v[:, b, 64 * s:64 * s + 64] for b in tiles],
                                      out=region(k, 0)[64 * s:64 * s + 64, t * P:(t + 1) * P], sink=4 * s + j,
                                      mask=0 if left else P))

        def prepare(dve, unit, src, dst):
            dve.tensor_tensor(dst, src, mask[:, unit["mask"]:unit["mask"] + unit["n"]], ALU.add)

        att = Attention(k, st, units, 1, SCALE, prepare=prepare, sinks=sinks)
        U = len(units)

        @st.block.sync
        def _(sp):
            for dst, name in ((rot, "rot"), (cos, "cos"), (sin, "sin"), (mask, "window_mask")):
                sp.dma_start(dst[:, :], k.io[name]).then_inc(landed, 16)
            sp.dma_start(rows[:, :], k.io["rows"].partition_broadcast(P)).then_inc(landed, 16)
            att.load(sp)
            feed.program(sp)

        @st.block.gpsimd
        def _(pool):
            st.clear_last(pool)
            with pool.Fori(0, 2) as i:
                for j in range(6):
                    split.write_low(pool, i, j)

        @st.block.tensor
        def _(pe):
            split.start(pe)
            pe.wait_ge(landed, 80)
            pe.wait_ge(att.ident_landed, 16)
            with pe.Fori(0, 2) as i:
                pe.wait_ge(chunk_done, 4 * i + 1)
                tile_products(k, pe, i, 0, region(k, 1), k.hn, TOK, split)
                token_products(k, pe, i, 1, region(k, 2), k.hn, TOK, split)
                pe.wait_ge(kv_copied, 2 * i + 1)
                pe.matmul(region(k, 3, LAT), rot[:, :], key[:, 0:LAT], start=True, stop=True).then_inc(rotated, 1)
                for j in range(4):
                    pe.wait_ge(chunk_done, 4 * i + j + 1)
                    tile_products(k, pe, i, 2 + j, region(k, 0), k.hn, LAT, split)
                    pe.wait_ge(q_copied, 4 * i + j + 1)
                    pe.wait_ge(roped, 5 * i + j + 1)
                    pe.matmul(region(k, 3, LAT), rot[:, :], q[:, 0:LAT], start=True, stop=True).then_inc(rotated, 1)
                    pe.wait_ge(roped, 5 * i + j + 2)
                    pe.wait_ge(kv_copied, 2 * i + 2)
                    att.tensor(pe, i, 8 * j, 8 * j + 8)

        @st.block.scalar
        def _(act):
            with act.Fori(0, 2) as i:
                for j in range(3):
                    split.write_high(act, i, j)
                split.wait_done(act, i, 0)
                act.activation(key[:, :], region(k, 1), ACT.Copy).then_inc(kv_copied, 1)
                split.wait_done(act, i, 1)
                act.activation(v[:, :, :].rearrange("p t c -> p (t c)"), region(k, 2), ACT.Copy).then_inc(kv_copied, 1)
                for j in range(4):
                    if j < 3:
                        split.write_high(act, i, 3 + j)
                    split.wait_done(act, i, 2 + j)
                    act.activation(q[:, :], region(k, 0, LAT), ACT.Copy).then_inc(q_copied, 1)
                    att.scalar(act, i, 8 * j, 8 * j + 8)

        @st.block.vector
        def _(dve):
            dve.sem_inc(chunk_done, 1)
            dve.wait_ge(landed, 80)
            with dve.Fori(0, 2) as i:
                dve.wait_ge(rotated, 5 * i + 1)
                rope(k, dve, key[:, 0:LAT], region(k, 3, LAT), cos[:, :], sin[:, :], tmp[:, :]).then_inc(roped, 1)
                dve.tensor_copy(sinks[:, :], rows[:, bass.ds(8 * i + ROWCOL["sink"], 8)])
                dve.drain()
                for j in range(4):
                    dve.wait_ge(rotated, 5 * i + j + 2)
                    rope(k, dve, q[:, 0:LAT], region(k, 3, LAT), cos[:, :], sin[:, :], tmp[:, :]).then_inc(roped, 1)
                    dve.drain()
                    att.vector(dve, i, 8 * j, 8 * j + 8)
                    dve.wait_ge(att.values_done, i * U + 8 * j + 8)
                    dve.tensor_copy(k.mo[:, bass.ds(4 * i + j, 1), 0:LAT].rearrange("p a t -> p (a t)"),
                                    region(k, 0, LAT)).then_inc(chunk_done, 1)
    feed.at += 1


def neighbourhood_attention(k):
    nc, feed = k.nc, k.feed
    T = TOK // P
    NB = (DR - 1) * GRID_W
    with Stage(k, "neighbour") as st:
        split = Split(k, st, 3)
        q, key, v = st.sb("q", [P, LAT]), st.sb("key", [P, TOK]), st.sb("v", [P, T, P])
        mask, = constants(k, st, "column_mask")
        bias, raw_bias = st.sb("bias", [P, 2, NB]), st.sb("raw_bias", [P, 2, NB])
        next_q, next_key, next_v = st.sb("next_q", [P, LAT]), st.sb("next_key", [P, TOK]), st.sb("next_v", [P, TOK])
        landed, bias_landed, bias_ready, bias_free = (st.sem("mask_landed"), k.bias_landed,
                                                      st.sem("bias_ready"), st.sem("bias_free"))
        part_done, piece_copied = st.sem("part_done"), st.sem("piece_copied")
        q_moved, key_moved, v_moved = st.sem("q_moved"), st.sem("key_moved"), st.sem("v_moved")
        pieces = [(0, 0, LAT, next_q), (1, 0, LAT, next_key), (1, LAT, TOK, next_key), (2, 0, LAT, next_v), (2, LAT, TOK, next_v)]
        bank = k.ps[:, 1, :]
        first, rest = feed.at, feed.at + 1
        units = []
        for s in range(2):
            for t in range(4):
                qt = q[64 * s:64 * s + 64, t * P:(t + 1) * P]
                kt = key[64 * s:64 * s + 64, :]
                units.append(dict(n=TOK, scores=[[(qt, kt[:, 0:LAT], 0, LAT), (qt, kt[:, LAT:TOK], LAT, CTX)]],
                                  values=[v[:, b, 64 * s:64 * s + 64] for b in range(T)],
                                  out=region(k, 0)[64 * s:64 * s + 64, t * P:(t + 1) * P],
                                  bias=bias[:, s, (6 - 2 * t) * GRID_W:(6 - 2 * t) * GRID_W + LAT]))

        def prepare(dve, unit, src, dst):
            dve.scalar_tensor_tensor(out=dst[:, 0:LAT], in0=src[:, 0:LAT], scalar=SCALE, in1=unit["bias"],
                                     op0=ALU.mult, op1=ALU.add)
            dve.tensor_scalar(dst[:, LAT:TOK], src[:, LAT:TOK], SCALE, None, ALU.mult)

        att = Attention(k, st, units, 1, 1.0, prepare=prepare)
        U = len(units)

        @st.block.sync
        def _(sp):
            sp.dma_start(mask[:, :], k.io["column_mask"]).then_inc(landed, 16)
            att.load(sp)
            feed.program(sp)
            feed.at = rest
            feed.program(sp)
            feed.at = first

        @st.block.gpsimd
        def _(pool):
            st.clear_last(pool)

            def load_bias(pair):
                for s in range(2):
                    for half in range(2):
                        src = k.toeplitz[bass.ds(2 * pair + s, 1), :, 1 - half:DR - half, :]
                        pool.dma_start(raw_bias[64 * half:64 * half + 64, s, :],
                                       src.rearrange("a q r c -> (a q) (r c)")).then_inc(bias_landed[2 * s + half], 16)

            pool.wait_ge(k.bias_sem, 16 * (2 + GRID_W))
            load_bias(0)
            for j in range(3):
                split.write_low(pool, 0, j)
            feed.at = rest
            with pool.Fori(0, KC - 1) as i:
                pool.wait_ge(bias_free, i + 1)
                load_bias(i + 1)
                for j in range(3):
                    split.write_low(pool, i, j, 3)
            feed.at = first

        @st.block.tensor
        def _(pe):
            def project(i, pair, n):
                j, a, b, _ = pieces[n]
                if n or not isinstance(pair, int):
                    pe.wait_ge(piece_copied, 5 * pair + n)
                split.wait(pe, i, j)
                slot = j % split.slots
                parts = (split.high[:, slot, :], split.low[:, slot, :])
                cols = [slice(c * P, (c + 1) * P) for c in range(KC)]
                if j < 2:
                    for c in range(KC):
                        mm = split.products_of(pe, bank[:, 0:b - a], [w[:, cols[c]] for w in parts],
                                               [x[:, c, a:b] for x in k.hn], c == 0, c == KC - 1)
                else:
                    for t in range(a, b, P):
                        for c in range(KC):
                            mm = split.products_of(pe, bank[:, t - a:t - a + P], [x[:, c, t:t + P] for x in k.hn],
                                                   [w[:, cols[c]] for w in parts], c == 0, c == KC - 1)
                mm.then_inc(part_done if n in (1, 3) else split.products, 1)

            def attend(pair, following):
                def between(u):
                    if u == 1:
                        pe.wait_ge(v_moved, pair + 1)
                    if following and 1 <= u <= 5:
                        following(u - 1)
                pe.wait_ge(q_moved, pair + 1)
                pe.wait_ge(key_moved, pair + 1)
                att.tensor(pe, pair, 0, U, between)

            split.start(pe)
            pe.wait_ge(att.ident_landed, 16)
            for n in range(5):
                project(0, 0, n)
            feed.at = rest
            with pe.Fori(0, KC - 1) as i:
                attend(i, lambda n: project(i, i + 1, n))
            attend(KC - 1, None)
            feed.at = first

        @st.block.scalar
        def _(act):
            def copy_piece(i, pair, n, base):
                j, a, b, dst = pieces[n]
                if n in (1, 3):
                    act.wait_ge(part_done, 2 * pair + (1 if n == 1 else 2))
                else:
                    split.wait_done(act, i, j, base)
                if not isinstance(pair, int):
                    act.wait_ge((q_moved, key_moved, v_moved)[j], pair)
                act.activation(dst[:, a:b], bank[:, 0:b - a], ACT.Copy).then_inc(piece_copied, 1)

            def move_key():
                act.drain()
                act.activation(key[:, :], next_key[:, :], ACT.Copy).then_inc(key_moved, 1)

            for j in range(3):
                split.write_high(act, 0, j)
            for n in range(5):
                copy_piece(0, 0, n, 0)
            move_key()
            feed.at = rest
            with act.Fori(0, KC - 1) as i:
                def between(u):
                    if u < 3:
                        split.write_high(act, i, u, 3)
                    if 2 <= u <= 6:
                        copy_piece(i, i + 1, u - 2, 3)
                att.scalar(act, i, 0, U, between)
                move_key()
            att.scalar(act, KC - 1, 0, U)
            feed.at = first

        @st.block.vector
        def _(dve):
            def move_q(pair):
                dve.wait_ge(piece_copied, 5 * pair + 5)
                dve.tensor_copy(q[:, :], next_q[:, :]).then_inc(q_moved, 1)

            def move_v():
                dve.tensor_copy(v[:, :, :].rearrange("p t c -> p (t c)"), next_v[:, :]).then_inc(v_moved, 1)

            def mask_bias(pair):
                for s in range(4):
                    dve.wait_ge(bias_landed[s], 16 * pair + 16)
                for s in range(2):
                    b3, raw3 = (b[:, s, :].rearrange("p (r c) -> p r c", c=GRID_W) for b in (bias, raw_bias))
                    ins = dve.tensor_tensor(b3, raw3, mask[:, :].unsqueeze(1).to_broadcast([P, DR - 1, GRID_W]), ALU.add)
                ins.then_inc(bias_free, 1)
                dve.drain()

            def put_out(pair):
                dve.wait_ge(att.values_done, U * pair + U)
                dve.tensor_copy(k.mo[:, bass.ds(pair, 1), 0:LAT].rearrange("p a t -> p (a t)"), region(k, 0, LAT))

            dve.wait_ge(landed, 16)
            mask_bias(0)
            move_q(0)
            move_v()
            with dve.Fori(0, KC - 1) as i:
                att.vector(dve, i, 0, U)
                move_q(i + 1)
                mask_bias(i + 1)
                put_out(i)
                move_v()
            att.vector(dve, KC - 1, 0, U)
            put_out(KC - 1)
    feed.at += 2


def shift_mix(dve, dst, raw, own, before, after):
    for op in range(3):
        for a, n, off in ((0, LAT, 1), (LAT, CTX, LAT + 2)):
            d = dst[:, a:a + n]
            if op == 0:
                ins = dve.tensor_scalar(d, raw[:, off:off + n], own, None, ALU.mult)
            else:
                o = off - 1 if op == 1 else off + 1
                ins = dve.scalar_tensor_tensor(out=d, in0=raw[:, o:o + n], scalar=before if op == 1 else after, in1=d,
                                               op0=ALU.mult, op1=ALU.add)
        if op < 2:
            dve.drain()
    return ins


RAWW = TOK + 3
POOLW = 8 + LAT + 8 + CTX + 8


def rwkv(k):
    keep = k.tmp
    new = lambda name, n: keep.enter_context(k.nc.sbuf_tensor(f"rwkv_{name}", [P, n], F32))
    wd, ad, gd = new("wd", TOK), new("ad", TOK), new("gd", TOK)
    with ExitStack() as k.tmp:
        lora_and_pooling(k, wd, ad, gd)
    with ExitStack() as k.tmp:
        rwkv_pairs(k, wd, ad, gd)


def lora_and_pooling(k, wd, ad, gd):
    feed = k.feed
    with Stage(k, "lora") as st:
        raw = st.sb("raw", [P, 3, RAWW])
        own = st.sb("own", [P, 3])
        pads = [st.sb(f"pooled{j}", [P, 2, POOLW]) for j in range(5)]
        pooled = st.sb("pooled", [P, 2, TOK])
        invc, poolw = constants(k, st, "pool_inv", "pool_w")
        zeroed, copied, mixed, landed, pooled_ready, products = (st.sem("zeroed"), st.sem("copied"), st.sem("mixed"),
                                                                 st.sem("landed"), st.sem("pooled_ready"), st.sem("pool_products"))
        saved = st.sem("stream_saved")
        seqs = ((0, LAT, 8), (LAT, CTX, 16 + LAT))

        @st.block.sync
        def _(sp):
            sp.dma_start(invc[:, :, :], k.io["pool_inv"]).then_inc(landed, 16)
            sp.dma_start(poolw[:, :, :], k.io["pool_w"]).then_inc(landed, 16)
            sp.dma_start(k.saved_h, k.h[:, :, :]).then_inc(saved, 16)
            feed.program(sp)
            sp.wait_ge(saved, 16)

        @st.block.gpsimd
        def _(pool):
            st.clear_last(pool)
            pool.memset(raw[:, :, :], 0.0)
            pool.memset(pads[0][:, :, :], 0.0).then_inc(zeroed, 1)

        @st.block.tensor
        def _(pe):
            for j in range(4):
                tile_products(k, pe, 0, j, region(k, j), k.hn, TOK)
            pe.wait_ge(copied, 1)
            tile_products(k, pe, 0, 4, region(k, 0), k.hn, TOK)
            pe.wait_ge(landed, 32)
            pe.wait_ge(pooled_ready, 1)
            pe.wait_ge(copied, 4)
            for j in range(2):
                for h in range(2):
                    for a, b, _ in spans(TOK):
                        mm = pe.matmul(region(k, 2 + j)[64 * h:64 * h + 64, a:b], poolw[64 * h:64 * h + 64, j, :],
                                       pooled[64 * h:64 * h + 64, j, a:b], start=True, stop=True)
            mm.then_inc(products, 1)

        @st.block.scalar
        def _(act):
            act.wait_ge(zeroed, 1)
            for j in range(5):
                feed.wait_done(act, 0, j)
                for a, n, off in (((0, LAT, 1), (LAT, CTX, LAT + 2)) if j < 3 else seqs):
                    dst = raw[:, j, off:off + n] if j < 3 else pads[0][:, j - 3, off:off + n]
                    ins = act.activation(dst, region(k, j % 4)[:, a:a + n], ACT.Copy)
                ins.then_inc(copied, 1)
            act.wait_ge(mixed, 3)
            act.activation(wd[:, :], wd[:, :], ACT.Tanh)
            act.activation(gd[:, :], gd[:, :], ACT.Sigmoid)
            act.wait_ge(products, 1)
            for j in range(2):
                act.activation(k.mo[:, 6 + j, :], region(k, 2 + j), ACT.Identity, scale=col(k, "pool_scale", j))

        @st.block.vector
        def _(dve):
            mu = lambda d, j: col(k, "mu_lora", 3 * d + j)
            dve.tensor_tensor(own[:, :], col(k, "mu_lora", 0, 3), col(k, "mu_lora", 3, 3), ALU.add)
            dve.drain()
            dve.tensor_scalar(own[:, :], own[:, :], -1.0, 1.0, ALU.mult, ALU.add)
            dve.drain()
            for j, dst in enumerate((wd, ad, gd)):
                dve.wait_ge(copied, j + 1)
                shift_mix(dve, dst, raw[:, j, :], own[:, j:j + 1], mu(0, j), mu(1, j)).then_inc(mixed, 1)
            dve.wait_ge(copied, 5)
            for n, (left, right) in enumerate(((1, 0), (1, 1), (2, 2), (4, 4))):
                a, b = pads[n], pads[n + 1]
                if n == 0:
                    dve.memset(b[:, :, 0:1], 0.0)
                edge = (1, 2, 4, 8)[n]
                m = POOLW - 2 * edge
                dve.tensor_tensor(b[:, :, edge:edge + m], a[:, :, edge - left:edge - left + m],
                                  a[:, :, edge + right:edge + right + m], ALU.add)
                dve.drain()
            dve.wait_ge(landed, 32)
            for a, n, off in seqs:
                for j in range(2):
                    for h in range(2):
                        dve.tensor_tensor(pooled[64 * h:64 * h + 64, j, a:a + n], pads[1 + 2 * j + h][64 * h:64 * h + 64, j, off:off + n],
                                          invc[64 * h:64 * h + 64, j, a:a + n], ALU.mult)
            dve.drain()
            for a, n, off in seqs:
                ins = dve.tensor_tensor(pooled[:, :, a:a + n], pooled[:, :, a:a + n], pads[0][:, :, off:off + n], ALU.subtract)
            ins.then_inc(pooled_ready, 1)
    feed.at += 1


def rwkv_pairs(k, wd, ad, gd):
    feed = k.feed
    GR = NCH // 2
    with Stage(k, "rwkv") as st:
        pw = st.sb("pair_weights", [P, NPAIR + 3 * P])
        bones, ident2, reset, lmask, levels = constants(k, st, "bones", "ident2", "reset", "tri_mask", "level_mask")
        own = st.sb("own", [P, 4])
        raw = st.sb("raw", [P, 3, RAWW])
        y, t1, t2 = (raw[:, j, 0:TOK] for j in range(3))
        x, g = (t.rearrange("p (n c) -> p n c", c=RC) for t in (y, t1))
        r, kf, v, kk = (st.sb(n, [P, TOK]) for n in ("r", "kf", "v", "kk"))
        c, cm, em = (st.sb(n, [P, TOK]) for n in ("c", "cm", "em"))
        a, kds = (st.sb(n, [P, TOK]) for n in ("a", "kds"))
        mid = st.sb("mid", [P, 2, NCH])
        factor = st.sb("factor", [P, 2, NCH])
        spare = k.h[:, :, :].rearrange("p c t -> p (c t)")

        def lend(width, *shape):
            nonlocal spare
            t, spare = spare[:, 0:width], spare[:, width:]
            names = "abc"[:len(shape)]
            return t.rearrange(f"p ({' '.join(names)}) -> p {' '.join(names)}", **dict(zip(names, shape)))

        qq = [st.sb("qq", [P, NCH, 2, RC])[:], lend(2 * TOK, NCH, 2, RC)]
        lt = [st.sb("lt", [P, NCH, 4, RC])[:], lend(4 * TOK, NCH, 4, RC)]
        bt = [st.sb("bt", [P, NCH, RC])[:], lend(TOK, NCH, RC)]
        kt = [st.sb("kt", [P, NCH, RC])[:], lend(TOK, NCH, RC)]
        bb, kb, xt = ([st.sb(f"{n}{d}", [P, NCH, RC])[:] for d in range(2)] for n in ("bb", "kb", "xt"))
        vt = st.sb("vt", [P, NCH, RC])
        ct = st.sb("ct", [P, 2, NCH, RC])
        sm, sf = st.sb("sm", [P, 2, 2, HEAD]), st.sb("sf", [P, 2, HEAD])
        zs, sa = st.sb("zs", [P, 2, HEAD]), st.sb("sa", [P, 2, HEAD])
        par = {n: pw[:, i:i + 1] for n, i in PAIRCOL.items()}
        w2, a2, g2 = (pw[:, NPAIR + P * j:NPAIR + P * (j + 1)] for j in range(3))
        S = {n: st.sem(n) for n in (
            "constants", "padded", "pair_done", "copied", "kk_ready", "sq_ready", "norm_summed", "norm_root",
            "mix_done", "vtok_done", "vtok_copied", "lora_done", "sig_done", "cum_ready", "exp_ready", "qk_ready",
            "tok_done", "tok_copied", "l_done", "lt_ready", "ct_ready", "g_done", "g_copied", "u_done", "x_ready",
            "state_ready", "z_done", "z_copied", "sa_done", "sa_copied", "ds_done", "y_done", "y_read")}
        S.update({n: st.sem(n) for n in ("mean_done", "centred", "ysq_ready", "var_done", "var_ready", "var_root", "sums_read")})
        S["pair_landed"] = k.pair_landed
        halves = (0, 64)
        order = [list(range(8, 12)) + list(range(8)), list(range(11, 7, -1)) + list(range(7, -1, -1))]
        def flat(t):
            return t[:, :, :].rearrange("p n c -> p (n c)")

        def chunked(t):
            return t.rearrange("p (n c) -> p n c", c=RC)

        def hold(eng, sem, value):
            eng.wait_ge(sem, value)
            eng.nop(nofuse=True)

        @st.block.sync
        def _(sp):
            for dst, name in ((bones, "bones"), (ident2, "ident2"), (reset, "reset"), (lmask, "tri_mask"), (levels, "level_mask")):
                sp.dma_start(dst[:], k.io[name]).then_inc(S["constants"], 16)
            feed.program(sp)

        @st.block.gpsimd
        def _(pool):
            st.clear_last(pool)
            pool.wait_ge(S["constants"], 80)
            with pool.Fori(0, PAIRS) as i:
                hold(pool, S["pair_done"], i + 1)
                pool.memset(raw[:, :, 0:1], 0.0)
                pool.memset(raw[:, :, LAT + 1:LAT + 2], 0.0)
                pool.memset(raw[:, :, TOK + 2:TOK + 3], 0.0).then_inc(S["padded"], 1)
                pool.dma_start(pw[:, :], k.io["pair"][bass.ds(i, 1)].rearrange("a p w -> (a p) w")).then_inc(S["pair_landed"], 16)
                for d in range(2):
                    dd = 2 * i + d
                    for l in range(LEVELS):
                        for gr in range(2):
                            ns = slice(GR * gr, GR * gr + GR)
                            if l == 0:
                                pool.wait_ge(S["lt_ready"], 6 * dd + 3 * gr + 3)
                            if l >= 2:
                                pool.wait_ge(S["g_done"], 12 * dd + 2 * (l - 2) + gr + 1)
                            ins = pool.tensor_tensor(ct[:, l % 2, ns, :], lt[d][:, ns, 0, :],
                                                     levels[:, d, l, :].unsqueeze(1).to_broadcast([P, GR, RC]), ALU.mult)
                            if l == 0:
                                pool.drain()
                                ins = pool.tensor_tensor(xt[d][:, ns, :], ident2[:, :].unsqueeze(1).to_broadcast([P, GR, RC]),
                                                         ct[:, 0, ns, :], ALU.subtract)
                            ins.then_inc(S["ct_ready"], 1)

        @st.block.tensor
        def _(pe):
            def turned(dst, src):
                for n in range(NCH):
                    for h in halves:
                        mm = pe.matmul(dst[h:h + 64, n * RC:(n + 1) * RC], src[h:h + 64, n * RC:(n + 1) * RC], ident2[h:h + 64, :],
                                       start=True, stop=True)
                return mm

            def summed(dst, src):
                for a_, b_, _ in spans(TOK):
                    mm = pe.matmul(dst[:, a_:b_], bones[:, :], src[:, a_:b_], start=True, stop=True)
                return mm

            def invert(dd, d):
                hold(pe, S["tok_copied"], 2 * dd + 2)
                for l in range(LEVELS):
                    for gr in range(2):
                        hold(pe, S["ct_ready"], 12 * dd + 2 * l + gr + 1)
                        if l > 0:
                            hold(pe, S["x_ready"], 12 * dd + 2 * (l - 1) + gr + 1)
                        for n in range(GR * gr, GR * gr + GR):
                            for h in halves:
                                rhs = x[h:h + 64, n, :] if l else ident2[h:h + 64, :]
                                mm = pe.matmul(k.ps[h:h + 64, gr, (n - GR * gr) * RC:(n - GR * gr + 1) * RC],
                                               ct[h:h + 64, l % 2, n, :], rhs, start=True, stop=True)
                        mm.then_inc(S["g_done"], 1)
                    if l == 0:
                        continue
                    for gr in range(2):
                        hold(pe, S["g_copied"], 10 * dd + 2 * (l - 1) + gr + 1)
                        for n in range(GR * gr, GR * gr + GR):
                            cols = slice((n - GR * gr) * RC, (n - GR * gr + 1) * RC)
                            for h in halves:
                                if l < LEVELS - 1:
                                    pe.matmul(k.ps[h:h + 64, 2 + gr, cols], xt[d][h:h + 64, n, :], g[h:h + 64, n, :], start=True, stop=True)
                                mm = pe.matmul(k.ps[h:h + 64, 4 + gr, cols], g[h:h + 64, n, :], xt[d][h:h + 64, n, :], start=True, stop=True)
                        mm.then_inc(S["u_done"], 1)

            def recur(i):
                hold(pe, S["x_ready"], 24 * i + 24)
                Z, DS = [k.ps[:, d, 0:64] for d in range(2)], [k.ps[:, d, 64:128] for d in range(2)]
                A, Y = [k.ps[:, 2 + d, 0:64] for d in range(2)], [region(k, 2 + d) for d in range(2)]
                for s in range(NCH):
                    last = s == NCH - 1
                    state = [sm[:, d, s % 2, :] for d in range(2)]
                    ns = [order[d][s] for d in range(2)]
                    yc = [Y[d][:, n * RC:(n + 1) * RC] for d, n in enumerate(ns)]
                    each = [(h, slice(h, h + 64)) for h in halves]
                    for d, n in enumerate(ns):
                        hold(pe, S["state_ready"], 24 * i + (2 * s + d + 1))
                        for h, hs in each:
                            pe.matmul(Z[d][hs, :], qq[d][hs, n, 0, :], state[d][hs, :], start=True, stop=False)
                            mm = pe.matmul(Z[d][hs, :], lt[d][hs, n, 2, :], vt[hs, n, :], start=False, stop=True)
                        mm.then_inc(S["z_done"], 1)
                    for d, n in enumerate(ns):
                        for h, hs in each:
                            pe.matmul(yc[d][hs, :], state[d][hs, :], qq[d][hs, n, 1, :], start=True, stop=False)
                            pe.matmul(yc[d][hs, :], vt[hs, n, :], lt[d][hs, n, 3, :], start=False, stop=False)
                    for d, n in enumerate(ns):
                        hold(pe, S["z_copied"], 24 * i + (2 * s + d + 1))
                        for h, hs in each:
                            mm = pe.matmul(A[d][hs, :], xt[d][hs, n, :], zs[hs, d, :], start=True, stop=True)
                        mm.then_inc(S["sa_done"], 1)
                    if not last:
                        for d, n in enumerate(ns):
                            for h, hs in each:
                                pe.matmul(DS[d][hs, :], kt[d][hs, n, :], vt[hs, n, :], start=True, stop=False)
                    for d, n in enumerate(ns):
                        hold(pe, S["sa_copied"], 24 * i + (2 * s + d + 1))
                        if not last:
                            for h, hs in each:
                                mm = pe.matmul(DS[d][hs, :], bt[d][hs, n, :], sa[hs, d, :], start=False, stop=True)
                            mm.then_inc(S["ds_done"], 1)
                    for d, n in enumerate(ns):
                        for h, hs in each:
                            mm = pe.matmul(yc[d][hs, :], sa[hs, d, :], lt[d][hs, n, 1, :], start=False, stop=True)
                mm.then_inc(S["y_done"], 1)

            pe.wait_ge(S["constants"], 80)
            with pe.Fori(0, PAIRS) as i:
                hold(pe, S["sums_read"], i + 1)
                for j in range(3):
                    tile_products(k, pe, i, j, region(k, j), k.hn, TOK)
                hold(pe, S["sq_ready"], i + 1)
                summed(region(k, 1), t1).then_inc(S["norm_summed"], 1)
                hold(pe, S["mix_done"], i + 1)
                turned(region(k, 2), v).then_inc(S["vtok_done"], 1)
                hold(pe, S["pair_done"], i + 1)
                hold(pe, S["pair_landed"], 16 * i + 16)
                for d, (for_c, for_a) in enumerate(((3, 0), (1, 2))):
                    if d:
                        hold(pe, S["norm_root"], i + 1)
                        hold(pe, S["vtok_copied"], i + 1)
                    ds_ = slice(64 * d, 64 * d + 64)
                    for reg, wt, src in ((for_c, w2, wd), (for_a, a2, ad)):
                        for a_, b_, _ in spans(TOK):
                            mm = pe.matmul(region(k, reg)[:, a_:b_], wt[ds_, :], src[ds_, a_:b_], start=True, stop=True)
                    mm.then_inc(S["lora_done"], 1)
                for d in range(2):
                    dd = 2 * i + d
                    hold(pe, S["qk_ready"], dd + 1)
                    turned(region(k, 0), flat(bb[d])).then_inc(S["tok_done"], 1)
                    if d == 0:
                        hold(pe, S["sig_done"], 2 * i + 2)
                    else:
                        hold(pe, S["x_ready"], 24 * i + 12)
                    for n in range(NCH):
                        for h in halves:
                            for j, w in enumerate((bb[d], kb[d])):
                                mm = pe.matmul(k.ps[h:h + 64, 2 + n // 2, (n % 2) * 256 + 128 * j:(n % 2) * 256 + 128 * j + 128],
                                               w[h:h + 64, n, :], qq[d][h:h + 64, n, :, :], start=True, stop=True)
                        if n % 2:
                            mm.then_inc(S["l_done"], 1)
                    hold(pe, S["tok_copied"], 2 * dd + 1)
                    turned(region(k, 0), flat(kb[d])).then_inc(S["tok_done"], 1)
                    hold(pe, S["lt_ready"], 6 * dd + 6)
                    invert(dd, d)
                recur(i)
                hold(pe, S["y_read"], i + 1)
                summed(region(k, 0), y).then_inc(S["mean_done"], 1)
                for a_, b_, _ in spans(TOK):
                    pe.matmul(region(k, 3)[:, a_:b_], g2, gd[:, a_:b_], start=True, stop=True)
                hold(pe, S["ysq_ready"], i + 1)
                summed(region(k, 1), t1)
                summed(region(k, 2), kds).then_inc(S["var_done"], 1)

        @st.block.scalar
        def _(act):
            def sigmoids(i, d):
                act.wait_ge(S["lora_done"], 2 * i + (d + 1))
                for_c, for_a = ((3, 0), (1, 2))[d]
                act.activation(c[:, :], region(k, for_c), ACT.Sigmoid, bias=par[f"w0_{d}"])
                act.activation(a[:, :], region(k, for_a), ACT.Sigmoid, bias=par[f"a0_{d}"]).then_inc(S["sig_done"], 1)

            def exponentials(i, d):
                act.wait_ge(S["cum_ready"], 2 * i + (d + 1))
                act.activation(mid[:, :, :], mid[:, :, :], ACT.Exp)
                act.activation(em[:, :], em[:, :], ACT.Exp, scale=1.0 if d == 0 else -1.0)
                act.activation(c[:, :], cm[:, :], ACT.Exp, scale=-1.0)
                act.drain()
                act.activation(cm[:, :], cm[:, :] if d == 0 else t1, ACT.Exp)
                act.drain()
                act.activation(zs[:, 0, 0:1], mid[:, 0, 0:1], ACT.Copy).then_inc(S["exp_ready"], 1)

            def copy_tokens(i, d, j):
                act.wait_ge(S["tok_done"], 4 * i + (2 * d + j + 1))
                act.activation(flat((bt, kt)[j][d]), region(k, 0), ACT.Copy).then_inc(S["tok_copied"], 1)

            def copy_g(dd):
                for l in range(1, LEVELS):
                    for gr in range(2):
                        if l >= 2:
                            act.wait_ge(S["u_done"], 10 * dd + (2 * (l - 2) + gr + 1))
                        act.wait_ge(S["g_done"], 12 * dd + (2 * l + gr + 1))
                        act.activation(g[:, GR * gr:GR * gr + GR, :].rearrange("p n c -> p (n c)"), k.ps[:, gr, 0:GR * RC],
                                       ACT.Copy).then_inc(S["g_copied"], 1)

            with act.Fori(0, PAIRS) as i:
                act.wait_ge(S["padded"], i + 1)
                for j in range(3):
                    feed.wait_done(act, i, j)
                    act.activation(raw[:, j, 1:LAT + 1], region(k, j)[:, 0:LAT], ACT.Copy)
                    act.activation(raw[:, j, LAT + 2:TOK + 2], region(k, j)[:, LAT:TOK], ACT.Copy).then_inc(S["copied"], 1)
                act.wait_ge(S["kk_ready"], i + 1)
                act.activation(t1, kk[:, :], ACT.Square).then_inc(S["sq_ready"], 1)
                act.wait_ge(S["norm_summed"], i + 1)
                act.activation(t2, region(k, 1), ACT.Sqrt).then_inc(S["norm_root"], 1)
                act.wait_ge(S["vtok_done"], i + 1)
                act.activation(flat(vt), region(k, 2), ACT.Copy).then_inc(S["vtok_copied"], 1)
                sigmoids(i, 0)
                exponentials(i, 0)
                act.wait_ge(S["qk_ready"], 2 * i + 1)
                sigmoids(i, 1)
                copy_tokens(i, 0, 0)
                exponentials(i, 1)
                copy_tokens(i, 0, 1)
                copy_g(2 * i)
                for j in range(2):
                    copy_tokens(i, 1, j)
                copy_g(2 * i + 1)
                for s in range(NCH):
                    for d in range(2):
                        act.wait_ge(S["z_done"], 24 * i + (2 * s + d + 1))
                        act.activation(zs[:, d, :], k.ps[:, d, 0:64], ACT.Copy).then_inc(S["z_copied"], 1)
                    for d in range(2):
                        act.wait_ge(S["sa_done"], 24 * i + (2 * s + d + 1))
                        act.activation(sa[:, d, :], k.ps[:, 2 + d, 0:64], ACT.Copy, scale=-1.0).then_inc(S["sa_copied"], 1)
                act.wait_ge(S["centred"], i + 1)
                act.activation(t1, y, ACT.Square).then_inc(S["ysq_ready"], 1)
                act.wait_ge(S["var_ready"], i + 1)
                act.activation(t2, t2, ACT.Sqrt).then_inc(S["var_root"], 1)

        @st.block.vector
        def _(dve):
            def sums(i, d):
                dd = 2 * i + d
                dve.wait_ge(S["sig_done"], dd + 1)
                dve.tensor_scalar(c[:, :], c[:, :], -math.exp(-0.5), None, ALU.mult)
                dve.drain()
                dve.tensor_tensor_scan(cm[:, :], reset[:, :], c[:, :], 0.0, ALU.mult, ALU.add)
                dve.drain()
                dve.tensor_copy(mid[:, 0, :], chunked(cm[:, :])[:, :, RC // 2 - 1])
                dve.tensor_tensor(em[:, :], cm[:, :], c[:, :], ALU.subtract)
                dve.drain()
                m = mid[:, 0, :].unsqueeze(2).to_broadcast([P, NCH, RC])
                dve.tensor_tensor(mid[:, 1, :], chunked(cm[:, :])[:, :, RC - 1], mid[:, 0, :], ALU.subtract)
                dve.tensor_tensor(chunked(em[:, :]), chunked(em[:, :]), m, ALU.subtract)
                dve.drain()
                dve.tensor_tensor(chunked(cm[:, :]), chunked(cm[:, :]), m, ALU.subtract)
                if d == 1:
                    dve.tensor_copy(t1, em[:, :])
                dve.drain()
                dve.tensor_copy(own[:, 0:1], own[:, 0:1]).then_inc(S["cum_ready"], 1)

            def operands(i, d):
                dd = 2 * i + d
                dve.tensor_scalar(t2, a[:, :], par["k_a"], own[:, 3:4], ALU.mult, ALU.add)
                dve.drain()
                dve.tensor_tensor(t2, t2, kf[:, :], ALU.mult)
                dve.tensor_tensor(a[:, :], a[:, :], kk[:, :], ALU.mult)
                dve.drain()
                if d == 0:
                    dve.tensor_copy(kds[:, :], t2)
                else:
                    dve.tensor_tensor(kds[:, :], kds[:, :], t2, ALU.add)
                dve.wait_ge(S["exp_ready"], dd + 1)
                ekk, er, eb = (em, cm, c) if d == 0 else (c, em, cm)
                dve.tensor_tensor(qq[d][:, :, 0, :], chunked(kk[:, :]), chunked(ekk[:, :]), ALU.mult)
                dve.tensor_tensor(qq[d][:, :, 1, :], chunked(r[:, :]), chunked(er[:, :]), ALU.mult)
                dve.tensor_tensor(flat(bb[d]), a[:, :], eb[:, :], ALU.mult)
                dve.tensor_tensor(flat(kb[d]), t2, eb[:, :], ALU.mult).then_inc(S["qk_ready"], 1)
                start, end = (0, 1) if d == 0 else (1, 0)
                for lo, hi in ((8, 12), (0, 8)):
                    if d == 0:
                        dve.tensor_tensor(factor[:, d, lo:hi - 1], mid[:, end, lo:hi - 1], mid[:, start, lo + 1:hi], ALU.mult)
                    else:
                        dve.tensor_tensor(factor[:, d, lo + 1:hi], mid[:, end, lo + 1:hi], mid[:, start, lo:hi - 1], ALU.mult)
                seam_from, seam_to = (11, 0) if d == 0 else (8, 7)
                dve.tensor_tensor(factor[:, d, seam_from:seam_from + 1], mid[:, end, seam_from:seam_from + 1],
                                  mid[:, start, seam_to:seam_to + 1], ALU.mult)

            def triangles(i, d):
                dd = 2 * i + d
                for b in range(6):
                    dve.wait_ge(S["l_done"], 6 * dd + b + 1)
                    dve.tensor_tensor(lt[d][:, 2 * b:2 * b + 2, :, :].rearrange("p n j c -> p n (j c)"),
                                      k.ps[:, 2 + b, :].rearrange("p (n w) -> p n w", n=2),
                                      lmask[:, d, :].unsqueeze(1).to_broadcast([P, 2, 256]), ALU.mult).then_inc(S["lt_ready"], 1)

            def inverses(i, d):
                dd = 2 * i + d
                for gr in range(2):
                    dve.wait_ge(S["g_done"], 12 * dd + gr + 1)
                    dve.scalar_tensor_tensor(out=x[:, GR * gr:GR * gr + GR, :], in0=k.ps[:, gr, 0:GR * RC].rearrange("p (n c) -> p n c", c=RC),
                                             scalar=-1.0, in1=ident2[:, :].unsqueeze(1).to_broadcast([P, GR, RC]),
                                             op0=ALU.mult, op1=ALU.add).then_inc(S["x_ready"], 1)
                for l in range(1, LEVELS):
                    for gr in range(2):
                        dve.wait_ge(S["u_done"], 10 * dd + 2 * (l - 1) + gr + 1)
                        gs = slice(GR * gr, GR * gr + GR)
                        if l < LEVELS - 1:
                            xs = x[:, gs, :].rearrange("p n c -> p (n c)")
                            dve.tensor_tensor(xs, xs, k.ps[:, 2 + gr, 0:GR * RC], ALU.subtract)
                        xs = xt[d][:, gs, :].rearrange("p n c -> p (n c)")
                        dve.tensor_tensor(xs, xs, k.ps[:, 4 + gr, 0:GR * RC], ALU.subtract).then_inc(S["x_ready"], 1)

            dve.sem_inc(S["pair_done"], 1)
            dve.sem_inc(S["sums_read"], 1)
            dve.wait_ge(S["constants"], 80)
            with dve.Fori(0, PAIRS) as i:
                dve.wait_ge(S["pair_landed"], 16 * i + 16)
                dve.tensor_tensor(own[:, 0:3], pw[:, 0:3], pw[:, 3:6], ALU.add)
                dve.drain()
                dve.tensor_scalar(own[:, 0:3], own[:, 0:3], -1.0, 1.0, ALU.mult, ALU.add)
                dve.tensor_scalar(own[:, 3:4], par["k_a"], -1.0, 1.0, ALU.mult, ALU.add)
                dve.drain()
                for j, dst in enumerate((r, kf, v)):
                    dve.wait_ge(S["copied"], 3 * i + j + 1)
                    ins = shift_mix(dve, dst, raw[:, j, :], own[:, j:j + 1], pw[:, j:j + 1], pw[:, 3 + j:4 + j])
                ins.then_inc(S["mix_done"], 1)
                dve.tensor_scalar(kk[:, :], kf[:, :], par["k_k"], None, ALU.mult).then_inc(S["kk_ready"], 1)
                sums(i, 0)
                dve.wait_ge(S["norm_root"], i + 1)
                dve.tensor_scalar(t2, t2, 1e-12, None, ALU.max)
                dve.drain()
                dve.reciprocal(t2, t2)
                dve.drain()
                dve.tensor_tensor(kk[:, :], kk[:, :], t2, ALU.mult)
                dve.drain()
                operands(i, 0)
                sums(i, 1)
                triangles(i, 0)
                operands(i, 1)
                inverses(i, 0)
                triangles(i, 1)
                inverses(i, 1)
                for d in range(2):
                    dve.memset(sm[:, d, 0, :], 0.0).then_inc(S["state_ready"], 1)
                for s in range(NCH - 1):
                    f = [factor[:, d, order[d][s]:order[d][s] + 1] for d in range(2)]
                    dve.drain()
                    for d in range(2):
                        dve.tensor_scalar(sf[:, d, :], sm[:, d, s % 2, :], f[d], None, ALU.mult)
                    dve.drain()
                    for d in range(2):
                        dve.wait_ge(S["ds_done"], 22 * i + (2 * s + d + 1))
                        dve.scalar_tensor_tensor(out=sm[:, d, (s + 1) % 2, :], in0=k.ps[:, d, 64:128], scalar=f[d], in1=sf[:, d, :],
                                                 op0=ALU.mult, op1=ALU.add).then_inc(S["state_ready"], 1)
                dve.scalar_tensor_tensor(out=kds[:, :], in0=r[:, :], scalar=par["r_k"], in1=kds[:, :], op0=ALU.mult, op1=ALU.mult)
                dve.wait_ge(S["y_done"], i + 1)
                dve.tensor_copy(y, region(k, 2))
                dve.drain()
                dve.tensor_tensor(y, y, region(k, 3), ALU.add).then_inc(S["y_read"], 1)
                dve.wait_ge(S["mean_done"], i + 1)
                dve.scalar_tensor_tensor(out=y, in0=region(k, 0), scalar=-1.0 / HEAD, in1=y, op0=ALU.mult, op1=ALU.add).then_inc(S["centred"], 1)
                dve.wait_ge(S["var_done"], i + 1)
                dve.tensor_scalar(t2, region(k, 1), 1.0 / HEAD, GN_EPS, ALU.mult, ALU.add).then_inc(S["var_ready"], 1)
                dve.tensor_tensor(t1, region(k, 2), v[:, :], ALU.mult).then_inc(S["sums_read"], 1)
                dve.wait_ge(S["var_root"], i + 1)
                dve.reciprocal(t2, t2)
                dve.drain()
                dve.tensor_tensor(y, y, t2, ALU.mult)
                dve.drain()
                dve.tensor_scalar(y, y, par["lnx_g"], par["lnx_b"], ALU.mult, ALU.add)
                dve.drain()
                dve.tensor_tensor(y, y, t1, ALU.add)
                dve.drain()
                dve.tensor_tensor(k.mo[:, bass.ds(i, 1), :].rearrange("p a t -> p (a t)"), y, region(k, 3), ALU.mult).then_inc(S["pair_done"], 1)
    feed.at += 1


def _tiles(w, kc=KC):
    w = w.reshape(kc, P, -1, P)
    return w.transpose(2, 1, 0, 3).reshape(-1, P, kc * P)


def _features(v):
    return v.reshape(-1, P).T


def _constants(np):
    c = {}
    c["ident"] = np.eye(P)
    pos = np.arange(LAT)
    nf = HEAD // 4
    inv = 10000.0 ** (-np.arange(nf, dtype=np.float32) / nf)
    ang = np.stack([(pos // GRID_W)[:, None] * inv, (pos % GRID_W)[:, None] * inv], axis=1).astype(np.float32)
    ang = np.broadcast_to(ang[:, :, None, :], (LAT, 2, 2, nf)).reshape(LAT, HEAD).T
    c["cos"], c["sin"] = np.tile(np.cos(ang), (2, 1)), np.tile(np.sin(ang), (2, 1))
    rot = np.zeros((P, P))
    for b in range(0, P, 32):
        for n in range(nf):
            rot[b + nf + n, b + n] = -1.0
            rot[b + n, b + nf + n] = 1.0
    c["rot"] = rot
    i, j = np.arange(P)[:, None], np.arange(P)[None, :]
    c["window_mask"] = np.concatenate([np.where(j >= i, 0.0, NEG), np.zeros((P, P + CTX)), np.where(j <= i, 0.0, NEG)], 1)
    start = np.clip(np.arange(GRID_W) - 8, 0, GRID_W - 16)[:, None]
    kc = np.arange(GRID_W)[None, :]
    c["column_mask"] = np.tile(np.where((kc >= start) & (kc < start + 16), 0.0, NEG), (2, 1))
    same = (i // RC) == (j // RC)
    c["bones"] = same.astype(np.float32)
    c["ident2"] = np.tile(np.eye(RC), (2, 1))
    c["reset"] = np.broadcast_to((np.arange(TOK) % RC != 0).astype(np.float32), (P, TOK))
    s, t = np.arange(RC)[:, None], np.arange(RC)[None, :]
    tri = [np.concatenate([s < t, s <= t, s < t, s <= t], 1), np.concatenate([s > t, s >= t, s > t, s >= t], 1)]
    c["tri_mask"] = np.tile(np.stack(tri, 1), (2, 1, 1))
    lev = [[((s >> (l + 1)) == (t >> (l + 1))) & ((s >> l) != (t >> l)) & ((s < t) if d == 0 else (s > t))
            for l in range(LEVELS)] for d in range(2)]
    c["level_mask"] = np.tile(np.array(lev).transpose(2, 0, 1, 3), (2, 1, 1, 1))
    inv = np.zeros((P, 2, TOK))
    for g, win in enumerate((2, 4, 8, 16)):
        for a, n in ((0, LAT), (LAT, CTX)):
            tt = np.arange(n)
            inv[64 * (g % 2):64 * (g % 2) + 64, g // 2, a:a + n] = 1.0 / (np.clip(tt + win // 2, 0, n) - np.clip(tt - win // 2, 0, n))
    c["pool_inv"] = inv
    return {n: np.ascontiguousarray(a, dtype=np.float32) for n, a in c.items()}


def _layout(np, x):
    a = _constants(np)
    both = np.concatenate([x["x"][0], x["ctx"][0]], 0)
    a["h0"] = both.T.reshape(KC, P, TOK).transpose(1, 0, 2)
    a["ctx2"] = x["ctx_2"][0].T.reshape(KC, P, CTX).transpose(1, 0, 2)
    for l in range(2):
        for n, w in ((l, x["ada_w"][l]), (2 + l, x["ada_w_2"][l])):
            a[f"ada{n}"] = w.reshape(4, 2, P, 12, 512).transpose(3, 0, 2, 1, 4).reshape(48, P, 1024) if n else _tiles(w)
        a[f"ffn_g{l}"], a[f"ffn_u{l}"] = _tiles(x["ffn_w_in"][l][:, :FF]), _tiles(x["ffn_w_in"][l][:, FF:])
        a[f"ffn_g{2 + l}"], a[f"ffn_u{2 + l}"] = _tiles(x["ffn_w1_2"][l]), _tiles(x["ffn_w3_2"][l])
        for n, w in ((l, x["ffn_w_out"][l]), (2 + l, x["ffn_w2_2"][l])):
            a[f"ffn_d{n}"] = w.reshape(2, HALF, P, KC, P).transpose(0, 3, 2, 1, 4).reshape(2 * KC, P, HALF * P)
    a["even_in"], a["even_out"] = _tiles(x["even_w_in"][0]), _tiles(x["even_w_out"][0])
    w = x["odd_w_qkv"][0]
    order = [8 * c + 4 * s + j for c in range(2) for j in range(4) for s in range(2)]
    wq = w[:, :1024].reshape(D, 16, HEAD)[:, order].reshape(D, 1024)
    a["odd_in"] = _tiles(np.concatenate([wq, w[:, 1024:]], 1))
    a["odd_out"] = _tiles(x["odd_w_out"][0].reshape(16, HEAD, D)[order].reshape(1024, D))
    w = x["ev_w_in_2"][0]
    a["ev_in"], a["ev_out"] = _tiles(w), _tiles(x["ev_w_out_2"][0])
    a["od_in"], a["od_out"] = _tiles(x["od_w_in_2"][0]), _tiles(x["od_w_out_2"][0])
    mu = x["ev_shift_mu_2"][0]
    small = dict(c=x["c"][0], cc=x["c_ctx"], c2=x["c_2"][0], cc2=x["c_ctx_2"], ada_b=x["ada_b"], ada_b2=x["ada_b_2"],
                 norm1=x["norm1_g"], norm2=x["norm2_g"], final=x["final_g"], subln=x["diff_subln_g"], ln_g=x["ln_g_2"],
                 ln_b=x["ln_b_2"], mu_lora=mu[:, 2304:], pool_scale=x["ev_pool_scale_2"])
    a["small"] = np.concatenate([_features(small[n]) for n, _ in SMALL], 1)
    pair = [mu[d, 768 * j:768 * j + 768] for d in range(2) for j in range(3)]
    pair += [x["ev_w0_2"][0, 0], x["ev_w0_2"][0, 1], x["ev_a0_2"][0, 0], x["ev_a0_2"][0, 1], x["ev_k_k_2"][0],
             x["ev_k_a_2"][0], x["ev_r_k_2"][0].reshape(-1), x["ev_lnx_g_2"][0], x["ev_lnx_b_2"][0]]
    pair = np.stack(pair, 1).reshape(PAIRS, P, NPAIR)
    lora = np.stack([x["ev_w2_2"][0].reshape(P, -1), x["ev_a2_2"][0].reshape(P, -1), x["ev_g2_2"][0]], 0)
    lora = lora.reshape(3, P, PAIRS, P).transpose(2, 1, 0, 3).reshape(PAIRS, P, 3 * P)
    a["pair"] = np.concatenate([pair, lora], 2)
    a["pool_w"] = x["ev_pool_w_2"][0].reshape(2, 2, 64, 64).transpose(1, 2, 0, 3).reshape(P, 2, 64)
    a["rows"] = np.concatenate([x[n].reshape(-1) for n in ("diff_lq1", "diff_lk1", "diff_lq2", "diff_lk2", "odd_sink", "sgu_b")])
    a["sgu_wt"] = x["sgu_w"][0].transpose(2, 0, 1)
    a["rpb"] = x["od_rpb_2"][0].reshape(16 * DR, DCOL)
    return {n: np.ascontiguousarray(v) for n, v in a.items()}


def kernel(**inputs):
    import numpy as np
    import concourse.bacc as bacc
    from concourse.bass_utils import run_bass_kernel_spmd

    nc = bacc.Bacc("TRN2", target_bir_lowering=False, num_devices=1)
    arrays = _layout(np, {n: np.asarray(v) for n, v in inputs.items()})
    io = {n: nc.dram_tensor(f"in_{n}", v.shape, F32, kind="ExternalInput").ap() for n, v in arrays.items()}
    out = nc.dram_tensor("out", (P, KC, LAT), F32, kind="ExternalOutput").ap()
    program(nc, io, out)
    result = run_bass_kernel_spmd(nc, [{f"in_{n}": v for n, v in arrays.items()}], core_ids=[0])
    y = result.results[0]["out"]
    return y.transpose(2, 1, 0).reshape(1, LAT, D)
```
